# Optimizing a Trainium2 kernel written in Bass

```python
import jax, jax.numpy as jnp
from jax import lax
import numpy as np
import math

D_MODEL = 1024
BATCH = 1
SEQ = 256
DEPTH = 1

N_MIXERS = 2
MLSTM_HEADS = 4
MLSTM_DK = 128
MLSTM_DV = D_MODEL // MLSTM_HEADS
MLSTM_CHUNK = 128
QK_WIDTH = MLSTM_HEADS * MLSTM_DK
V_WIDTH = MLSTM_HEADS * MLSTM_DV
N_GATE_COLS = 4 * MLSTM_HEADS
MLSTM_IN_WIDTH = 2 * QK_WIDTH + 2 * V_WIDTH + N_GATE_COLS
FORGET_BIAS = 3.0
POOL_WINDOWS = (2, 4, 8, 16)
POOL_GROUPS = len(POOL_WINDOWS)
POOL_GROUP_WIDTH = D_MODEL // POOL_GROUPS
D_FF = 4 * D_MODEL
PLE_DIM = 256
N_MLSTM_LAYERS = (DEPTH + N_MIXERS - 1) // N_MIXERS
N_POOL_LAYERS = DEPTH // N_MIXERS
EPS = 1e-6


def rmsnorm(x, gain):
    x32 = x.astype(jnp.float32)
    y = x32 * lax.rsqrt(jnp.mean(jnp.square(x32), axis=-1, keepdims=True) + EPS)
    return (y * gain.astype(jnp.float32)).astype(x.dtype)

def mlstm_scan(q, k, v, i_pre, f_pre):
    B, H, S, DK = q.shape
    DV = v.shape[-1]
    L = MLSTM_CHUNK
    NC = S // L

    def chunks(t):
        return jnp.moveaxis(t.reshape((B, H, NC, L) + t.shape[3:]), 2, 0)

    qc, kc, vc = chunks(q), chunks(k), chunks(v)
    ic = chunks(i_pre)
    bc = jnp.cumsum(chunks(jax.nn.log_sigmoid(f_pre)), axis=-1)
    lower = jnp.tril(jnp.ones((L, L), dtype=bool))

    def step(carry, xs):
        C, n, m = carry
        q_, k_, v_, i_, b_ = xs
        b_last = b_[..., -1]
        log_d = jnp.where(lower, b_[..., :, None] - b_[..., None, :] + i_[..., None, :], -jnp.inf)
        log_inter = b_ + m[..., None]
        m_t = jnp.maximum(log_inter, jnp.max(log_d, axis=-1))
        d = jnp.exp(log_d - m_t[..., None])
        inter = jnp.exp(log_inter - m_t)
        s = jnp.einsum('bhtd,bhsd->bhts', q_, k_) * d
        num = jnp.einsum('bhts,bhsv->bhtv', s, v_) + inter[..., None] * jnp.einsum('bhtd,bhvd->bhtv', q_, C)
        den = jnp.sum(s, axis=-1) + inter * jnp.einsum('bhtd,bhd->bht', q_, n)
        h = num / jnp.maximum(jnp.abs(den), jnp.exp(-m_t))[..., None]
        log_w = b_last[..., None] - b_ + i_
        m_new = jnp.maximum(b_last + m, jnp.max(log_w, axis=-1))
        w = jnp.exp(log_w - m_new[..., None])
        decay = jnp.exp(b_last + m - m_new)
        C = decay[..., None, None] * C + jnp.einsum('bhsv,bhsd->bhvd', w[..., None] * v_, k_)
        n = decay[..., None] * n + jnp.einsum('bhs,bhsd->bhd', w, k_)
        return (C, n, m_new), h

    init = (jnp.zeros((B, H, DV, DK), jnp.float32),
            jnp.zeros((B, H, DK), jnp.float32),
            jnp.zeros((B, H), jnp.float32))
    _, hs = lax.scan(step, init, (qc, kc, vc, ic, bc))
    return jnp.moveaxis(hs, 0, 2).reshape(B, H, S, DV)

def mlstm_mixer(xn, w_in, b_gates, head_norm, w_out):
    B, S, _ = xn.shape
    u = xn @ w_in
    q, k, v, o, g = jnp.split(u, [QK_WIDTH, 2 * QK_WIDTH, 2 * QK_WIDTH + V_WIDTH,
                                  2 * QK_WIDTH + 2 * V_WIDTH], axis=-1)
    q = q.reshape(B, S, MLSTM_HEADS, MLSTM_DK).transpose(0, 2, 1, 3).astype(jnp.float32)
    k = (k.reshape(B, S, MLSTM_HEADS, MLSTM_DK).transpose(0, 2, 1, 3).astype(jnp.float32)
         * (MLSTM_DK ** -0.5))
    v = v.reshape(B, S, MLSTM_HEADS, MLSTM_DV).transpose(0, 2, 1, 3).astype(jnp.float32)
    g = g.reshape(B, S, 4, MLSTM_HEADS).astype(jnp.float32) + b_gates.astype(jnp.float32)
    g = g.transpose(2, 0, 3, 1)
    h_fwd = mlstm_scan(q, k, v, g[0], g[1])
    flip = lambda t: jnp.flip(t, axis=2)
    h_bwd = flip(mlstm_scan(flip(q), flip(k), flip(v), flip(g[2]), flip(g[3])))
    h = (h_fwd + h_bwd).transpose(0, 2, 1, 3)
    h = h * lax.rsqrt(jnp.mean(jnp.square(h), axis=-1, keepdims=True) + EPS)
    h = h * head_norm.astype(jnp.float32).reshape(MLSTM_HEADS, MLSTM_DV)
    h = h.reshape(B, S, V_WIDTH) * jax.nn.sigmoid(o.astype(jnp.float32))
    return h.astype(xn.dtype) @ w_out

def pool_mixer(xn, w_in, w_grp, scale, w_out):
    B, S, D = xn.shape
    u = (xn @ w_in).astype(jnp.float32)
    cs = jnp.concatenate([jnp.zeros((B, 1, D), jnp.float32), jnp.cumsum(u, axis=1)], axis=1)
    t = jnp.arange(S)
    pooled = []
    for gi, win in enumerate(POOL_WINDOWS):
        c0, c1 = gi * POOL_GROUP_WIDTH, (gi + 1) * POOL_GROUP_WIDTH
        lo = jnp.clip(t - win // 2, 0, S)
        hi = jnp.clip(t + win - win // 2, 0, S)
        csg = cs[:, :, c0:c1]
        mean = (csg[:, hi] - csg[:, lo]) / (hi - lo).astype(jnp.float32)[None, :, None]
        pooled.append(mean)
    y = jnp.concatenate(pooled, axis=-1) - u
    y = jnp.einsum('bsgc,gcd->bsgd', y.reshape(B, S, POOL_GROUPS, POOL_GROUP_WIDTH),
                   w_grp.astype(jnp.float32)).reshape(B, S, D)
    y = y * scale.astype(jnp.float32)
    return y.astype(xn.dtype) @ w_out

def sqrelu_mlp(xn, w1, w2):
    return jnp.square(jax.nn.relu(xn @ w1)) @ w2

def first_inputs(seed: int = 0) -> dict:
    key = jax.random.key(seed)
    ks = jax.random.split(key, 24)

    def nrm(k, shape, fan_in):
        return jax.random.normal(k, shape, jnp.float32) * (fan_in ** -0.5)

    def gain(k, shape):
        return 1.0 + 0.05 * jax.random.normal(k, shape, jnp.float32)

    nA, nB = N_MLSTM_LAYERS, N_POOL_LAYERS
    gate_base = jnp.array([0.0, FORGET_BIAS, 0.0, FORGET_BIAS], jnp.float32)[None, :, None]
    return {
        'x': jax.random.normal(ks[0], (BATCH, SEQ, D_MODEL), jnp.float32),
        'p': jax.random.normal(ks[1], (DEPTH, BATCH, SEQ, PLE_DIM), jnp.float32),
        'norm_mix': gain(ks[2], (DEPTH, D_MODEL)),
        'norm_mlp': gain(ks[3], (DEPTH, D_MODEL)),
        'norm_ple': gain(ks[4], (DEPTH, D_MODEL)),
        'norm_final': gain(ks[5], (D_MODEL,)),
        'mlstm_w_in': nrm(ks[6], (nA, D_MODEL, MLSTM_IN_WIDTH), D_MODEL),
        'mlstm_b_gates': gate_base + 0.1 * jax.random.normal(ks[7], (nA, 4, MLSTM_HEADS), jnp.float32),
        'mlstm_head_norm': gain(ks[8], (nA, V_WIDTH)),
        'mlstm_w_out': nrm(ks[9], (nA, V_WIDTH, D_MODEL), V_WIDTH),
        'pool_w_in': nrm(ks[10], (nB, D_MODEL, D_MODEL), D_MODEL),
        'pool_w_grp': nrm(ks[11], (nB, POOL_GROUPS, POOL_GROUP_WIDTH, POOL_GROUP_WIDTH), POOL_GROUP_WIDTH),
        'pool_scale': gain(ks[12], (nB, D_MODEL)),
        'pool_w_out': nrm(ks[13], (nB, D_MODEL, D_MODEL), D_MODEL),
        'mlp_w1': nrm(ks[14], (DEPTH, D_MODEL, D_FF), D_MODEL),
        'mlp_w2': nrm(ks[15], (DEPTH, D_FF, D_MODEL), D_FF),
        'ple_w': nrm(ks[16], (DEPTH, PLE_DIM, D_MODEL), PLE_DIM),
        'ple_gate_w': nrm(ks[17], (DEPTH, D_MODEL, D_MODEL), D_MODEL),
        'ple_gate_b': 0.02 * jax.random.normal(ks[18], (DEPTH, D_MODEL), jnp.float32),
    }

def first_block(x, p, norm_mix, norm_mlp, norm_ple, norm_final,
              mlstm_w_in, mlstm_b_gates, mlstm_head_norm, mlstm_w_out,
              pool_w_in, pool_w_grp, pool_scale, pool_w_out,
              mlp_w1, mlp_w2, ple_w, ple_gate_w, ple_gate_b):
    h = x
    for i in range(DEPTH):
        xn = rmsnorm(h, norm_mix[i])
        j = i // N_MIXERS
        if i % N_MIXERS == 0:
            mix = mlstm_mixer(xn, mlstm_w_in[j], mlstm_b_gates[j], mlstm_head_norm[j], mlstm_w_out[j])
        else:
            mix = pool_mixer(xn, pool_w_in[j], pool_w_grp[j], pool_scale[j], pool_w_out[j])
        h = h + mix
        h = h + sqrelu_mlp(rmsnorm(h, norm_mlp[i]), mlp_w1[i], mlp_w2[i])
        gate = jax.nn.sigmoid((rmsnorm(h, norm_ple[i]) @ ple_gate_w[i] + ple_gate_b[i]).astype(jnp.float32))
        h = h + (gate * (p[i] @ ple_w[i]).astype(jnp.float32)).astype(h.dtype)
    return rmsnorm(h, norm_final)


CHUNK = 64
Q_BLOCK = 128
FOX_HEADS = 8
FOX_HEAD_DIM = 64
FOX_WIDTH = FOX_HEADS * FOX_HEAD_DIM
RWKV_HEADS = 8
RWKV_HEAD_DIM = 64
RWKV_WIDTH = RWKV_HEADS * RWKV_HEAD_DIM
W_LORA = 64
A_LORA = 64
G_LORA = 128
GN_EPS = 64e-5
PEER_HEADS = 8
PEER_N_KEYS = 128
PEER_N_EXPERTS = PEER_N_KEYS * PEER_N_KEYS
PEER_HALF = 128
PEER_TOPK = 16
PEER_TOKEN_BLOCK = 128
DN_ALPHA = (2 * DEPTH) ** 0.25
DN_BETA = (8 * DEPTH) ** -0.25
LN_EPS = 1e-5
FOX_SPLITS = (FOX_WIDTH, FOX_WIDTH, FOX_WIDTH, FOX_HEADS)
RWKV_SPLITS = (RWKV_WIDTH, RWKV_WIDTH, RWKV_WIDTH, W_LORA, A_LORA, G_LORA)
FOX_COLS = 3 * FOX_WIDTH + FOX_HEADS
RWKV_COLS = 3 * RWKV_WIDTH + W_LORA + A_LORA + G_LORA
IN_WIDTH = FOX_COLS + RWKV_COLS + 2 * D_MODEL


def _split(t, sizes):
    out = []
    start = 0
    for n in sizes:
        out.append(t[..., start:start + n])
        start += n
    return out

def _layer_norm(x, g, b):
    xf = x.astype(jnp.float32)
    mu = jnp.mean(xf, axis=-1, keepdims=True)
    var = jnp.mean(jnp.square(xf - mu), axis=-1, keepdims=True)
    return ((xf - mu) * lax.rsqrt(var + LN_EPS) * g + b).astype(x.dtype)

def _token_shift(p, mu):
    prev = jnp.pad(p, ((0, 0), (1, 0), (0, 0)))[:, :-1]
    return p + mu * (prev - p)

def _forgetting_attention(q, k, v, f_logit):
    B, S = q.shape[0], q.shape[1]
    heads = lambda t: t.reshape(B, S, FOX_HEADS, FOX_HEAD_DIM).transpose(0, 2, 1, 3)
    q, k, v = heads(q), heads(k), heads(v)
    log_f = jax.nn.log_sigmoid(f_logit.astype(jnp.float32))
    c = jnp.cumsum(log_f, axis=1).transpose(0, 2, 1)
    scale = FOX_HEAD_DIM ** -0.5
    outs = []
    for blk in range(S // Q_BLOCK):
        q0 = blk * Q_BLOCK
        q1 = q0 + Q_BLOCK
        s = jnp.einsum('bhqd,bhkd->bhqk', q[:, :, q0:q1], k[:, :, :q1]).astype(jnp.float32) * scale
        s = s + c[:, :, q0:q1, None] - c[:, :, None, :q1]
        causal = jnp.arange(q0, q1)[:, None] >= jnp.arange(q1)[None, :]
        s = jnp.where(causal, s, -jnp.inf)
        p = jax.nn.softmax(s, axis=-1).astype(v.dtype)
        outs.append(jnp.einsum('bhqk,bhkd->bhqd', p, v[:, :, :q1]))
    o = jnp.concatenate(outs, axis=2)
    return o.transpose(0, 2, 1, 3).reshape(B, S, FOX_WIDTH)

def _rwkv7_time_mix(r, k, v, w_lora, a_lora, g_lora, w0, w2, a0, a2, g2, k_k, k_a, r_k, ln_g, ln_b):
    B, S = r.shape[0], r.shape[1]
    f32 = jnp.float32
    H, N = RWKV_HEADS, RWKV_HEAD_DIM
    w_pre = (w0 + jnp.tanh(w_lora) @ w2).astype(f32)
    decay = jnp.exp(-jnp.exp(-jax.nn.softplus(-w_pre) - 0.5))
    a = jax.nn.sigmoid((a0 + a_lora @ a2).astype(f32))
    g = jax.nn.sigmoid(g_lora) @ g2
    heads = lambda t: t.astype(f32).reshape(B, S, H, N)
    kk = heads(k * k_k)
    kk = kk / jnp.maximum(jnp.sqrt(jnp.sum(kk * kk, axis=-1, keepdims=True)), 1e-12)
    k_mod = k.astype(f32) * (1.0 + (a - 1.0) * k_a.astype(f32))
    r_h, k_h, v_h, w_h, a_h = heads(r), heads(k_mod), heads(v), heads(decay), heads(a)

    def to_chunks(t):
        return t.transpose(1, 0, 2, 3).reshape(S // CHUNK, CHUNK, B, H, N)

    def frame_step(state, inp):
        r_t, w_t, k_t, v_t, kk_t, a_t = inp
        sa = jnp.einsum('bhij,bhj->bhi', state, -kk_t)
        state = (state * w_t[:, :, None, :] + sa[..., None] * (kk_t * a_t)[:, :, None, :]
                 + v_t[..., None] * k_t[:, :, None, :])
        return state, jnp.einsum('bhij,bhj->bhi', state, r_t)

    def chunk_step(state, chunk_inp):
        return lax.scan(frame_step, state, chunk_inp)

    state0 = jnp.zeros((B, H, N, N), f32)
    xs = (to_chunks(r_h), to_chunks(w_h), to_chunks(k_h), to_chunks(v_h), to_chunks(kk), to_chunks(a_h))
    _, y = lax.scan(chunk_step, state0, xs)
    y = y.reshape(S, B, H, N).transpose(1, 0, 2, 3)
    mu = jnp.mean(y, axis=-1, keepdims=True)
    var = jnp.mean(jnp.square(y - mu), axis=-1, keepdims=True)
    y = ((y - mu) * lax.rsqrt(var + GN_EPS)).reshape(B, S, RWKV_WIDTH) * ln_g + ln_b
    bonus = jnp.sum(r_h * k_h * r_k.astype(f32).reshape(H, N), axis=-1, keepdims=True) * v_h
    y = (y + bonus.reshape(B, S, RWKV_WIDTH)) * g
    return y.astype(r.dtype)

def _peer(x, w_q, sub_keys, u_table, v_table):
    B, S, D = x.shape
    xt = x.reshape((B * S) // PEER_TOKEN_BLOCK, PEER_TOKEN_BLOCK, D)
    K = PEER_TOPK

    def block(xb):
        t = xb.shape[0]
        q = (xb @ w_q).reshape(t, PEER_HEADS, 2, PEER_HALF)
        s = jnp.einsum('thpd,hpkd->thpk', q, sub_keys).astype(jnp.float32)
        top_s, top_i = lax.top_k(s, K)
        cand_s = top_s[:, :, 0, :, None] + top_s[:, :, 1, None, :]
        cand_i = top_i[:, :, 0, :, None] * PEER_N_KEYS + top_i[:, :, 1, None, :]
        best_s, best_pos = lax.top_k(cand_s.reshape(t, PEER_HEADS, K * K), K)
        idx = jnp.take_along_axis(cand_i.reshape(t, PEER_HEADS, K * K), best_pos, axis=-1)
        gate = jax.nn.softmax(best_s, axis=-1).astype(xb.dtype)
        h = jax.nn.gelu(jnp.einsum('thkd,td->thk', u_table[idx], xb), approximate=False)
        return jnp.einsum('thk,thkd->td', gate * h, v_table[idx])

    return lax.map(block, xt).reshape(B, S, D)

def second_inputs(seed: int = 0) -> dict:
    key = jax.random.key(seed)
    ks = jax.random.split(key, 32)
    L = DEPTH
    nrm = lambda k, shape, scale: jax.random.normal(k, shape, jnp.float32) * scale
    return {
        "x": nrm(ks[0], (BATCH, SEQ, D_MODEL), 1.0),
        "w_in": nrm(ks[1], (L, D_MODEL, IN_WIDTH), D_MODEL ** -0.5),
        "fox_f_bias": 3.0 + nrm(ks[2], (L, FOX_HEADS), 0.5),
        "rwkv_mu": jax.random.uniform(ks[3], (L, RWKV_COLS), jnp.float32),
        "rwkv_w0": nrm(ks[4], (L, RWKV_WIDTH), 1.0),
        "rwkv_w2": nrm(ks[5], (L, W_LORA, RWKV_WIDTH), 0.1 * W_LORA ** -0.5),
        "rwkv_a0": nrm(ks[6], (L, RWKV_WIDTH), 0.5),
        "rwkv_a2": nrm(ks[7], (L, A_LORA, RWKV_WIDTH), A_LORA ** -0.5),
        "rwkv_g2": nrm(ks[8], (L, G_LORA, RWKV_WIDTH), G_LORA ** -0.5),
        "rwkv_k_k": 0.85 + nrm(ks[9], (L, RWKV_WIDTH), 0.05),
        "rwkv_k_a": 1.0 + nrm(ks[10], (L, RWKV_WIDTH), 0.05),
        "rwkv_r_k": nrm(ks[11], (L, RWKV_WIDTH), 0.1),
        "rwkv_ln_g": 1.0 + nrm(ks[12], (L, RWKV_WIDTH), 0.05),
        "rwkv_ln_b": nrm(ks[13], (L, RWKV_WIDTH), 0.01),
        "p_fox": nrm(ks[14], (L, FOX_WIDTH, D_MODEL), FOX_WIDTH ** -0.5),
        "p_rwkv": nrm(ks[15], (L, RWKV_WIDTH, D_MODEL), RWKV_WIDTH ** -0.5),
        "w_o": nrm(ks[16], (L, D_MODEL, D_MODEL), DN_BETA * D_MODEL ** -0.5),
        "ln1_g": 1.0 + nrm(ks[17], (L, D_MODEL), 0.05),
        "ln1_b": nrm(ks[18], (L, D_MODEL), 0.01),
        "peer_w_q": nrm(ks[19], (L, D_MODEL, PEER_HEADS * 2 * PEER_HALF), D_MODEL ** -0.5),
        "peer_sub_keys": nrm(ks[20], (L, PEER_HEADS, 2, PEER_N_KEYS, PEER_HALF), PEER_HALF ** -0.5),
        "peer_u": nrm(ks[21], (L, PEER_N_EXPERTS, D_MODEL), D_MODEL ** -0.5),
        "peer_v": nrm(ks[22], (L, PEER_N_EXPERTS, D_MODEL), DN_BETA * PEER_HEADS ** -0.5),
        "ln2_g": 1.0 + nrm(ks[23], (L, D_MODEL), 0.05),
        "ln2_b": nrm(ks[24], (L, D_MODEL), 0.01),
    }

def second_block(x, w_in, fox_f_bias, rwkv_mu, rwkv_w0, rwkv_w2, rwkv_a0, rwkv_a2, rwkv_g2,
              rwkv_k_k, rwkv_k_a, rwkv_r_k, rwkv_ln_g, rwkv_ln_b, p_fox, p_rwkv, w_o,
              ln1_g, ln1_b, peer_w_q, peer_sub_keys, peer_u, peer_v, ln2_g, ln2_b):
    for l in range(DEPTH):
        p = x @ w_in[l]
        fox_cols = p[..., :FOX_COLS]
        rwkv_cols = _token_shift(p[..., FOX_COLS:FOX_COLS + RWKV_COLS], rwkv_mu[l])
        gate_cols = p[..., FOX_COLS + RWKV_COLS:]
        q, k, v, f_logit = _split(fox_cols, FOX_SPLITS)
        r_r, r_k, r_v, r_wl, r_al, r_gl = _split(rwkv_cols, RWKV_SPLITS)
        gate_fox, gate_rwkv = _split(gate_cols, (D_MODEL, D_MODEL))

        y_fox = _forgetting_attention(q, k, v, f_logit + fox_f_bias[l])
        y_rwkv = _rwkv7_time_mix(r_r, r_k, r_v, r_wl, r_al, r_gl,
                                 rwkv_w0[l], rwkv_w2[l], rwkv_a0[l], rwkv_a2[l], rwkv_g2[l],
                                 rwkv_k_k[l], rwkv_k_a[l], rwkv_r_k[l], rwkv_ln_g[l], rwkv_ln_b[l])
        merged = (jax.nn.sigmoid(gate_fox) * (y_fox @ p_fox[l])
                  + jax.nn.sigmoid(gate_rwkv) * (y_rwkv @ p_rwkv[l]))
        x = _layer_norm(DN_ALPHA * x + merged @ w_o[l], ln1_g[l], ln1_b[l])
        x = _layer_norm(DN_ALPHA * x + _peer(x, peer_w_q[l], peer_sub_keys[l], peer_u[l], peer_v[l]),
                        ln2_g[l], ln2_b[l])
    return x


def setup_inputs(seed=0):
    out = dict(first_inputs(seed))
    for name, value in second_inputs(seed + 1).items():
        if name != "x":
            out[name + "_2"] = value
    return out


def reference(
    x, p, norm_mix, norm_mlp, norm_ple, norm_final, mlstm_w_in, mlstm_b_gates, mlstm_head_norm,
    mlstm_w_out, pool_w_in, pool_w_grp, pool_scale, pool_w_out, mlp_w1, mlp_w2, ple_w,
    ple_gate_w, ple_gate_b, w_in_2, fox_f_bias_2, rwkv_mu_2, rwkv_w0_2, rwkv_w2_2, rwkv_a0_2,
    rwkv_a2_2, rwkv_g2_2, rwkv_k_k_2, rwkv_k_a_2, rwkv_r_k_2, rwkv_ln_g_2, rwkv_ln_b_2, p_fox_2,
    p_rwkv_2, w_o_2, ln1_g_2, ln1_b_2, peer_w_q_2, peer_sub_keys_2, peer_u_2, peer_v_2, ln2_g_2,
    ln2_b_2,
):
    x = first_block(
        x, p, norm_mix, norm_mlp, norm_ple, norm_final, mlstm_w_in, mlstm_b_gates,
        mlstm_head_norm, mlstm_w_out, pool_w_in, pool_w_grp, pool_scale, pool_w_out, mlp_w1,
        mlp_w2, ple_w, ple_gate_w, ple_gate_b,
    )
    return second_block(
        x, w_in_2, fox_f_bias_2, rwkv_mu_2, rwkv_w0_2, rwkv_w2_2, rwkv_a0_2, rwkv_a2_2,
        rwkv_g2_2, rwkv_k_k_2, rwkv_k_a_2, rwkv_r_k_2, rwkv_ln_g_2, rwkv_ln_b_2, p_fox_2,
        p_rwkv_2, w_o_2, ln1_g_2, ln1_b_2, peer_w_q_2, peer_sub_keys_2, peer_u_2, peer_v_2,
        ln2_g_2, ln2_b_2,
    )


_drawn_inputs = setup_inputs


def setup_inputs(seed=0):
    import zlib

    import numpy as np

    out = dict(_drawn_inputs(seed))
    spreads = {}
    factors = {'norm_ple': 5.877,
     'ple_gate_b': 26.945,
     'fox_f_bias_2': 38.144,
     'rwkv_w2_2': 8.0,
     'rwkv_k_k_2': 37.732,
     'rwkv_k_a_2': 3.901,
     'rwkv_ln_g_2': 4.872,
     'rwkv_ln_b_2': 33.527,
     'ln1_b_2': 3.963,
     'ln2_b_2': 5.682}
    for name, (base, spread) in spreads.items():
        noise = np.random.default_rng([zlib.crc32(name.encode()), seed]).standard_normal(out[name].shape)
        drawn = base * np.exp(spread * noise) if base else spread * noise
        out[name] = __import__('jax').numpy.asarray(drawn.astype(out[name].dtype))
    for name, factor in factors.items():
        out[name] = (out[name] * factor).astype(out[name].dtype)
    return out
```

```python
from contextlib import ExitStack

import concourse.bass as bass
from concourse import mybir

ALU = mybir.AluOpType
ACT = mybir.ActivationFunctionType
F32 = mybir.dt.float32
F32R = mybir.dt.float32r
BF16 = mybir.dt.bfloat16
U32 = mybir.dt.uint32
AX_X = mybir.AxisListType.X

P = 128
S = 256
NT = S // P
D = 1024
KC = D // P
EPS = 1e-6
LN_EPS = 1e-5
GN_EPS = 64e-5
DN_ALPHA = 2.0 ** 0.25

MH, MDK, MDV = 4, 128, 256
FH, FD = 8, 64
RH, RN = 8, 64
CH_T = 64
NCH = S // CH_T
NPAIR = RH // 2
RW_CHUNKS = (3 * RH * RN + 64 + 64 + 128) // P
DECAY = 0.6065306597126334
NEG = -1.0e30
BLK = 16
PH, NK, TOPK = 8, 128, 16
LISTS = 2 * PH

COUNTS = [
    ("qk", 8), ("v", 8), ("o", 8), ("mix_out", 8), ("w1", 32), ("w2", 32), ("ple_gate", 8), ("ple", 2),
    ("rwkv", RW_CHUNKS), ("fox_qk", 8), ("fox_v", 4), ("gates", 16), ("p_fox", 4), ("p_rwkv", 4), ("w_o", 8),
    ("peer_q", 16), ("keys", 2), ("u", NK), ("v_table", NK),
]
FIRST = {}
_at = 0
for _name, _n in COUNTS:
    FIRST[_name] = _at
    _at += _n
N_ITEMS = _at
RING = 4

VEC = {}
_at = 0
for _name, _n in [("norm_mix", 8), ("norm_mlp", 8), ("norm_ple", 8), ("head_norm", 8), ("mu", RW_CHUNKS), ("w0", 4),
                  ("a0", 4), ("k_k", 4), ("k_a", 4), ("r_k", 4), ("ln_g", 4), ("ln_b", 4)]:
    VEC[_name] = _at
    _at += _n
N_VEC = _at
ROWS = ["norm_final", "ple_gate_b", "ln1_g", "ln1_b", "ln2_g", "ln2_b"]

T_MIX, T_HEADS, T_MLP, T_PLE, T_X1, T_MERGED, T_X2 = range(7)

INVERSE = [
    ("P0", "I", "T0", False, -1),
    ("T0", "P0", "P1", False, 0), ("P0", "T0", "T1", False, 0),
    ("T1", "X", "X", True, 2), ("T1", "P1", "P0", False, 2),
    ("P1", "T1", "T0", False, 2), ("T0", "X", "X", True, 5),
    ("P0", "T0", "T1", False, 5), ("T1", "X", "X", True, 7),
    ("X", "I", "T0", False, 8),
    ("T0", "NO", "P0", False, 9), ("NO", "T0", "P1", False, 9),
    ("P0", "P1", "T1", False, 11), ("T1", "X", "X", True, 12),
    ("P1", "X", "X", True, 13),
]


def evacuated(upto, adds):
    return sum(r[3] == adds for r in INVERSE[:upto + 1])


def bass_blocks(nc, weights, x_in, p_in, vec_in, rows_in, gate_w_in, lora_in, mb_in, fb_in, out):
    with ExitStack() as ctx:
        base = 16512
        slab = ctx.enter_context(nc.sbuf_tensor("slab", [P, 53208], F32))

        def at(name, shape, dt, offset):
            return nc.alloc_sbuf_tensor_at(name, shape, dt, offset=base + offset)

        H = at("H", [P, NT, D], F32, 0)
        XH = at("XH", [P, KC, S], F32R, 8192)
        XL = at("XL", [P, KC, S], F32R, 16384)
        RAW = at("RAW", [P, RING, D], F32, 24576)
        WH = at("WH", [P, RING, D], F32R, 40960)
        WL = at("WL", [P, RING, D], F32R, 57344)
        C0 = 73728
        ident = at("ident", [P, P], F32, C0)
        ident_b = at("ident_b", [P, P], BF16, C0 + 512)
        iota_b = at("iota_b", [P, P], BF16, C0 + 768)
        iota_f = at("iota_f", [P, P], F32, C0 + 1024)
        vec = at("vec", [P, N_VEC], F32, C0 + 1536)
        ST = at("ST", [P, 192], F32, C0 + 1856)
        ones_row = at("ones_row", [1, P], F32, C0 + 2624)
        IT = at("IT", [P, S], F32, C0 + 3136)
        JT = at("JT", [P, S], F32, C0 + 4160)
        GT = at("GT", [P, S], F32, C0 + 5184)
        HT = at("HT", [P, S], F32, C0 + 6208)
        fbias = at("fbias", [FH, 1], F32, C0 + 7232)
        mbias = at("mbias", [MH, 4], F32, C0 + 7264)
        eps_c = at("eps_c", [P, 4], F32, C0 + 7296)
        A0 = 81664
        M0 = A0 + 114688
        mask_m = at("mask_m", [P, 2, 2, S], F32, M0)
        fpt = at("fpt", [P, 2, 384], F32, M0)
        mask_f = at("mask_f", [P, S], F32, M0 + 4096)
        mask_r = at("mask_r", [P, P], F32, M0 + 5120)
        blk_ones = at("blk_ones", [P, P], F32, M0 + 5632)
        blk16 = at("blk16", [64, 64], F32, M0 + 6144)
        resets = at("resets", [P, D], BF16, M0 + 6400)
        sel4 = at("sel4", [MH, MH, P], F32, M0 + 8448)
        sel8 = at("sel8", [FH, FH, P], F32, M0 + 10496)
        XS = at("XS", [P, NT, D], F32, A0)
        qkT = at("qkT", [P, 2 * MH, S], F32, A0 + 8192)
        v1 = at("v1", [P, NT, MH, MDV + 1], F32, A0 + 16384)
        og = at("og", [P, NT, D], F32, A0 + 24640)
        hacc = at("hacc", [P, NT, D], F32, A0 + 32832)
        WE = at("WE", [P, 2, 2, S], F32, A0 + 41024)
        SM = at("SM", [P, 2, 2, S], F32, A0 + 45120)
        GR = at("GR", [MH, 4, S], F32, A0 + 49216)
        GA = at("GA", [MH, 8, S], F32, A0 + 53312)
        AT = at("AT", [P, 8, MH], F32, A0 + 61504)
        gtok = at("gtok", [P, NT, 16], F32, A0 + 61632)
        GWH = at("GWH", [P, KC, 24], F32R, A0 + 62208)
        GWL = at("GWL", [P, KC, 24], F32R, A0 + 62976)
        gw = at("gw", [P, KC, 24], F32, A0 + 63744)
        ZH = at("ZH", [P, 32, S], F32R, A0 + 8192)
        ZL = at("ZL", [P, 32, S], F32R, A0 + 40960)
        RT = at("RT", [P, 4, S], F32, A0 + 73728)
        ZF = at("ZF", [P, 4, S], F32, A0 + 77824)
        P2 = at("P2", [P, NT, S], F32, A0 + 81920)
        PTH = at("PTH", [P, 2, S], F32R, A0 + 83968)
        PTL = at("PTL", [P, 2, S], F32R, A0 + 86016)
        SGP = at("SGP", [P, NT, D], F32, A0 + 88064)
        brow = at("brow", [1, D], F32, A0 + 96256)
        nfin = at("nfin", [P, D], F32, A0 + 100352)
        FWH = at("FWH", [P, KC, 8], F32R, A0 + 104448)
        FWL = at("FWL", [P, KC, 8], F32R, A0 + 104704)
        SG = at("SG", [P, NT, 2 * D], F32, A0 + 8192)
        YFH = at("YFH", [P, 4, S], F32R, A0 + 24576)
        YFL = at("YFL", [P, 4, S], F32R, A0 + 28672)
        YRH = at("YRH", [P, 4, S], F32R, A0 + 32768)
        YRL = at("YRL", [P, 4, S], F32R, A0 + 36864)
        fqk = at("fqk", [P, 8, S], F32, A0)
        fv = at("fv", [P, NT, 512], F32, A0 + 32768)
        fp = at("fp", [P, 2, 384], F32, A0 + 36864)
        fr = at("fr", [FH, 3, S], F32, C0 + 3136)
        ftok = at("ftok", [P, NT, 8], F32, A0 + 40960)
        lora = at("lora", [P, 2, 512], F32, A0 + 24576)
        BK = at("BK", [P, NPAIR, NCH, 2, CH_T], F32, A0 + 40960)
        CR = at("CR", [P, NPAIR, NCH, 2, CH_T], F32, A0 + 49152)
        PK = at("PK", [P, NCH, 2, NPAIR, P], F32, A0 + 57344)
        BKT = at("BKT", [P, NCH, NPAIR, P], F32, A0 + 73728)
        UV = at("UV", [P, NCH, NPAIR, P], F32, A0 + 81920)
        SH = at("SH", [P, RW_CHUNKS, S], F32, A0 + 90112)
        Z = at("Z", [P, RW_CHUNKS, S + 1], F32, A0 + 57344)
        T = [at(f"T{k}", [P, 4, S], F32, A0 + 57344 + 4096 * k) for k in range(8)]
        GG = at("GG", [P, 4, S], F32, A0 + 104448)
        BON = at("BON", [P, 4, S], F32, A0 + 108544)
        GL = at("GL", [P, NPAIR, NCH], F32, C0 + 7328)
        LT = at("LT", [P, 2, S], F32, A0 + 112640)
        MINV = at("MINV", [64, NCH, 8, 64], F32, A0)
        I0 = {"T0": 8192, "P0": 12288, "P1": 16384, "T1": 20480}
        inv = {k: at("inv_" + k, [64, 16, 64], F32, v) for k, v in I0.items()}
        inv["NO"] = at("inv_NO", [64, 16, 64], F32, A0 + 40960)
        ZS = at("ZS", [64, 512], F32, A0 + 45056)
        S2 = at("S2", [P, NPAIR, P], F32, A0 + 47104)
        YT = at("YT", [P, 4, S], F32, A0 + 90112)
        YC = at("YC", [P, 4, S], F32, A0 + 94208)
        S2T = at("S2T", [P, NPAIR, P], F32, A0 + 102400)
        LG1 = at("LG1", [P, D], F32, A0 + 24576)
        LB1 = at("LB1", [P, D], F32, A0 + 28672)
        HS = at("HS", [P, NK, S], F32, A0)
        R0 = A0 + 65536
        QH = at("QH", [P, LISTS, S], F32R, R0)
        QL = at("QL", [P, LISTS, S], F32R, R0 + 16384)
        SC = at("SC", [P, NT, LISTS, NK], F32, R0 + 32768)
        cand = at("cand", [P, PH, TOPK, TOPK], F32, R0 + 49152)
        tmp1 = at("tmp1", [P, PH, TOPK, TOPK], F32, R0 + 57344)
        tv = at("tv", [P, LISTS, TOPK], F32, R0)
        ti = at("ti", [P, LISTS, TOPK], U32, R0 + 1024)
        tif = at("tif", [P, LISTS, TOPK], F32, R0 + 2048)
        bv = at("bv", [P, NT, PH, TOPK], F32, R0 + 9216)
        be = at("be", [P, NT, PH, TOPK], F32, R0 + 10240)
        bp = at("bp", [P, PH, TOPK], U32, R0 + 3584)
        bai = at("bai", [P, PH, TOPK], U32, R0 + 4096)
        bbi = at("bbi", [P, PH, TOPK], U32, R0 + 4608)
        baf = at("baf", [P, PH, TOPK], F32, R0 + 5120)
        bbf = at("bbf", [P, PH, TOPK], F32, R0 + 5632)
        ijg = at("ijg", [P, NT, 3, P], F32, R0 + 6144)
        A4 = at("A4", [P, 2, 4, P], BF16, 8192)
        AT4 = at("AT4", [P, 2, 4, P], F32, 10240)
        hjunk = at("hjunk", [P, 8, P], F32, 14336)
        A4F = at("A4F", [P, 2, 4, P], F32, 8192)
        B4F = at("B4F", [P, 2, 4, P], F32, 12288)
        CH = at("CH", [P, RING, S], F32R, 8192)
        CL = at("CL", [P, RING, S], F32R, 12288)
        LG2 = at("LG2", [P, D], F32, 16384)
        LB2 = at("LB2", [P, D], F32, 20480)

        PS = ctx.enter_context(nc.psum_tensor("PS", [P, 8, 512], F32))

        sems = {}

        def sem(name):
            if name not in sems:
                sems[name] = ctx.enter_context(nc.semaphore(name))
            return sems[name]

        w_landed = [sem(f"w_landed{i}") for i in range(RING)]
        w_hi, w_lo, w_used = sem("w_hi"), sem("w_lo"), sem("w_used")

        def col(name, c):
            k = VEC[name] + c
            return vec[:, k:k + 1]

        def plain(ap):
            return ap.bitcast(F32)

        ALL = {}

        def after(name, n=1):
            ALL[name] = ALL.get(name, 0) + n
            return ALL[name]

        block = ctx.enter_context(nc.Block())

        @block.sync
        def _(sp):
            sp.dma_start(H[:, :, :], x_in.rearrange("(t p) d -> p t d", p=P)).then_inc(sem("x_landed"), 16)
            for n in range(RING):
                sp.dma_start(RAW[:, n, :], weights[n]).then_inc(w_landed[n], 16)
            full = (N_ITEMS // RING) * RING
            with sp.Fori(1, N_ITEMS // RING) as i:
                for slot in range(RING):
                    n = i * RING
                    sp.wait_ge(w_lo, n + (slot + 1 - RING))
                    sp.dma_start(RAW[:, slot, :], weights[bass.ds(n + slot, 1)].rearrange("a p d -> p (a d)")).then_inc(w_landed[slot], 16)
            for n in range(full, N_ITEMS):
                sp.wait_ge(w_lo, n + 1 - RING)
                sp.dma_start(RAW[:, n % RING, :], weights[n]).then_inc(w_landed[n % RING], 16)
            for t in range(NT):
                sp.wait_ge(sem("y_ready"), t + 1)
                sp.dma_start(out[t * P:(t + 1) * P, :], H[:, t, :]).then_inc(sem("y_stored"), 16)
            sp.wait_ge(sem("y_stored"), 16 * NT)

        @block.gpsimd
        def _(pool):
            made = sem("pool_made")
            count = [0]

            def link(ins):
                count[0] += 1
                ins.then_inc(made, 1)
                pool.wait_ge(made, count[0])

            def keep(view, pattern, base, cm, op, fill=0.0):
                link(nc.gpsimd.affine_select(out=view, in_=view, compare_op=op, fill=fill, base=base,
                                             pattern=pattern, channel_multiplier=cm))

            link(nc.gpsimd.memset(ident[:, :], 1.0))
            keep(ident[:, :], [[-1, P]], 0, 1, ALU.is_equal)
            nc.gpsimd.memset(ones_row[:, :], 1.0).then_inc(sem("ident_ready"), 1)
            link(nc.gpsimd.memset(sel4[:, :, :], 1.0))
            keep(sel4[:, :, :], [[-1, MH], [0, P]], 0, 1, ALU.is_equal)
            link(nc.gpsimd.memset(sel8[:, :, :], 1.0))
            keep(sel8[:, :, :], [[-1, FH], [0, P]], 0, 1, ALU.is_equal)
            link(nc.gpsimd.memset(mask_m[:, :, :, :], 1.0))
            for sb in range(NT):
                keep(mask_m[:, 0, sb, :], [[1, S]], -sb * P, -1, ALU.is_ge)
                keep(mask_m[:, 1, sb, :], [[-1, S]], sb * P, 1, ALU.is_ge)
            link(nc.gpsimd.memset(mask_f[:, :], 0.0))
            keep(mask_f[:, :], [[-1, S]], P, 1, ALU.is_ge, NEG)
            link(nc.gpsimd.memset(mask_r[:, :], 1.0))
            for half in range(2):
                v = mask_r[64 * half:64 * half + 64, :]
                keep(v[:, 0:64], [[1, 64]], -1, -1, ALU.is_ge)
                keep(v[:, 64:128], [[1, 64]], 0, -1, ALU.is_ge)
            link(nc.gpsimd.memset(blk_ones[:, :], 0.0))
            link(nc.gpsimd.memset(blk_ones[0:64, 0:64], 1.0))
            link(nc.gpsimd.memset(blk_ones[64:128, 64:128], 1.0))
            link(nc.gpsimd.memset(blk16[:, :], 1.0))
            keep(blk16[:, :], [[-BLK, 64 // BLK], [0, BLK]], 0, 1, ALU.is_ge)
            keep(blk16[:, :], [[BLK, 64 // BLK], [0, BLK]], BLK - 1, -1, ALU.is_ge)
            link(nc.gpsimd.memset(resets[:, :], 1.0))
            link(nc.gpsimd.memset(resets[:, :].rearrange("p (c t) -> p c t", t=CH_T)[:, :, 0:1], 0.0))
            link(nc.gpsimd.iota(iota_f[:, :], [[1, P]], base=0, channel_multiplier=0,
                                allow_small_or_imprecise_dtypes=True))
            nc.gpsimd.memset(eps_c[:, 0:1], 1.0).then_inc(sem("consts_ready"), 1)

            def split_low(n, slot):
                pool.wait_ge(w_hi, n + 1)
                nc.gpsimd.tensor_tensor(WL[:, slot, :], RAW[:, slot, :], plain(WH[:, slot, :]),
                                        ALU.subtract).then_inc(w_lo, 1)

            full = (N_ITEMS // RING) * RING
            with pool.Fori(0, N_ITEMS // RING) as i:
                for slot in range(RING):
                    split_low(i * RING + slot, slot)
            for n in range(full, N_ITEMS):
                split_low(n, n % RING)

        @block.scalar
        def _(act):
            A = nc.scalar.activation
            feed_at = [0]

            def split_high(n, slot, used=None):
                act.wait_ge(w_landed[slot], landed_value(n))
                if used is not None:
                    act.wait_ge(w_used, used)
                nc.scalar.copy(WH[:, slot, :], RAW[:, slot, :]).then_inc(w_hi, 1)

            def landed_value(n):
                return 16 * (n // RING + 1)

            def feed(last):
                while feed_at[0] <= min(last + RING - 1, N_ITEMS - 1):
                    n = feed_at[0]
                    split_high(n, n % RING, n + 1 - RING if n >= RING else None)
                    feed_at[0] += 1

            def used(n):
                feed(n)
                act.wait_ge(w_used, n + 1)

            act.dma_start(vec[:, :], vec_in).then_inc(sem("vec_landed"), 16)
            act.dma_start(gw[:, :, :], gate_w_in).then_inc(sem("gw_landed"), 16)
            act.dma_start(mbias[:, :], mb_in).then_inc(sem("mb_landed"), 16)
            act.dma_start(fbias[:, :], fb_in).then_inc(sem("fb_landed"), 16)
            act.dma_start(P2[:, :, :], p_in.rearrange("(t p) d -> p t d", p=P)).then_inc(sem("p_landed"), 16)
            act.dma_start(brow[:, :], rows_in[1:2, :]).then_inc(sem("brow_landed"), 16)
            act.dma_start(nfin[:, :], rows_in[0:1, :].broadcast_to([P, D])).then_inc(sem("nfin_landed"), 16)

            def root(r, src, dst, msem):
                act.wait_ge(sem("ms_ready"), msem)
                A(dst, src, ACT.Sqrt).then_inc(sem("sq_ready"), 1)

            def sumsq(r, h_sem, h_val):
                act.wait_ge(sem(h_sem), h_val)
                for t in range(NT):
                    A(XS[:, t, :], H[:, t, :], ACT.Square, accum_out=ST[:, 2 * r + t:2 * r + t + 1]).then_inc(
                        sem("ss_ready"), 1)

            def evac_high(r, gain):
                for c in range(KC):
                    act.wait_ge(sem("tr_ready"), 4 * r + c // 2 + 1)
                    src = PS[:, 4 + c // 2, (c % 2) * S:(c % 2 + 1) * S]
                    A(XH[:, c, :], src, ACT.Copy, scale=col(gain, c) if gain else 1.0).then_inc(sem("xh_ready"), 1)

            feed(0)
            act.wait_ge(sem("gw_landed"), 16)
            nc.scalar.copy(GWH[:, :, :], gw[:, :, :])
            nc.scalar.copy(FWH[:, :, :], gw[:, :, 16:24]).then_inc(sem("gwh_ready"), 1)

            sumsq(0, "x_landed", 16)
            root(0, ST[:, 16:18], ST[:, 16:18], 1)
            act.wait_ge(sem("vec_landed"), 16)
            evac_high(T_MIX, "norm_mix")

            f2 = GR[:, :, :].rearrange("h (d k) s -> h d k s", k=2)[:, :, 1, :]
            act.wait_ge(sem("gr_ready"), 1)
            A(GA[:, 2:4, :], f2, ACT.Abs).then_inc(sem("g_act"), 1)
            act.wait_ge(sem("g_act"), 1)
            A(GA[:, 2:4, :], GA[:, 2:4, :], ACT.Exp, scale=-1.0).then_inc(sem("g_act"), 1)
            act.wait_ge(sem("g_act"), 2)
            act.wait_ge(sem("consts_ready"), 1)
            A(GA[:, 2:4, :], GA[:, 2:4, :], ACT.Ln, bias=eps_c[0:MH, 0:1]).then_inc(sem("g_act"), 1)
            act.wait_ge(sem("m_ready"), 1)
            A(GA[:, 0:2, :], GA[:, 0:2, :], ACT.Exp, scale=-1.0).then_inc(sem("emt_ready"), 1)

            for g in range(2):
                used(FIRST["o"] + 4 * g + 3)
                for t in range(NT):
                    last = A(og[:, t, g * 512:(g + 1) * 512], PS[:, 2 * (g % 2) + t, :], ACT.Sigmoid)
                last.then_inc(sem("o_out"), 1)

            for e in range(2 * MH):
                act.wait_ge(sem("w_ready"), e + 1)
                A(WE[:, e % 2], WE[:, e % 2], ACT.Exp, scale=-1.0).then_inc(sem("e_ready"), 1)
            act.wait_ge(sem("fin_done"), 2 * MH)
            for t in range(NT):
                for h in range(MH):
                    last = A(XS[:, t, h * MDV:(h + 1) * MDV], hacc[:, t, h * MDV:(h + 1) * MDV], ACT.Square,
                             accum_out=ST[:, 24 + 4 * t + h:25 + 4 * t + h])
            last.then_inc(sem("hss_ready"), 1)
            root(0, ST[:, 32:40], ST[:, 32:40], 2)
            evac_high(T_HEADS, "head_norm")

            feed(FIRST["mix_out"] + 7)
            sumsq(1, "h_ready", 1)
            root(1, ST[:, 18:20], ST[:, 18:20], 3)
            evac_high(T_MLP, "norm_mlp")

            def z_high(m):
                act.wait_ge(sem("zf_ready"), m + 1)
                nc.scalar.copy(ZH[:, m, :], ZF[:, m % 4, :]).then_inc(sem("zh_ready"), 1)

            for m in range(32):
                used(FIRST["w1"] + m)
                if m >= 4:
                    act.wait_ge(sem("zf_ready"), m - 3)
                A(RT[:, m % 4, :], PS[:, 4 + m % 4, 0:S], ACT.Relu).then_inc(sem("relu_ready"), 1)
                if m >= 1:
                    z_high(m - 1)
            z_high(31)

            feed(FIRST["w2"] + 31)
            sumsq(2, "h_ready", 2)
            root(2, ST[:, 20:22], ST[:, 20:22], 4)
            evac_high(T_PLE, "norm_ple")
            act.wait_ge(sem("ptr_ready"), 1)
            nc.scalar.copy(PTH[:, :, :], PS[:, 0, :].rearrange("p (c s) -> p c s", c=2)).then_inc(sem("pth_ready"), 1)
            for g in range(2):
                used(FIRST["ple_gate"] + 4 * g + 3)
                for t in range(NT):
                    last = A(SGP[:, t, g * 512:(g + 1) * 512], PS[:, 2 * (g % 2) + t, :], ACT.Sigmoid)
                last.then_inc(sem("sgp_out"), 1)

            feed(FIRST["ple"] + 1)
            sumsq(3, "h_ready", 3)
            root(3, ST[:, 22:24], ST[:, 22:24], 5)
            act.dma_start(lora[:, :, :], lora_in).then_inc(sem("lora_landed"), 16)
            evac_high(T_X1, None)

            for m in range(RW_CHUNKS):
                used(FIRST["rwkv"] + m)
                if m == 0:
                    act.wait_ge(sem("z_zero"), 1)
                nc.scalar.copy(Z[:, m, 1:S + 1], PS[:, 4 + m % 4, 0:S]).then_inc(sem("b2_out"), 1)
            for m in range(8):
                used(FIRST["fox_qk"] + m)
                nc.scalar.copy(fqk[:, m, :], PS[:, 4 + (RW_CHUNKS + m) % 4, 0:S]).then_inc(sem("b2_out"), 1)
            act.wait_ge(sem("sh_ready"), RW_CHUNKS)
            A(LT[0:64, 0, :], SH[0:64, 12, :], ACT.Tanh)
            nc.scalar.copy(LT[64:128, 0, :], SH[64:128, 12, :])
            A(LT[:, 1, :], SH[:, 13, :], ACT.Sigmoid).then_inc(sem("lt_ready"), 1)
            feed(FIRST["fox_v"] + 3)
            act.wait_ge(sem("fr_ready"), 1)
            A(fr[:, 1, :], fr[:, 0, :], ACT.Abs).then_inc(sem("f_act"), 1)
            act.wait_ge(sem("f_act"), 1)
            A(fr[:, 1, :], fr[:, 1, :], ACT.Exp, scale=-1.0).then_inc(sem("f_act"), 1)
            act.wait_ge(sem("f_act"), 2)
            A(fr[:, 1, :], fr[:, 1, :], ACT.Ln, bias=eps_c[0:FH, 0:1]).then_inc(sem("f_act"), 1)
            act.wait_ge(sem("lora_mm"), 1)
            for c in range(4):
                last = A(T[4][:, c, :], PS[:, 4 + c // 2, (c % 2) * S:(c % 2 + 1) * S], ACT.Sigmoid, bias=col("w0", c))
            last.then_inc(sem("sigw_ready"), 1)
            for c in range(4):
                last = A(T[3][:, c, :], PS[:, 6 + c // 2, (c % 2) * S:(c % 2 + 1) * S], ACT.Sigmoid, bias=col("a0", c))
            last.then_inc(sem("aa_ready"), 1)
            act.wait_ge(sem("lora_mm"), 2)
            nc.scalar.copy(GG[:, :, :].rearrange("p c s -> p (c s)"), PS[:, 0:2, :].rearrange("p b n -> p (b n)")).then_inc(
                sem("gg_ready"), 1)
            feed(FIRST["gates"])
            act.wait_ge(sem("lg_ready"), 2)
            A(T[0][:, :, :], T[5][:, :, :], ACT.Exp, scale=-DECAY)
            A(T[1][:, :, :], T[5][:, :, :], ACT.Exp, scale=DECAY)
            A(T[2][:, :, :], T[2][:, :, :], ACT.Exp, scale=-DECAY).then_inc(sem("gdec_ready"), 1)

            def gate_out(g):
                used(FIRST["gates"] + 4 * g + 3)
                for t in range(NT):
                    last = A(SG[:, t, g * 512:(g + 1) * 512], PS[:, 2 * ((g + 1) % 2) + t, :], ACT.Sigmoid)
                last.then_inc(sem("gate_out"), 1)

            gate_out(0)
            root(0, T[7][:, :, :], T[7][:, :, :], 6)
            gate_out(1)
            gate_out(2)
            gate_out(3)

            def f_exp(h):
                act.wait_ge(sem("fmax_ready"), h + 1)
                s0 = 64 + 8 * (h % 2)
                A(fp[:, h % 2, 0:P], fp[:, h % 2, 0:P], ACT.Exp, bias=ST[:, s0 + 2:s0 + 3], scale=FD ** -0.5,
                  accum_out=ST[:, s0 + 4:s0 + 5])
                A(fp[:, h % 2, P:384], fp[:, h % 2, P:384], ACT.Exp, bias=ST[:, s0 + 3:s0 + 4], scale=FD ** -0.5,
                  accum_out=ST[:, s0 + 5:s0 + 6]).then_inc(sem("fexp_ready"), 1)

            def f_pt(h):
                act.wait_ge(sem("fpt_mm"), h + 1)
                if h >= 2:
                    act.wait_ge(sem("fo_mm"), h - 1)
                nc.scalar.copy(fpt[:, h % 2, :], PS[:, 6 + h % 2, 0:384]).then_inc(sem("fpt_ready"), 1)

            for h in range(FH + 1):
                if h < FH:
                    f_exp(h)
                if h >= 1:
                    f_pt(h - 1)
            act.wait_ge(sem("fo_mm"), FH)
            nc.scalar.copy(YFH[:, :, :].rearrange("p c s -> p (c s)"), PS[:, 0:2, :].rearrange("p b n -> p (b n)")).then_inc(
                sem("yfh_ready"), 1)

            act.wait_ge(sem("bkt_mm"), 1)
            nc.scalar.copy(BKT[:, :, :, :].rearrange("p c q n -> p (c q n)"),
                           PS[:, 0:4, :].rearrange("p b n -> p (b n)")).then_inc(sem("bkt_ready"), 1)
            act.wait_ge(sem("uv_mm"), 1)
            nc.scalar.copy(UV[:, :, :, :].rearrange("p c q n -> p (c q n)"),
                           PS[:, 4:8, :].rearrange("p b n -> p (b n)")).then_inc(sem("uv_ready"), 1)
            for half in range(2):
                for k, (_, _, dst, adds, _) in enumerate(INVERSE):
                    if adds:
                        continue
                    act.wait_ge(sem("inv_mm"), half * len(INVERSE) + k + 1)
                    b = 2 * (k % 4)
                    nc.scalar.copy(inv[dst][:, :, :].rearrange("p u n -> p (u n)"),
                                   PS[0:64, b:b + 2, :].rearrange("p b n -> p (b n)")).then_inc(sem("inv_copied"), 1)
            for c in range(NCH):
                act.wait_ge(sem("u_mm"), c + 1)
                nc.scalar.copy(UV[0:64, c, :, :].rearrange("p q n -> p (q n)"), PS[0:64, 1, :]).then_inc(sem("u_ready"), 1)
                act.wait_ge(sem("y_mm"), c + 1)
                nc.scalar.copy(YT[:, :, c * CH_T:(c + 1) * CH_T],
                               PS[:, 2, 0:S].rearrange("p (q t) -> p q t", q=NPAIR)).then_inc(sem("yt_ready"), 1)
            root(0, T[2][:, :, :], T[2][:, :, :], 7)
            act.wait_ge(sem("yr_ready"), 1)
            nc.scalar.copy(YRH[:, :, :], YC[:, :, :]).then_inc(sem("yrh_ready"), 1)
            feed(FIRST["p_rwkv"] + 3)
            act.wait_ge(w_used, FIRST["p_rwkv"])
            act.dma_start(LG1[:, :], rows_in[2:3, :].broadcast_to([P, D])).then_inc(sem("ln1_landed"), 16)
            act.dma_start(LB1[:, :], rows_in[3:4, :].broadcast_to([P, D])).then_inc(sem("ln1_landed"), 16)
            evac_high(T_MERGED, None)
            feed(FIRST["w_o"] + 7)

            def layer_norm(k, h_val, ms_val):
                act.wait_ge(sem("h_ready"), h_val)
                for t in range(NT):
                    A(XS[:, t, :], H[:, t, :], ACT.Copy, accum_out=ST[:, 80 + 2 * k + t:81 + 2 * k + t]).then_inc(
                        sem("sum_ready"), 1)
                for t in range(NT):
                    act.wait_ge(sem("xc_ready"), 2 * k + t + 1)
                    A(XS[:, t, :], H[:, t, :], ACT.Square, accum_out=ST[:, 88 + 2 * k + t:89 + 2 * k + t]).then_inc(
                        sem("var_ready"), 1)
                root(0, ST[:, 96 + 2 * k:98 + 2 * k], ST[:, 96 + 2 * k:98 + 2 * k], ms_val)

            layer_norm(0, 5, 8)
            evac_high(T_X2, None)
            for m in range(LISTS):
                used(FIRST["peer_q"] + m)
                nc.scalar.copy(QH[:, m, :], PS[:, 4 + m % 4, 0:S]).then_inc(sem("qh_ready"), 1)
            used(FIRST["keys"] + 1)
            for t in range(NT):
                nc.scalar.copy(SC[:, t, :, :].rearrange("p l k -> p (l k)"),
                               PS[:, 4 * t:4 * t + 4, :].rearrange("p b n -> p (b n)")).then_inc(sem("u_bank_free"), 1)

            U0 = FIRST["u"]
            feed(U0 - 1 + 1)
            assert feed_at[0] == U0 + RING

            def u_evac(i, half, static):
                act.wait_ge(w_used, U0 + 4 * i + 2 * half + 2)
                nc.scalar.copy(HS[:, bass.ds(4 * i + 2 * half, 2), :],
                               PS[:, half, :].rearrange("p (j s) -> p j s", j=2)).then_inc(sem("u_bank_free"), 1)

            def u_body(i):
                for half in range(2):
                    for c in (2 * half, 2 * half + 1):
                        n = 4 * i + RING + c
                        split_high_dyn(U0, n, c)
                    u_evac(i, half, False)

            def split_high_dyn(first, rel, c):
                slot = (first + c) % RING
                act.wait_ge(w_landed[slot], 16 * ((first + c) // RING + 1) + 4 * (rel - c))
                act.wait_ge(w_used, rel + (first + 1 - RING))
                nc.scalar.copy(WH[:, slot, :], RAW[:, slot, :]).then_inc(w_hi, 1)

            with act.Fori(0, NK // 8) as i:
                u_body(i)
            act.wait_ge(sem("bv_ready"), 1)
            A(be[:, :, :, :], be[:, :, :, :], ACT.Exp).then_inc(sem("bexp_ready"), 1)
            act.wait_ge(sem("ijg_ready"), 1)
            act.wait_ge(sem("ijg_mm"), 1)
            nc.scalar.copy(IT[:, :], PS[:, 2, 0:S])
            nc.scalar.copy(JT[:, :], PS[:, 2, S:2 * S])
            nc.scalar.copy(GT[:, :], PS[:, 3, 0:S]).then_inc(sem("ijgT_ready"), 1)
            with act.Fori(NK // 8, NK // 4) as i:
                u_body(i)
            feed_at[0] = FIRST["v_table"] + RING

            def x_evac(q, g, first):
                act.wait_ge(sem("x_tr"), q + 1)
                if not first:
                    act.wait_ge(sem("r_mm"), q - 1)
                nc.scalar.copy(AT4[:, g, :, :].rearrange("p a n -> p (a n)"),
                               PS[:, 4 + g, 0:256].bitcast(BF16)).then_inc(sem("at_ready"), 1)

            for g in range(2):
                x_evac(g, g, True)
            with act.Fori(1, S // 8) as i:
                for g in range(2):
                    x_evac(2 * i + g, g, False)
            act.wait_ge(sem("hx_done"), S // 4)
            A(HT[:, :], HT[:, :], ACT.Gelu).then_inc(sem("gelu_ready"), 1)
            act.dma_start(LG2[:, :], rows_in[4:5, :].broadcast_to([P, D])).then_inc(sem("ln2_landed"), 16)
            act.dma_start(LB2[:, :], rows_in[5:6, :].broadcast_to([P, D])).then_inc(sem("ln2_landed"), 16)

            def c_evac(q, g):
                act.wait_ge(sem("c_mm"), q + 1)
                nc.scalar.copy(HS[:, :, bass.ds(4 * q, 4)].rearrange("p j a -> p a j"),
                               PS[:, g, :].rearrange("p (a j) -> p a j", a=4)).then_inc(sem("c_out"), 1)

            with act.Fori(0, S // 8) as i:
                for g in range(2):
                    c_evac(2 * i + g, g)

            V0 = FIRST["v_table"]

            def c_high(j, slot, first=False):
                if not first:
                    act.wait_ge(w_used, j + (V0 + 1 - RING))
                nc.scalar.copy(CH[:, slot, :], HS[:, j, :] if isinstance(j, int) else HS[:, bass.ds(j, 1), :].rearrange(
                    "p a s -> p (a s)")).then_inc(sem("ch_ready"), 1)

            act.wait_ge(sem("c_out"), S // 4)
            for c in range(RING):
                c_high(c, c, True)
            with act.Fori(0, NK // 4 - 1) as i:
                for c in range(4):
                    split_high_dyn(V0, 4 * i + RING + c, c)
                    c_high(4 * i + RING + c, c)
            layer_norm(1, 7, 9)

        @block.tensor
        def _(pe):
            mm = nc.tensor.matmul
            tp = nc.tensor.transpose

            def transposes(r, src, name, value):
                if value is not None:
                    pe.wait_ge(sem(name), value)
                for c in range(KC):
                    for t in range(NT):
                        last = tp(PS[:, 4 + c // 2, (c % 2) * S + t * P:(c % 2) * S + (t + 1) * P],
                                  src[:, t, c * P:(c + 1) * P], ident[:, :])
                    if c % 2:
                        last.then_inc(sem("tr_ready"), 1)

            def split(pairs, dst, start, stop):
                for k, (a, b) in enumerate(pairs):
                    last = mm(dst, a, b, start=start and k == 0, stop=stop and k == len(pairs) - 1)
                return last

            def form_a(first, groups, per_group, xh, xl, bank=lambda g: 2 * (g % 2), free=None, seed=None, ready=None):
                n = first
                for g in range(groups):
                    if free:
                        free(g)
                    if seed:
                        seed(g)
                    for i in range(per_group):
                        if ready and g == 0:
                            ready(i)
                        pe.wait_ge(w_lo, n + 1)
                        for kk in range(2):
                            k = 2 * i + kk
                            wh = WH[:, n % RING, kk * 512:(kk + 1) * 512]
                            wl = WL[:, n % RING, kk * 512:(kk + 1) * 512]
                            for t in range(NT):
                                h, l = xh[:, k, t * P:(t + 1) * P], xl[:, k, t * P:(t + 1) * P]
                                last = split([(h, wh), (h, wl), (l, wh)], PS[:, bank(g) + t, :],
                                             k == 0 and not seed, k == 2 * per_group - 1)
                        last.then_inc(w_used, 1)
                        n += 1

            def form_b(first, count, place, free):
                for m in range(count):
                    n = first + m
                    free(m)
                    pe.wait_ge(w_lo, n + 1)
                    for k in range(KC):
                        wh, wl = WH[:, n % RING, k * P:(k + 1) * P], WL[:, n % RING, k * P:(k + 1) * P]
                        last = split([(wh, XH[:, k, :]), (wh, XL[:, k, :]), (wl, XH[:, k, :])], place(m),
                                     k == 0, k == KC - 1)
                    last.then_inc(w_used, 1)

            def wait(name, value):
                if value > 0:
                    pe.wait_ge(sem(name), value)

            def small_gates(bank, wh, wl, n):
                for t in range(NT):
                    for k in range(KC):
                        h, l = XH[:, k, t * P:(t + 1) * P], XL[:, k, t * P:(t + 1) * P]
                        last = split([(h, wh[:, k]), (h, wl[:, k]), (l, wh[:, k])], PS[:, bank, t * n:(t + 1) * n],
                                     k == 0, k == KC - 1)
                return last

            pe.wait_ge(sem("ident_ready"), 1)
            transposes(T_MIX, XS, "xs_ready", 2)
            wait("xl_ready", 8)
            wait("gwl_ready", 1)
            small_gates(3, GWH[:, :, 0:16], GWL[:, :, 0:16], 16).then_inc(sem("gates_mm"), 1)
            wait("gtok_ready", 1)
            for c in range(4):
                for t in range(NT):
                    last = tp(PS[0:MH, 1 + c // 2, (c % 2) * S + t * P:(c % 2) * S + (t + 1) * P],
                              gtok[:, t, 4 * c:4 * c + 4], ident[:, :])
            last.then_inc(sem("grow_mm"), 1)
            form_b(FIRST["qk"], 8, lambda m: PS[:, 4 + m % 4, 0:S], lambda m: wait("qk_out", m - 3))
            wait("gr_ready", 1)
            form_a(FIRST["v"], 2, 4, XH, XL)
            form_a(FIRST["o"], 2, 4, XH, XL, free=lambda g: wait("v_out", g + 1))

            wait("m_ready", 1)
            wait("emt_ready", 1)
            wait("qk_out", 8)
            for k in range(2):
                for d in range(2):
                    for t in range(NT):
                        j = 4 * k + 2 * d + t
                        row = (4 if k == 0 else 0) + d
                        last = tp(PS[:, 7, 4 * j:4 * j + 4], GA[:, row, t * P:(t + 1) * P], ident[0:MH, 0:MH])
            last.then_inc(sem("at_mm"), 1)
            wait("at_ready_m", 1)
            wait("consts_ready", 1)

            def scores(h):
                wait("sm_ready", 2 * h - 2)
                for sb in range(NT):
                    last = mm(PS[:, 4 + h % 2, sb * S:(sb + 1) * S], qkT[:, MH + h, sb * P:(sb + 1) * P],
                              qkT[:, h, :], start=True, stop=True)
                last.then_inc(sem("st_mm"), 1)
                wait("w_ready", 2 * h - 2)
                for d in range(2):
                    last = mm(PS[:, 6 + h % 2, d * S:(d + 1) * S], sel4[:, h, :], GA[:, 6 + d, :], start=True,
                              stop=True)
                last.then_inc(sem("mb_mm"), 1)

            def numerators(e):
                h, d = e // 2, e % 2
                wait("p_ready", e + 1)
                if e < 2:
                    wait("o_out", 2)
                wait("fin_done", e - 1)
                for t in range(NT):
                    sources = range(0, t + 1) if d == 0 else range(t, NT)
                    for sb in sources:
                        last = mm(PS[:, 2 * (e % 2) + t, 0:MDV + 1], SM[:, e % 2, sb, t * P:(t + 1) * P],
                                  v1[:, sb, h, :], start=(sb == sources[0]), stop=(sb == sources[-1]))
                last.then_inc(sem("num_mm"), 1)

            scores(0)
            for e in range(2 * MH):
                if e % 2 == 0 and e + 2 < 2 * MH:
                    scores(e // 2 + 1)
                numerators(e)
            transposes(T_HEADS, XS, "xs_ready", 4)
            wait("xl_ready", 16)
            form_a(FIRST["mix_out"], 2, 4, XH, XL)

            transposes(T_MLP, XS, "xs_ready", 6)
            wait("xl_ready", 24)
            form_b(FIRST["w1"], 32, lambda m: PS[:, 4 + m % 4, 0:S], lambda m: wait("relu_ready", m - 3))
            form_a(FIRST["w2"], 2, 16, ZH, ZL, ready=lambda i: wait("zl_ready", 2 * i + 2))

            transposes(T_PLE, XS, "xs_ready", 8)
            wait("p_landed", 16)
            for c in range(2):
                for t in range(NT):
                    last = tp(PS[:, 0, c * S + t * P:c * S + (t + 1) * P], P2[:, t, c * P:(c + 1) * P], ident[:, :])
            last.then_inc(sem("ptr_ready"), 1)
            wait("xl_ready", 32)
            wait("ptl_ready", 1)
            wait("brow_landed", 16)

            def bias(g):
                for t in range(NT):
                    mm(PS[:, 2 * (g % 2) + t, :], ones_row[0:1, :], brow[0:1, g * 512:(g + 1) * 512], start=True,
                       stop=False)

            form_a(FIRST["ple_gate"], 2, 4, XH, XL, seed=bias)
            form_a(FIRST["ple"], 2, 1, PTH, PTL, free=lambda g: wait("sgp_out", g + 1))

            transposes(T_X1, H, "h_ready", 4)
            wait("xl_ready", 40)
            form_b(FIRST["rwkv"], RW_CHUNKS, lambda m: PS[:, 4 + m % 4, 0:S], lambda m: wait("b2_out", m - 3))
            form_b(FIRST["fox_qk"], 8, lambda m: PS[:, 4 + (RW_CHUNKS + m) % 4, 0:S],
                   lambda m: wait("b2_out", RW_CHUNKS + m - 3))
            small_gates(3, FWH, FWL, 8).then_inc(sem("f_mm"), 1)
            form_a(FIRST["fox_v"], 1, 4, XH, XL)
            wait("ftok_ready", 1)
            for t in range(NT):
                last = tp(PS[0:FH, 2, t * P:(t + 1) * P], ftok[:, t, :], ident[:, :])
            last.then_inc(sem("frow_mm"), 1)
            wait("lt_ready", 1)
            wait("lora_landed", 16)
            wait("b2_out", RW_CHUNKS + 8)
            for c in range(4):
                mm(PS[:, 4 + c // 2, (c % 2) * S:(c % 2 + 1) * S], lora[0:64, 0, c * P:(c + 1) * P], LT[0:64, 0, :],
                   start=True, stop=True)
            for c in range(4):
                last = mm(PS[:, 6 + c // 2, (c % 2) * S:(c % 2 + 1) * S], lora[64:128, 0, c * P:(c + 1) * P],
                          LT[64:128, 0, :], start=True, stop=True)
            last.then_inc(sem("lora_mm"), 1)
            wait("fv_ready", 1)
            for c in range(4):
                last = mm(PS[:, c // 2, (c % 2) * S:(c % 2 + 1) * S], lora[:, 1, c * P:(c + 1) * P], LT[:, 1, :],
                          start=True, stop=True)
            last.then_inc(sem("lora_mm"), 1)
            wait("fr_ready", 1)

            def gates(g, free=None):
                form_a(FIRST["gates"] + 4 * g, 1, 4, XH, XL, bank=lambda _: 2 * ((g + 1) % 2), free=free)

            gates(0)
            wait("kksq_ready", 1)
            wait("sigw_ready", 1)
            for b in range(2):
                last = mm(PS[:, 4 + b, :], blk_ones[:, :], T[7][:, 2 * b:2 * b + 2, :], start=True, stop=True)
            last.then_inc(sem("kkss_mm"), 1)
            gates(1, lambda _: wait("gg_ready", 1))
            wait("bonp_ready", 1)
            wait("aa_ready", 1)
            for b in range(2):
                last = mm(PS[:, 6 + b, :], blk_ones[:, :], T[7][:, 2 * b:2 * b + 2, :], start=True, stop=True)
            last.then_inc(sem("bon_mm"), 1)
            gates(2, lambda _: wait("gate_out", 1))
            gates(3, lambda _: wait("gate_out", 2))

            wait("nc8_ready", 1)
            wait("nk_ready", 1)
            wait("bon_ready", 1)
            wait("gate_out", 4)

            def f_scores(h):
                b = 64 * (h % 2)
                wait("fmax_ready", h - 1)
                for t in range(NT):
                    n = (t + 1) * P
                    dst = PS[:, 4 + h % 2, t * P:t * P + n]
                    mm(dst, fqk[b:b + 64, h // 2, t * P:(t + 1) * P], fqk[b:b + 64, 4 + h // 2, 0:n], start=True,
                       stop=False)
                    last = mm(dst, sel8[:, h, :], fr[:, 2, 0:n], start=False, stop=True)
                last.then_inc(sem("fs_mm"), 1)

            def f_transposes(h):
                wait("fnorm_ready", h + 1)
                wait("fpt_ready", h - 1)
                for k in range(3):
                    last = tp(PS[:, 6 + h % 2, k * P:(k + 1) * P], fp[:, h % 2, k * P:(k + 1) * P], ident[:, :])
                last.then_inc(sem("fpt_mm"), 1)

            def f_values(h):
                wait("fpt_ready", h + 1)
                b = 64 * (h % 2)
                for t in range(NT):
                    for sb in range(t + 1):
                        k = 0 if t == 0 else 1 + sb
                        last = mm(PS[b:b + 64, h // 4, (h // 2 % 2) * S + t * P:(h // 2 % 2) * S + (t + 1) * P],
                                  fv[:, sb, h * FD:(h + 1) * FD], fpt[:, h % 2, k * P:(k + 1) * P], start=(sb == 0),
                                  stop=(sb == t))
                last.then_inc(sem("fo_mm"), 1)

            f_scores(0)
            f_scores(1)
            for h in range(FH):
                f_transposes(h)
                if h + 2 < FH:
                    f_scores(h + 2)
                f_values(h)

            wait("bk_ready", 1)
            wait("yfh_ready", 1)
            wait("yfl_ready", 1)
            for c in range(NCH):
                for q in range(NPAIR):
                    last = tp(PS[:, c, q * P:(q + 1) * P], BK[:, q, c, :, :].rearrange("p a t -> p (a t)"), ident[:, :])
            last.then_inc(sem("bkt_mm"), 1)
            wait("bkt_ready", 1)
            for c in range(NCH):
                for h2 in range(2):
                    b = 64 * h2
                    for q in range(NPAIR):
                        last = mm(PS[:, 2 * c + h2, q * P:(q + 1) * P],
                                  BK[b:b + 64, q, c, :, :].rearrange("p a t -> p (a t)"),
                                  CR[b:b + 64, q, c, :, :].rearrange("p a t -> p (a t)"), start=True, stop=True)
                    last.then_inc(sem("sc_mm"), 1)
            wait("vp_ready", 1)
            for c in range(NCH):
                for q in range(NPAIR):
                    last = tp(PS[:, 4 + c, q * P:(q + 1) * P], BK[:, q, c, :, :].rearrange("p a t -> p (a t)"),
                              ident[:, :])
            last.then_inc(sem("uv_mm"), 1)
            wait("uv_ready", 1)

            for half in range(2):
                wait("inv_in", half + 1)
                adds0 = half * evacuated(len(INVERSE) - 1, True)
                copies0 = half * evacuated(len(INVERSE) - 1, False)
                for k, (a, b, dst, adds, need) in enumerate(INVERSE):
                    upto = max(need, k - 4)
                    wait("inv_added", adds0 + evacuated(upto, True))
                    wait("inv_copied", copies0 + evacuated(upto, False))
                    X = MINV[:, 2 * half:2 * half + 2, :, :].rearrange("p c u n -> p (c u) n")
                    bank = 2 * (k % 4)
                    for u in range(16):
                        dst = PS[0:64, bank + u // 8, (u % 8) * 64:(u % 8 + 1) * 64]
                        left = X[:, u, :] if a == "X" else inv[a][:, u, :]
                        if b == "I":
                            last = tp(dst, left, ident[0:64, 0:64])
                        else:
                            last = mm(dst, left, X[:, u, :] if b == "X" else inv[b][:, u, :], start=True, stop=True)
                    last.then_inc(sem("inv_mm"), 1)
            wait("inv_added", 2 * evacuated(len(INVERSE) - 1, True))

            for c in range(NCH):
                wait("s_ready", c)
                for q in range(NPAIR):
                    if c:
                        mm(PS[0:64, 0, q * P:(q + 1) * P], CR[:, q, c, 0, :], S2[:, q, :], start=True, stop=True)
                    for h2 in range(2):
                        last = mm(PS[0:64, 0, q * P + 64 * h2:q * P + 64 * h2 + 64], PK[:, c, h2, q, 0:64],
                                  UV[:, c, q, 64 * h2:64 * h2 + 64], start=(c == 0), stop=True,
                                  skip_group_check=True)
                last.then_inc(sem("z_mm"), 1)
                wait("zs_ready", c + 1)
                for q in range(NPAIR):
                    for h2 in range(2):
                        k = q * P + 64 * h2
                        last = mm(PS[0:64, 1, k:k + 64], MINV[:, c, h2 * NPAIR + q, :], ZS[:, k:k + 64], start=True,
                                  stop=True)
                last.then_inc(sem("u_mm"), 1)
                wait("u_ready", c + 1)
                for q in range(NPAIR):
                    last = mm(PS[:, 3, q * P:(q + 1) * P], BKT[:, c, q, :], UV[:, c, q, :], start=True, stop=True)
                last.then_inc(sem("su_mm"), 1)
                wait("yt_ready", c)
                for q in range(NPAIR):
                    if c:
                        mm(PS[:, 2, q * 64:(q + 1) * 64], S2[:, q, :], CR[:, q, c, 1, :], start=True, stop=True)
                    for h2 in range(2):
                        last = mm(PS[64 * h2:64 * h2 + 64, 2, q * 64:(q + 1) * 64], UV[:, c, q, 64 * h2:64 * h2 + 64],
                                  PK[:, c, h2, q, 64:128], start=(c == 0), stop=True,
                                  skip_group_check=True)
                last.then_inc(sem("y_mm"), 1)
            wait("yt_ready", NCH)
            for b in range(2):
                last = mm(PS[:, 4 + b, :], blk_ones[:, :], YT[:, 2 * b:2 * b + 2, :], start=True, stop=True)
            last.then_inc(sem("gn_mm"), 1)
            wait("ysq_ready", 1)
            for b in range(2):
                last = mm(PS[:, 6 + b, :], blk_ones[:, :], T[0][:, 2 * b:2 * b + 2, :], start=True, stop=True)
            last.then_inc(sem("gn_mm"), 1)

            form_a(FIRST["p_fox"], 2, 2, YFH, YFL)
            wait("yrl_ready", 1)
            form_a(FIRST["p_rwkv"], 2, 2, YRH, YRL, free=lambda g: wait("pf_out", g + 1))
            transposes(T_MERGED, XS, "xs_ready", 10)
            wait("xl_ready", 48)
            form_a(FIRST["w_o"], 2, 4, XH, XL)

            transposes(T_X2, H, "h_ready", 6)
            wait("xl_ready", 56)
            form_b(FIRST["peer_q"], LISTS, lambda m: PS[:, 4 + m % 4, 0:S], lambda m: wait("ql_ready", m - 3))
            wait("ql_ready", LISTS)
            for i in range(2):
                n = FIRST["keys"] + i
                pe.wait_ge(w_lo, n + 1)
                for j in range(LISTS // 2):
                    l = i * (LISTS // 2) + j
                    wh, wl = WH[:, n % RING, j * NK:(j + 1) * NK], WL[:, n % RING, j * NK:(j + 1) * NK]
                    for t in range(NT):
                        h, lo = QH[:, l, t * P:(t + 1) * P], QL[:, l, t * P:(t + 1) * P]
                        last = split([(h, wh), (h, wl), (lo, wh)], PS[:, 4 * t + l // 4, (l % 4) * NK:(l % 4 + 1) * NK],
                                     True, True)
                last.then_inc(w_used, 1)

            U0 = FIRST["u"]

            def u_body(i):
                for c in range(4):
                    slot = (U0 + c) % RING
                    if c % 2 == 0:
                        pe.wait_ge(sem("u_bank_free"), 2 * i + (c // 2 + 1))
                    pe.wait_ge(w_lo, 4 * i + (U0 + c + 1))
                    for k in range(KC):
                        wh, wl = WH[:, slot, k * P:(k + 1) * P], WL[:, slot, k * P:(k + 1) * P]
                        last = split([(wh, XH[:, k, :]), (wh, XL[:, k, :]), (wl, XH[:, k, :])],
                                     PS[:, c // 2, (c % 2) * S:(c % 2 + 1) * S], k == 0, k == KC - 1)
                    last.then_inc(w_used, 1)

            with pe.Fori(0, NK // 8) as i:
                u_body(i)
            wait("ijg_ready", 1)
            for a in range(3):
                for t in range(NT):
                    k = a * S + t * P
                    last = tp(PS[:, 2 + a // 2, (a % 2) * S + t * P:(a % 2) * S + (t + 1) * P], ijg[:, t, a, :],
                              ident[:, :])
            last.then_inc(sem("ijg_mm"), 1)
            with pe.Fori(NK // 8, NK // 4) as i:
                u_body(i)

            def x_transposes(q, g, first):
                pe.wait_ge(sem("a4_ready"), q + 1)
                if not first:
                    pe.wait_ge(sem("at_ready"), q - 1)
                for a in range(4):
                    last = tp(PS[:, 4 + g, 64 * a:64 * (a + 1)].bitcast(BF16), A4[:, g, a, :], ident_b[:, :])
                last.then_inc(sem("x_tr"), 1)

            def rows(q, g, first):
                pe.wait_ge(sem("at_ready"), q + 1)
                if not first:
                    pe.wait_ge(sem("hx_done"), q - 1)
                for a in range(4):
                    t = 4 * q + a
                    rhs = HS[:, :, t] if isinstance(t, int) else HS[:, :, bass.ds(t, 1)].rearrange("p j a -> p (j a)")
                    last = mm(PS[:, 6 + g, a * P:(a + 1) * P], AT4[:, g, a, :], rhs, start=True, stop=True)
                last.then_inc(sem("r_mm"), 1)

            wait("u_bank_free", 2 + NK // 2)
            x_transposes(0, 0, True)
            x_transposes(1, 1, True)
            rows(0, 0, True)
            x_transposes(2, 0, False)
            rows(1, 1, True)
            with pe.Fori(1, S // 8 - 1) as i:
                x_transposes(2 * i + 1, 1, False)
                rows(2 * i, 0, False)
                x_transposes(2 * i + 2, 0, False)
                rows(2 * i + 1, 1, False)
            x_transposes(S // 4 - 1, 1, False)
            rows(S // 4 - 2, 0, False)
            rows(S // 4 - 1, 1, False)

            def coefficients(q, g, first):
                pe.wait_ge(sem("b4_ready"), q + 1)
                if not first:
                    pe.wait_ge(sem("c_out"), q - 1)
                for a in range(4):
                    last = mm(PS[:, g, a * P:(a + 1) * P], A4F[:, g, a, :], B4F[:, g, a, :], start=True, stop=True)
                last.then_inc(sem("c_mm"), 1)

            for g in range(2):
                coefficients(g, g, True)
            with pe.Fori(1, S // 8) as i:
                for g in range(2):
                    coefficients(2 * i + g, g, False)

            V0 = FIRST["v_table"]

            def v_item(j, c, start=False, stop=False):
                slot = (V0 + c) % RING
                pe.wait_ge(w_lo, j + (V0 + 1))
                pe.wait_ge(sem("cl_ready"), j + 1)
                for t in range(NT):
                    h, l = CH[:, c, t * P:(t + 1) * P], CL[:, c, t * P:(t + 1) * P]
                    for half in range(2):
                        wh = WH[:, slot, half * 512:(half + 1) * 512]
                        wl = WL[:, slot, half * 512:(half + 1) * 512]
                        last = split([(h, wh), (h, wl), (l, wh)], PS[:, 2 * t + half, :], start, stop)
                last.then_inc(w_used, 1)

            wait("c_out", S // 4)
            for c in range(4):
                v_item(c, c, start=(c == 0))
            with pe.Fori(1, NK // 4 - 1) as i:
                for c in range(4):
                    v_item(4 * i + c, c)
            for c in range(4):
                v_item(NK - 4 + c, c, stop=(c == 3))

        @block.vector
        def _(dve):
            V = nc.vector
            step = sem("dve_step")
            steps = [0]

            def link(ins):
                steps[0] += 1
                ins.then_inc(step, 1)
                dve.wait_ge(step, steps[0])

            def wait(name, value):
                if value > 0:
                    dve.wait_ge(sem(name), value)

            def used(n):
                dve.wait_ge(w_used, n + 1)

            def mean_eps(dst, src, scale, eps):
                V.tensor_scalar(dst, src, scale, eps, ALU.mult, ALU.add).then_inc(sem("ms_ready"), 1)

            def normed(r, ss_val, root_val):
                wait("ss_ready", ss_val)
                rs = ST[:, 16 + 2 * r:18 + 2 * r]
                mean_eps(rs, ST[:, 2 * r:2 * r + 2], 1.0 / D, EPS)
                wait("sq_ready", root_val)
                link(V.reciprocal(rs, rs))

            def low_half(r, gain):
                for c in range(KC):
                    wait("xh_ready", 8 * r + c // 2 * 2 + 2)
                    V.scalar_tensor_tensor(XL[:, c, :], PS[:, 4 + c // 2, (c % 2) * S:(c % 2 + 1) * S],
                                           col(gain, c) if gain else 1.0, plain(XH[:, c, :]), ALU.mult,
                                           ALU.subtract).then_inc(sem("xl_ready"), 1)

            def scale_xs(r):
                for t in range(NT):
                    V.tensor_scalar(XS[:, t, :], H[:, t, :], ST[:, 16 + 2 * r + t:17 + 2 * r + t], None,
                                    ALU.mult).then_inc(sem("xs_ready"), 1)

            wait("consts_ready", 1)
            V.tensor_copy(iota_b[:, :], iota_f[:, :])
            V.tensor_copy(ident_b[:, :], ident[:, :])
            V.memset(v1[:, :, :, MDV:MDV + 1], 1.0)
            normed(0, 2, 1)
            scale_xs(0)
            wait("gwh_ready", 1)
            V.tensor_tensor(FWL[:, :, :], gw[:, :, 16:24], plain(FWH[:, :, :]), ALU.subtract)
            V.tensor_tensor(GWL[:, :, :], gw[:, :, :], plain(GWH[:, :, :]), ALU.subtract).then_inc(sem("gwl_ready"), 1)
            wait("vec_landed", 16)
            low_half(T_MIX, "norm_mix")

            wait("gates_mm", 1)
            V.tensor_copy(gtok[:, :, :].rearrange("p t g -> p (t g)"), PS[:, 3, 0:32]).then_inc(sem("gtok_ready"), 1)
            wait("grow_mm", 1)
            wait("mb_landed", 16)
            for k in range(4):
                last = V.tensor_scalar(GR[:, k, :], PS[0:MH, 1 + k // 2, (k % 2) * S:(k % 2 + 1) * S],
                                       mbias[:, k:k + 1], None, ALU.add)
            last.then_inc(sem("gr_ready"), 1)
            wait("gr_ready", 1)

            def qk_copy(m):
                used(FIRST["qk"] + m)
                V.tensor_copy(qkT[:, m, :], PS[:, 4 + m % 4, 0:S]).then_inc(sem("qk_out"), 1)

            for m in range(4):
                qk_copy(m)
            wait("g_act", 3)
            for d in range(2):
                f, i_ = GR[:, 2 * d + 1, :], GR[:, 2 * d, :]
                link(V.scalar_tensor_tensor(GA[:, 0, :], f, 0.0, GA[:, 2 + d, :], ALU.min, ALU.subtract))
                order = slice(None) if d == 0 else slice(None, None, -1)
                link(V.tensor_tensor_scan(GA[:, 2 + d, order], GA[:, 0, order], GA[:, 0, order], 0.0, ALU.add,
                                          ALU.bypass))
                link(V.tensor_tensor(GA[:, 4 + d, :], i_, GA[:, 2 + d, :], ALU.subtract))
                link(V.tensor_tensor_scan(GA[:, 6 + d, order], GA[:, 4 + d, order], GA[:, 4 + d, order], 0.0, ALU.max,
                                          ALU.bypass))
            V.tensor_tensor(GA[:, 0:2, :], GA[:, 2:4, :], GA[:, 6:8, :], ALU.add).then_inc(sem("m_ready"), 1)
            for m in range(4, 8):
                qk_copy(m)
            for g in range(2):
                used(FIRST["v"] + 4 * g + 3)
                for t in range(NT):
                    last = V.tensor_copy(v1[:, t, 2 * g:2 * g + 2, 0:MDV],
                                         PS[:, 2 * g + t, :].rearrange("p (h v) -> p h v", h=2))
                last.then_inc(sem("v_out"), 1)
            wait("at_mm", 1)
            V.tensor_copy(AT[:, :, :].rearrange("p j h -> p (j h)"), PS[:, 7, 0:32]).then_inc(sem("at_ready_m"), 1)
            wait("at_ready_m", 1)

            def exponents(e):
                h, d = e // 2, e % 2
                wait("mb_mm", h + 1)
                wait("p_ready", e - 1)
                for sb in range(NT):
                    a = AT[:, 2 * d + sb, h:h + 1]
                    last = V.tensor_scalar(WE[:, e % 2, sb, :], PS[:, 6 + h % 2, d * S:(d + 1) * S], a, 0.0,
                                           ALU.subtract, ALU.max)
                last.then_inc(sem("w_ready"), 1)

            def masked_scores(e):
                h, d = e // 2, e % 2
                wait("st_mm", h + 1)
                wait("num_mm", e - 1)
                V.scalar_tensor_tensor(SM[:, e % 2].rearrange("p a s -> p (a s)"), PS[:, 4 + h % 2, :], MDK ** -0.5,
                                       mask_m[:, d].rearrange("p a s -> p (a s)"), ALU.mult,
                                       ALU.mult).then_inc(sem("sm_ready"), 1)

            def weights_of(e):
                wait("e_ready", e + 1)
                wait("sm_ready", e + 1)
                V.tensor_tensor(SM[:, e % 2], SM[:, e % 2], WE[:, e % 2], ALU.mult).then_inc(sem("p_ready"), 1)

            def finish(e):
                h, d = e // 2, e % 2
                wait("num_mm", e + 1)
                wait("emt_ready", 1)
                den = [ST[:, 44 + 2 * (e % 2) + t:45 + 2 * (e % 2) + t] for t in range(NT)]
                raw = [PS[:, 2 * (e % 2) + t, MDV:MDV + 1] for t in range(NT)]
                least = [AT[:, 4 + 2 * d + t, h:h + 1] for t in range(NT)]
                for t in range(NT):
                    ins = V.tensor_scalar(den[t], raw[t], -1.0, least[t], ALU.mult, ALU.max)
                link(ins)
                for t in range(NT):
                    ins = V.scalar_tensor_tensor(den[t], raw[t], least[t], den[t], ALU.max, ALU.max)
                link(ins)
                both = ST[:, 44 + 2 * (e % 2):46 + 2 * (e % 2)]
                link(V.reciprocal(both, both))
                wait("fin_done", e)
                for t in range(NT):
                    num, acc = PS[:, 2 * (e % 2) + t, 0:MDV], hacc[:, t, h * MDV:(h + 1) * MDV]
                    if d == 0:
                        last = V.tensor_scalar(acc, num, den[t], None, ALU.mult)
                    else:
                        last = V.scalar_tensor_tensor(acc, num, den[t], acc, ALU.mult, ALU.add)
                last.then_inc(sem("fin_done"), 1)

            for e in range(2 * MH + 2):
                if e < 2 * MH:
                    exponents(e)
                    masked_scores(e)
                if 1 <= e <= 2 * MH:
                    weights_of(e - 1)
                if e >= 2:
                    finish(e - 2)
            wait("hss_ready", 1)
            mean_eps(ST[:, 32:40], ST[:, 24:32], 1.0 / MDV, EPS)
            wait("sq_ready", 2)
            link(V.reciprocal(ST[:, 32:40], ST[:, 32:40]))
            wait("o_out", 2)
            for t in range(NT):
                for h in range(MH):
                    k = slice(h * MDV, (h + 1) * MDV)
                    last = V.scalar_tensor_tensor(XS[:, t, k], hacc[:, t, k], ST[:, 32 + 4 * t + h:33 + 4 * t + h],
                                                  og[:, t, k], ALU.mult, ALU.mult)
                last.then_inc(sem("xs_ready"), 1)
            low_half(T_HEADS, "head_norm")

            def add_to_h(first, per_group, alpha=None):
                for g in range(2):
                    used(first + per_group * (g + 1) - 1)
                    for t in range(NT):
                        k = slice(g * 512, (g + 1) * 512)
                        src = PS[:, 2 * (g % 2) + t, :]
                        if alpha is None:
                            last = V.tensor_tensor(H[:, t, k], H[:, t, k], src, ALU.add)
                        else:
                            last = V.scalar_tensor_tensor(H[:, t, k], H[:, t, k], alpha, src, ALU.mult, ALU.add)
                return last

            add_to_h(FIRST["mix_out"], 4).then_inc(sem("h_ready"), 1)

            normed(1, 4, 3)
            scale_xs(1)
            low_half(T_MLP, "norm_mlp")

            def z_low(m):
                wait("zh_ready", m + 1)
                V.tensor_tensor(ZL[:, m, :], ZF[:, m % 4, :], plain(ZH[:, m, :]), ALU.subtract).then_inc(
                    sem("zl_ready"), 1)

            for m in range(32):
                wait("relu_ready", m + 1)
                wait("zl_ready", m - 3)
                V.tensor_tensor(ZF[:, m % 4, :], RT[:, m % 4, :], RT[:, m % 4, :], ALU.mult).then_inc(
                    sem("zf_ready"), 1)
                if m >= 1:
                    z_low(m - 1)
            z_low(31)
            add_to_h(FIRST["w2"], 16).then_inc(sem("h_ready"), 1)

            normed(2, 6, 4)
            scale_xs(2)
            low_half(T_PLE, "norm_ple")
            wait("pth_ready", 1)
            V.tensor_tensor(PTL[:, :, :], PS[:, 0, :].rearrange("p (c s) -> p c s", c=2), plain(PTH[:, :, :]),
                            ALU.subtract).then_inc(sem("ptl_ready"), 1)
            wait("sgp_out", 2)
            for g in range(2):
                used(FIRST["ple"] + g)
                k = slice(g * 512, (g + 1) * 512)
                for t in range(NT):
                    ins = V.tensor_tensor(XS[:, t, k], PS[:, 2 * g + t, :], SGP[:, t, k], ALU.mult)
                link(ins)
                for t in range(NT):
                    last = V.tensor_tensor(H[:, t, k], H[:, t, k], XS[:, t, k], ALU.add)
            last.then_inc(sem("h_ready"), 1)
            normed(3, 8, 5)
            wait("nfin_landed", 16)
            for t in range(NT):
                last = V.scalar_tensor_tensor(H[:, t, :], H[:, t, :], ST[:, 22 + t:23 + t], nfin[:, :], ALU.mult,
                                              ALU.mult)
            last.then_inc(sem("h_ready"), 1)
            V.memset(Z[:, :, 0:1], 0.0).then_inc(sem("z_zero"), 1)
            low_half(T_X1, None)

            wait("z_zero", 1)
            for m in range(RW_CHUNKS):
                wait("b2_out", m + 1)
                link(V.tensor_tensor(T[4][:, m % 4, :], Z[:, m, 0:S], Z[:, m, 1:S + 1], ALU.subtract))
                V.scalar_tensor_tensor(SH[:, m, :], T[4][:, m % 4, :], col("mu", m), Z[:, m, 1:S + 1], ALU.mult,
                                       ALU.add).then_inc(sem("sh_ready"), 1)
            wait("f_mm", 1)
            V.tensor_copy(ftok[:, :, :].rearrange("p t g -> p (t g)"), PS[:, 3, 0:16]).then_inc(sem("ftok_ready"), 1)
            used(FIRST["fox_v"] + 3)
            for t in range(NT):
                last = V.tensor_copy(fv[:, t, :], PS[:, t, :])
            last.then_inc(sem("fv_ready"), 1)
            wait("frow_mm", 1)
            wait("fb_landed", 16)
            V.tensor_scalar(fr[:, 0, :], PS[0:FH, 2, 0:S], fbias[:, 0:1], None, ALU.add).then_inc(sem("fr_ready"), 1)
            wait("sh_ready", RW_CHUNKS)
            for c in range(4):
                ins = V.tensor_scalar(T[6][:, c, :], SH[:, 4 + c, :], col("k_k", c), None, ALU.mult)
            link(ins)
            V.tensor_tensor(T[7][:, :, :], T[6][:, :, :], T[6][:, :, :], ALU.mult).then_inc(sem("kksq_ready"), 1)
            wait("f_act", 3)
            link(V.scalar_tensor_tensor(fr[:, 0, :], fr[:, 0, :], 0.0, fr[:, 1, :], ALU.min, ALU.subtract))
            link(V.tensor_tensor_scan(fr[:, 1, :], fr[:, 0, :], fr[:, 0, :], 0.0, ALU.add, ALU.bypass))
            V.tensor_scalar(fr[:, 2, :], fr[:, 1, :], -float(FD) ** 0.5, None, ALU.mult).then_inc(sem("nc8_ready"), 1)
            wait("sigw_ready", 1)
            flat = lambda x: x.rearrange("p c s -> p (c s)")
            link(V.tensor_tensor_scan(flat(T[5][:, :, :]), resets[:, :], flat(T[4][:, :, :]), 0.0, ALU.mult, ALU.add))
            V.tensor_tensor(T[2][:, :, :], T[5][:, :, :], T[4][:, :, :], ALU.subtract).then_inc(sem("lg_ready"), 2)
            wait("kkss_mm", 1)
            V.tensor_scalar(flat(T[7][:, :, :]), PS[:, 4:6, :].rearrange("p b n -> p (b n)"), 1e-24, None,
                            ALU.max).then_inc(sem("ms_ready"), 1)
            wait("gdec_ready", 1)
            V.tensor_copy(GL[:, :, :], T[0][:, :, :].rearrange("p q (c t) -> p q c t", t=CH_T)[:, :, :, CH_T - 1])
            wait("aa_ready", 1)
            for c in range(4):
                ins = V.tensor_scalar(T[5][:, c, :], T[3][:, c, :], 1.0, col("k_a", c), ALU.subtract, ALU.mult)
            link(ins)
            link(V.scalar_tensor_tensor(T[5][:, :, :], T[5][:, :, :], 1.0, SH[:, 4:8, :], ALU.add, ALU.mult))
            wait("sq_ready", 6)
            link(V.reciprocal(T[7][:, :, :], T[7][:, :, :]))
            V.tensor_tensor(T[6][:, :, :], T[6][:, :, :], T[7][:, :, :], ALU.mult).then_inc(sem("nk_ready"), 1)
            wait("nk_ready", 1)
            link(V.tensor_tensor(T[7][:, :, :], SH[:, 0:4, :], T[5][:, :, :], ALU.mult))
            for c in range(4):
                last = V.tensor_scalar(T[7][:, c, :], T[7][:, c, :], col("r_k", c), None, ALU.mult)
            last.then_inc(sem("bonp_ready"), 1)
            link(V.tensor_tensor(T[4][:, :, :], T[6][:, :, :], T[3][:, :, :], ALU.mult))
            chunked = lambda x: x.rearrange("p c (n t) -> p (c n) t", t=CH_T)
            part = lambda x, k: x[:, :, :, k, :].rearrange("p q c t -> p (q c) t")
            V.tensor_tensor(part(BK, 0), chunked(T[4][:, :, :]), chunked(T[1][:, :, :]), ALU.mult)
            V.tensor_tensor(part(BK, 1), chunked(T[5][:, :, :]), chunked(T[1][:, :, :]), ALU.mult)
            V.tensor_tensor(part(CR, 0), chunked(T[6][:, :, :]), chunked(T[2][:, :, :]), ALU.mult)
            V.tensor_tensor(part(CR, 1), chunked(SH[:, 0:4, :]), chunked(T[0][:, :, :]), ALU.mult).then_inc(
                sem("bk_ready"), 1)
            wait("bon_mm", 1)
            V.tensor_tensor(flat(BON[:, :, :]), PS[:, 6:8, :].rearrange("p b n -> p (b n)"), flat(SH[:, 8:12, :]),
                            ALU.mult).then_inc(sem("bon_ready"), 1)

            def f_max(h):
                wait("fs_mm", h + 1)
                wait("fpt_mm", h - 1)
                s0 = 64 + 8 * (h % 2)
                V.tensor_tensor_reduce(out=fp[:, h % 2, 0:P], in0=PS[:, 4 + h % 2, 0:P], in1=mask_f[:, P:S], scale=1.0,
                                       scalar=3.0 * NEG, op0=ALU.add, op1=ALU.max, accum_out=ST[:, s0:s0 + 1])
                link(V.tensor_tensor_reduce(out=fp[:, h % 2, P:384], in0=PS[:, 4 + h % 2, P:384], in1=mask_f[:, :],
                                            scale=1.0, scalar=3.0 * NEG, op0=ALU.add, op1=ALU.max,
                                            accum_out=ST[:, s0 + 1:s0 + 2]))
                V.tensor_scalar(ST[:, s0 + 2:s0 + 4], ST[:, s0:s0 + 2], -float(FD) ** -0.5, None, ALU.mult).then_inc(
                    sem("fmax_ready"), 1)

            def f_norm(h):
                wait("fexp_ready", h + 1)
                s0 = 64 + 8 * (h % 2)
                link(V.reciprocal(ST[:, s0 + 4:s0 + 6], ST[:, s0 + 4:s0 + 6]))
                V.tensor_scalar(fp[:, h % 2, 0:P], fp[:, h % 2, 0:P], ST[:, s0 + 4:s0 + 5], None, ALU.mult)
                V.tensor_scalar(fp[:, h % 2, P:384], fp[:, h % 2, P:384], ST[:, s0 + 5:s0 + 6], None,
                                ALU.mult).then_inc(sem("fnorm_ready"), 1)

            f_max(0)
            for h in range(FH):
                if h + 1 < FH:
                    f_max(h + 1)
                f_norm(h)
            wait("yfh_ready", 1)
            V.tensor_tensor(flat(YFL[:, :, :]), PS[:, 0:2, :].rearrange("p b n -> p (b n)"),
                            flat(plain(YFH[:, :, :])), ALU.subtract).then_inc(sem("yfl_ready"), 1)

            for c in range(NCH):
                for h2 in range(2):
                    wait("sc_mm", 2 * c + h2 + 1)
                    last = V.tensor_tensor(PK[:, c, h2, :, :], PS[:, 2 * c + h2, :].rearrange("p (q n) -> p q n", n=P),
                                           mask_r[:, :].unsqueeze(1).broadcast_to([P, NPAIR, P]), ALU.mult)
            link(last)
            V.memset(part(BK, 0), 0.0)
            V.tensor_copy(part(BK, 1), chunked(SH[:, 8:12, :])).then_inc(sem("vp_ready"), 1)
            wait("uv_mm", 1)

            for half in range(2):
                cs = slice(2 * half, 2 * half + 2)
                A_ = PK[0:64, cs, :, :, 0:64].rearrange("p c a q n -> p (c a q) n")
                X = MINV[:, cs, :, :].rearrange("p c u n -> p (c u) n")
                bc = lambda m: m.unsqueeze(1).broadcast_to([64, 16, 64])
                link(V.scalar_tensor_tensor(inv["P0"][:, :, :], A_, -1.0, bc(blk16[:, :]), ALU.mult, ALU.mult))
                V.scalar_tensor_tensor(inv["NO"][:, :, :], A_, -1.0, inv["P0"][:, :, :], ALU.mult, ALU.subtract)
                V.tensor_tensor(X, inv["P0"][:, :, :], bc(ident[0:64, 0:64]), ALU.add).then_inc(sem("inv_in"), 1)
                wait("inv_in", half + 1)
                for k, (_, _, dst, adds, _) in enumerate(INVERSE):
                    if not adds:
                        continue
                    wait("inv_mm", half * len(INVERSE) + k + 1)
                    b = 2 * (k % 4)
                    V.tensor_tensor(X.rearrange("p u n -> p (u n)"), X.rearrange("p u n -> p (u n)"),
                                    PS[0:64, b:b + 2, :].rearrange("p b n -> p (b n)"), ALU.add).then_inc(
                        sem("inv_added"), 1)
                    wait("inv_added", half * evacuated(len(INVERSE) - 1, True) + evacuated(k, True))

            for c in range(NCH):
                wait("z_mm", c + 1)
                V.tensor_scalar(ZS[:, :], PS[0:64, 0, :], -1.0, None, ALU.mult).then_inc(sem("zs_ready"), 1)
                wait("su_mm", c + 1)
                src = PS[:, 3, :].rearrange("p (q n) -> p q n", n=P)
                if c:
                    link(V.tensor_tensor(S2T[:, :, :], S2[:, :, :], src, ALU.add))
                    src = S2T[:, :, :]
                    wait("y_mm", c + 1)
                for q in range(NPAIR):
                    last = V.scalar_tensor_tensor(S2[:, q, :], src[:, q, :], GL[:, q, c:c + 1], blk_ones[:, :],
                                                  ALU.mult, ALU.mult)
                last.then_inc(sem("s_ready"), 1)
                wait("s_ready", c + 1)

            wait("gn_mm", 1)
            link(V.scalar_tensor_tensor(flat(YC[:, :, :]), PS[:, 4:6, :].rearrange("p b n -> p (b n)"), -1.0 / RN,
                                        flat(YT[:, :, :]), ALU.mult, ALU.add))
            V.tensor_tensor(T[0][:, :, :], YC[:, :, :], YC[:, :, :], ALU.mult).then_inc(sem("ysq_ready"), 1)
            wait("gn_mm", 2)
            mean_eps(flat(T[2][:, :, :]), PS[:, 6:8, :].rearrange("p b n -> p (b n)"), 1.0 / RN, GN_EPS)
            wait("sq_ready", 7)
            link(V.reciprocal(T[2][:, :, :], T[2][:, :, :]))
            link(V.tensor_tensor(YC[:, :, :], YC[:, :, :], T[2][:, :, :], ALU.mult))
            for c in range(4):
                ins = V.tensor_scalar(YC[:, c, :], YC[:, c, :], col("ln_g", c), col("ln_b", c), ALU.mult, ALU.add)
            link(ins)
            link(V.tensor_tensor(YC[:, :, :], YC[:, :, :], BON[:, :, :], ALU.add))
            V.tensor_tensor(YC[:, :, :], YC[:, :, :], GG[:, :, :], ALU.mult).then_inc(sem("yr_ready"), 1)
            wait("yrh_ready", 1)
            V.tensor_tensor(YRL[:, :, :], YC[:, :, :], plain(YRH[:, :, :]), ALU.subtract).then_inc(sem("yrl_ready"), 1)

            for g in range(2):
                used(FIRST["p_fox"] + 2 * g + 1)
                k = slice(g * 512, (g + 1) * 512)
                for t in range(NT):
                    last = V.tensor_tensor(XS[:, t, k], PS[:, 2 * g + t, :], SG[:, t, k], ALU.mult)
                last.then_inc(sem("pf_out"), 1)
            wait("pf_out", 2)
            for g in range(2):
                wait("xs_ready", 8 + g)
                used(FIRST["p_rwkv"] + 2 * g + 1)
                k = slice(g * 512, (g + 1) * 512)
                for t in range(NT):
                    ins = V.tensor_tensor(flat(T[3][:, 2 * t:2 * t + 2, :]), PS[:, 2 * g + t, :],
                                          SG[:, t, D + g * 512:D + (g + 1) * 512], ALU.mult)
                link(ins)
                for t in range(NT):
                    last = V.tensor_tensor(XS[:, t, k], XS[:, t, k], flat(T[3][:, 2 * t:2 * t + 2, :]), ALU.add)
                last.then_inc(sem("xs_ready"), 1)
            low_half(T_MERGED, None)
            add_to_h(FIRST["w_o"], 4, DN_ALPHA).then_inc(sem("h_ready"), 1)

            def layer_norm(k, gain, shift, landed, root_val, ready):
                for t in range(NT):
                    wait("sum_ready", 2 * k + t + 1)
                    m = ST[:, 80 + 2 * k + t:81 + 2 * k + t]
                    link(V.tensor_scalar(m, m, 1.0 / D, None, ALU.mult))
                    V.tensor_scalar(H[:, t, :], H[:, t, :], m, None, ALU.subtract).then_inc(sem("xc_ready"), 1)
                wait("var_ready", 2 * k + 2)
                r = ST[:, 96 + 2 * k:98 + 2 * k]
                mean_eps(r, ST[:, 88 + 2 * k:90 + 2 * k], 1.0 / D, LN_EPS)
                wait("sq_ready", root_val)
                link(V.reciprocal(r, r))
                wait(landed, 32)
                for t in range(NT):
                    link(V.scalar_tensor_tensor(H[:, t, :], H[:, t, :], r[:, t:t + 1], gain[:, :], ALU.mult, ALU.mult))
                    ins = V.tensor_tensor(H[:, t, :], H[:, t, :], shift[:, :], ALU.add)
                    if ready == "y_ready" or t == NT - 1:
                        ins.then_inc(sem(ready), 1)

            layer_norm(0, LG1, LB1, "ln1_landed", 8, "h_ready")
            low_half(T_X2, None)

            for m in range(LISTS):
                wait("qh_ready", m + 1)
                V.tensor_tensor(QL[:, m, :], PS[:, 4 + m % 4, 0:S], plain(QH[:, m, :]), ALU.subtract).then_inc(
                    sem("ql_ready"), 1)

            wait("u_bank_free", NT)
            for t in range(NT):
                def best(values, top, index, lists, n):
                    for r in range(2):
                        for l in range(lists):
                            ins = V.max(top(l)[:, 8 * r:8 * r + 8], values(l))
                        link(ins)
                        for l in range(lists):
                            ins = V.max_index(index(l)[:, 8 * r:8 * r + 8], top(l)[:, 8 * r:8 * r + 8], values(l))
                        link(ins)
                        if r == 0:
                            for l in range(lists):
                                ins = V.match_replace(values(l), top(l)[:, 0:8], values(l), -3.0e38)
                            link(ins)

                best(lambda l: SC[:, t, l, :], lambda l: tv[:, l, :], lambda l: ti[:, l, :], LISTS, NK)
                V.tensor_copy(tif[:, :, :], ti[:, :, :])
                pair = tv[:, :, :].rearrange("p (h two) k -> p h two k", two=2)
                shape = [P, PH, TOPK, TOPK]
                link(V.tensor_tensor(cand[:, :, :, :], pair[:, :, 0, :].unsqueeze(3).broadcast_to(shape),
                                     pair[:, :, 1, :].unsqueeze(2).broadcast_to(shape), ALU.add))
                best(lambda l: cand[:, l, :, :].rearrange("p a b -> p (a b)"), lambda l: bv[:, t, l, :],
                     lambda l: bp[:, l, :], PH, TOPK * TOPK)
                V.tensor_scalar(bai[:, :, :], bp[:, :, :], 4, None, ALU.logical_shift_right)
                link(V.tensor_scalar(bbi[:, :, :], bp[:, :, :], TOPK - 1, None, ALU.bitwise_and))
                V.tensor_copy(baf[:, :, :], bai[:, :, :])
                link(V.tensor_copy(bbf[:, :, :], bbi[:, :, :]))
                keys = tif[:, :, :].rearrange("p (h two) k -> p h two k", two=2)
                for which, place in ((0, baf), (1, bbf)):
                    flat3 = tmp1[:, :, :, :].rearrange("p h k a -> p (h k) a")
                    link(V.tensor_tensor(flat3, iota_f[:, 0:TOPK].unsqueeze(1).broadcast_to([P, P, TOPK]),
                                         place[:, :, :].rearrange("p h k -> p (h k)").unsqueeze(2).broadcast_to(
                                             [P, P, TOPK]), ALU.is_equal))
                    link(V.tensor_tensor(tmp1[:, :, :, :], tmp1[:, :, :, :],
                                         keys[:, :, which, :].unsqueeze(2).broadcast_to(shape), ALU.mult))
                    link(V.tensor_reduce(ijg[:, t, which, :], flat3, AX_X, ALU.add))
                last = V.tensor_tensor(be[:, t], bv[:, t], bv[:, t, :, 0:1].broadcast_to([P, PH, TOPK]), ALU.subtract)
            last.then_inc(sem("bv_ready"), 1)
            wait("bexp_ready", 1)
            both = be[:, :, :, :].rearrange("p t h k -> p (t h) k")
            link(V.tensor_reduce(ST[:, 112:128], both, AX_X, ALU.add))
            link(V.reciprocal(ST[:, 112:128], ST[:, 112:128]))
            for t in range(NT):
                last = V.tensor_tensor(ijg[:, t, 2, :].rearrange("p (h k) -> p h k", h=PH), be[:, t],
                                       ST[:, 112 + 8 * t:120 + 8 * t].unsqueeze(2).broadcast_to([P, PH, TOPK]),
                                       ALU.mult)
            last.then_inc(sem("ijg_ready"), 1)

            wait("ijgT_ready", 1)

            def at_token(x, t):
                return x[:, t:t + 1] if isinstance(t, int) else x[:, bass.ds(t, 1)]

            def one_hot_rows(q, g, first):
                if not first:
                    dve.wait_ge(sem("x_tr"), q - 1)
                for a in range(4):
                    last = V.tensor_scalar(A4[:, g, a, :], iota_b[:, :], at_token(IT, 4 * q + a), None, ALU.is_equal)
                last.then_inc(sem("a4_ready"), 1)

            def pick(q, g):
                dve.wait_ge(sem("r_mm"), q + 1)
                for a in range(4):
                    last = V.scalar_tensor_tensor(hjunk[:, 4 * g + a, :], iota_f[:, :], at_token(JT, 4 * q + a),
                                                  PS[:, 6 + g, a * P:(a + 1) * P], ALU.is_equal, ALU.mult,
                                                  accum_out=at_token(HT, 4 * q + a))
                last.then_inc(sem("hx_done"), 1)

            used(FIRST["v_table"] - 1)
            one_hot_rows(0, 0, True)
            one_hot_rows(1, 1, True)
            with dve.Fori(0, S // 8 - 1) as i:
                for g in range(2):
                    one_hot_rows(2 * i + (g + 2), g, False)
                    pick(2 * i + g, g)
            for g in range(2):
                pick(S // 4 - 2 + g, g)
            wait("gelu_ready", 1)
            link(V.tensor_tensor(HT[:, :], HT[:, :], GT[:, :], ALU.mult))

            def coefficient_rows(q, g, first):
                if not first:
                    dve.wait_ge(sem("c_mm"), q - 1)
                for a in range(4):
                    t = 4 * q + a
                    V.tensor_scalar(A4F[:, g, a, :], iota_f[:, :], at_token(IT, t), None, ALU.is_equal)
                    last = V.tensor_scalar(B4F[:, g, a, :], iota_f[:, :], at_token(JT, t), at_token(HT, t),
                                           ALU.is_equal, ALU.mult)
                last.then_inc(sem("b4_ready"), 1)

            for g in range(2):
                coefficient_rows(g, g, True)
            with dve.Fori(1, S // 8) as i:
                for g in range(2):
                    coefficient_rows(2 * i + g, g, False)

            def c_low(j, c):
                dve.wait_ge(sem("ch_ready"), j + 1)
                hs = HS[:, j, :] if isinstance(j, int) else HS[:, bass.ds(j, 1), :].rearrange("p a s -> p (a s)")
                V.tensor_tensor(CL[:, c, :], hs, plain(CH[:, c, :]), ALU.subtract).then_inc(sem("cl_ready"), 1)

            with dve.Fori(0, NK // 4) as i:
                for c in range(4):
                    c_low(4 * i + c, c)
            used(N_ITEMS - 1)
            for t in range(NT):
                last = V.scalar_tensor_tensor(H[:, t, :], H[:, t, :], DN_ALPHA,
                                              PS[:, 2 * t:2 * t + 2, :].rearrange("p b n -> p (b n)"), ALU.mult, ALU.add)
            last.then_inc(sem("h_ready"), 1)
            layer_norm(1, LG2, LB2, "ln2_landed", 9, "y_ready")


def kernel(**inputs):
    import numpy as np
    import concourse.bacc as bacc
    from concourse.bass_utils import run_bass_kernel_spmd

    a = {k: np.asarray(v) for k, v in inputs.items()}

    def form_a(w):
        k, n = w.shape
        return w.reshape(k // 256, 2, P, n // 512, 512).transpose(3, 0, 2, 1, 4).reshape(-1, P, D)

    def form_b(w):
        return w.reshape(KC, P, -1, P).transpose(2, 1, 0, 3).reshape(-1, P, D)

    w1 = a["mlstm_w_in"][0]
    w2 = a["w_in_2"][0]
    fox = 3 * FH * FD + FH
    rw = fox + RW_CHUNKS * P
    parts = {
        "qk": form_b(w1[:, :1024]),
        "v": form_a(w1[:, 1024:2048]),
        "o": form_a(w1[:, 2048:3072]),
        "mix_out": form_a(a["mlstm_w_out"][0]),
        "w1": form_b(a["mlp_w1"][0]),
        "w2": form_a(a["mlp_w2"][0]),
        "ple_gate": form_a(a["ple_gate_w"][0]),
        "ple": form_a(a["ple_w"][0]),
        "rwkv": form_b(w2[:, fox:rw]),
        "fox_qk": form_b(w2[:, :1024]),
        "fox_v": form_a(w2[:, 1024:1536]),
        "gates": form_a(w2[:, rw:]),
        "p_fox": form_a(a["p_fox_2"][0]),
        "p_rwkv": form_a(a["p_rwkv_2"][0]),
        "w_o": form_a(a["w_o_2"][0]),
        "peer_q": form_b(a["peer_w_q_2"][0]),
        "keys": a["peer_sub_keys_2"][0].reshape(2, PH, NK, P).transpose(0, 3, 1, 2).reshape(2, P, D),
        "u": a["peer_u_2"][0].reshape(NK, NK, KC, P).transpose(1, 3, 2, 0).reshape(NK, P, D),
        "v_table": a["peer_v_2"][0].reshape(NK, NK, D).transpose(1, 0, 2),
    }
    for name, n in COUNTS:
        assert parts[name].shape == (n, P, D), name
    vectors = [a["norm_mix"], a["norm_mlp"], a["norm_ple"], a["mlstm_head_norm"], a["rwkv_mu_2"], a["rwkv_w0_2"],
               a["rwkv_a0_2"], a["rwkv_k_k_2"], a["rwkv_k_a_2"], a["rwkv_r_k_2"], a["rwkv_ln_g_2"], a["rwkv_ln_b_2"]]
    columns = lambda w: w.reshape(KC, P, -1).transpose(1, 0, 2)
    arrays = {
        "weights": np.concatenate([parts[name] for name, _ in COUNTS]),
        "x": a["x"][0],
        "p": a["p"][0, 0],
        "vectors": np.concatenate([v[0].reshape(-1, P).T for v in vectors], axis=1),
        "rows": np.stack([a["norm_final"], a["ple_gate_b"][0], a["ln1_g_2"][0], a["ln1_b_2"][0], a["ln2_g_2"][0],
                          a["ln2_b_2"][0]]),
        "gate_weights": np.concatenate([columns(w1[:, 3072:]), columns(w2[:, 1536:fox])], axis=2),
        "low_rank": np.stack([np.concatenate([a["rwkv_w2_2"][0], a["rwkv_a2_2"][0]]), a["rwkv_g2_2"][0]], axis=1),
        "gate_bias": a["mlstm_b_gates"][0].T,
        "fox_bias": a["fox_f_bias_2"][0].reshape(FH, 1),
    }
    arrays = {k: np.ascontiguousarray(v) for k, v in arrays.items()}
    nc = bacc.Bacc("TRN2", target_bir_lowering=False, num_devices=1)
    args = [nc.dram_tensor(k, v.shape, mybir.dt.from_np(v.dtype), kind="ExternalInput").ap() for k, v in arrays.items()]
    out = nc.dram_tensor("y", (S, D), F32, kind="ExternalOutput").ap()
    bass_blocks(nc, *args, out)
    r = run_bass_kernel_spmd(nc, [arrays], core_ids=[0])
    return r.results[0]["y"].reshape(1, S, D)
```

```python
from contextlib import ExitStack

import concourse.bass as bass
from concourse import mybir

ALU = mybir.AluOpType
ACT = mybir.ActivationFunctionType
F32 = mybir.dt.float32
F32R = mybir.dt.float32r
BF16 = mybir.dt.bfloat16
U32 = mybir.dt.uint32
AX_X = mybir.AxisListType.X

P = 128
S = 256
NT = S // P
D = 1024
KC = D // P
EPS = 1e-6
LN_EPS = 1e-5
GN_EPS = 64e-5
DN_ALPHA = 2.0 ** 0.25

MH, MDK, MDV = 4, 128, 256
FH, FD = 8, 64
RH, RN = 8, 64
CH_T = 64
NCH = S // CH_T
NPAIR = RH // 2
RW_CHUNKS = (3 * RH * RN + 64 + 64 + 128) // P
DECAY = 0.6065306597126334
NEG = -1.0e30
BLK = 16
PH, NK, TOPK = 8, 128, 16
LISTS = 2 * PH

COUNTS = [
    ("qk", 8), ("v", 8), ("o", 8), ("mix_out", 8), ("w1", 32), ("w2", 32), ("ple_gate", 8), ("ple", 2),
    ("rwkv", RW_CHUNKS), ("fox_qk", 8), ("fox_v", 4), ("gates", 16), ("p_fox", 4), ("p_rwkv", 4), ("w_o", 8),
    ("peer_q", 16), ("keys", 2), ("u", NK), ("v_table", NK),
]
FIRST = {}
_at = 0
for _name, _n in COUNTS:
    FIRST[_name] = _at
    _at += _n
N_ITEMS = _at
RING = 4

VEC = {}
_at = 0
for _name, _n in [("norm_mix", 8), ("norm_mlp", 8), ("norm_ple", 8), ("head_norm", 8), ("mu", RW_CHUNKS), ("w0", 4),
                  ("a0", 4), ("k_k", 4), ("k_a", 4), ("r_k", 4), ("ln_g", 4), ("ln_b", 4)]:
    VEC[_name] = _at
    _at += _n
N_VEC = _at
ROWS = ["norm_final", "ple_gate_b", "ln1_g", "ln1_b", "ln2_g", "ln2_b"]

T_MIX, T_HEADS, T_MLP, T_PLE, T_X1, T_MERGED, T_X2 = range(7)

INVERSE = [
    ("P0", "I", "T0", False, -1),
    ("T0", "P0", "P1", False, 0), ("P0", "T0", "T1", False, 0),
    ("T1", "X", "X", True, 2), ("T1", "P1", "P0", False, 2),
    ("P1", "T1", "T0", False, 2), ("T0", "X", "X", True, 5),
    ("P0", "T0", "T1", False, 5), ("T1", "X", "X", True, 7),
    ("X", "I", "T0", False, 8),
    ("T0", "NO", "P0", False, 9), ("NO", "T0", "P1", False, 9),
    ("P0", "P1", "T1", False, 11), ("T1", "X", "X", True, 12),
    ("P1", "X", "X", True, 13),
]


def evacuated(upto, adds):
    return sum(r[3] == adds for r in INVERSE[:upto + 1])


def bass_blocks(nc, weights, x_in, p_in, vec_in, rows_in, gate_w_in, lora_in, mb_in, fb_in, out):
    with ExitStack() as ctx:
        base = 16512
        slab = ctx.enter_context(nc.sbuf_tensor("slab", [P, 53208], F32))

        def at(name, shape, dt, offset):
            return nc.alloc_sbuf_tensor_at(name, shape, dt, offset=base + offset)

        H = at("H", [P, NT, D], F32, 0)
        XH = at("XH", [P, KC, S], F32R, 8192)
        XL = at("XL", [P, KC, S], F32R, 16384)
        RAW = at("RAW", [P, RING, D], F32, 24576)
        WH = at("WH", [P, RING, D], F32R, 40960)
        WL = at("WL", [P, RING, D], F32R, 57344)
        C0 = 73728
        iota_f = at("iota_f", [P, P], F32, C0)
        ST = at("ST", [P, P], F32, C0 + 512)
        ident = at("ident", [P, P], F32, C0 + 1024)
        vec = at("vec", [P, N_VEC], F32, C0 + 1536)
        ones_row = at("ones_row", [1, P], F32, C0 + 1856)
        IT = at("IT", [P, S], F32, C0 + 4160)
        JT = at("JT", [P, S], F32, C0 + 5184)
        GT = at("GT", [P, S], F32, C0 + 6208)
        fbias = at("fbias", [FH, 1], F32, C0 + 7232)
        mbias = at("mbias", [MH, 4], F32, C0 + 7264)
        eps_c = at("eps_c", [P, 4], F32, C0 + 7296)
        A0 = 81664
        M0 = A0 + 114688
        mask_m = at("mask_m", [P, 2, 2, S], F32, M0)
        fpt = at("fpt", [P, 2, 384], F32, M0)
        mask_f = at("mask_f", [P, S], F32, M0 + 4096)
        mask_r = at("mask_r", [P, P], F32, M0 + 5120)
        blk_ones = at("blk_ones", [P, P], F32, M0 + 5632)
        blk16 = at("blk16", [P, 64], F32, M0 + 6144)
        resets = at("resets", [P, D], BF16, M0 + 6400)
        sel4 = at("sel4", [MH, MH, P], F32, M0 + 8448)
        sel8 = at("sel8", [FH, FH, P], F32, M0 + 10496)
        XS = at("XS", [P, NT, D], F32, A0)
        qkT = at("qkT", [P, 2 * MH, S], F32, A0 + 8192)
        v1 = at("v1", [P, NT, MH, MDV + 1], F32, A0 + 16384)
        og = at("og", [P, NT, D], F32, A0 + 24640)
        hacc = at("hacc", [P, NT, D], F32, A0 + 32832)
        WE = at("WE", [P, 2, 2, S], F32, A0 + 41024)
        SM = at("SM", [P, 2, 2, S], F32, A0 + 45120)
        GR = at("GR", [MH, 4, S], F32, A0 + 49216)
        GA = at("GA", [MH, 8, S], F32, A0 + 53312)
        AT = at("AT", [P, 8, MH], F32, A0 + 61504)
        gtok = at("gtok", [P, NT, 16], F32, A0 + 61632)
        GWH = at("GWH", [P, KC, 24], F32R, A0 + 62208)
        GWL = at("GWL", [P, KC, 24], F32R, A0 + 62976)
        gw = at("gw", [P, KC, 24], F32, A0 + 63744)
        ZH = at("ZH", [P, 32, S], F32R, A0 + 8192)
        ZL = at("ZL", [P, 32, S], F32R, A0 + 40960)
        RT = at("RT", [P, 4, S], F32, A0 + 73728)
        ZF = at("ZF", [P, 4, S], F32, A0 + 77824)
        P2 = at("P2", [P, NT, S], F32, A0 + 81920)
        PTH = at("PTH", [P, 2, S], F32R, A0 + 83968)
        PTL = at("PTL", [P, 2, S], F32R, A0 + 86016)
        SGP = at("SGP", [P, NT, D], F32, A0 + 88064)
        brow = at("brow", [1, D], F32, A0 + 96256)
        nfin = at("nfin", [P, D], F32, A0 + 100352)
        FWH = at("FWH", [P, KC, 8], F32R, A0 + 104448)
        FWL = at("FWL", [P, KC, 8], F32R, A0 + 104704)
        SG = at("SG", [P, NT, 2 * D], F32, A0 + 8192)
        YFH = at("YFH", [P, 4, S], F32R, A0 + 24576)
        YFL = at("YFL", [P, 4, S], F32R, A0 + 28672)
        YRH = at("YRH", [P, 4, S], F32R, A0 + 32768)
        YRL = at("YRL", [P, 4, S], F32R, A0 + 36864)
        fqk = at("fqk", [P, 8, S], F32, A0)
        fv = at("fv", [P, NT, 512], F32, A0 + 32768)
        fp = at("fp", [P, 2, 384], F32, A0 + 36864)
        fr = at("fr", [FH, 3, S], F32, C0 + 4160)
        ftok = at("ftok", [P, NT, 8], F32, A0 + 40960)
        lora = at("lora", [P, 2, 512], F32, A0 + 24576)
        BK = at("BK", [P, NPAIR, NCH, 2, CH_T], F32, A0 + 40960)
        CR = at("CR", [P, NPAIR, NCH, 2, CH_T], F32, A0 + 49152)
        PK = at("PK", [P, NCH, 2, NPAIR, P], F32, A0 + 57344)
        BKT = at("BKT", [P, NCH, NPAIR, P], F32, A0 + 73728)
        UV = at("UV", [P, NCH, NPAIR, P], F32, A0 + 81920)
        SH = at("SH", [P, RW_CHUNKS, S], F32, A0 + 90112)
        Z = at("Z", [P, RW_CHUNKS, S + 1], F32, A0 + 57344)
        T = [at(f"T{k}", [P, 4, S], F32, A0 + 57344 + 4096 * k) for k in range(8)]
        GG = at("GG", [P, 4, S], F32, A0 + 104448)
        BON = at("BON", [P, 4, S], F32, A0 + 108544)
        GL = at("GL", [P, NPAIR, NCH], F32, C0 + 7328)
        LT = at("LT", [P, 2, S], F32, A0 + 112640)
        MINV = at("MINV", [P, NCH, NPAIR, P], F32, A0)
        INV_AT = [{"T0": 8192, "P0": 12288, "P1": 16384, "T1": 20480, "NO": A0 + 32768},
                  {"T0": A0 + 90112, "P0": A0 + 94208, "P1": A0 + 98304, "T1": A0 + 40960, "NO": A0 + 36864}]
        inv = [{k: at(f"inv_{k}_{half}", [P, 8, P], F32, v) for k, v in INV_AT[half].items()} for half in range(2)]
        for half in range(2):
            inv[half]["X"] = MINV[:, 2 * half:2 * half + 2, :, :].rearrange("p c q n -> p (c q) n")
        FY = at("FY", [P, NT, D], F32, 8192)
        ZS = at("ZS", [P, NPAIR, RN], F32, A0 + 45056)
        S2 = at("S2", [P, NPAIR, P], F32, A0 + 47104)
        YT = at("YT", [P, 4, S], F32, A0 + 90112)
        YC = at("YC", [P, 4, S], F32, A0 + 94208)
        S2T = at("S2T", [P, NPAIR, P], F32, A0 + 102400)
        LG1 = at("LG1", [P, D], F32, A0 + 24576)
        LB1 = at("LB1", [P, D], F32, A0 + 28672)
        HS = at("HS", [P, NK, S], F32, A0)
        R0 = A0 + 65536
        QH = at("QH", [P, LISTS, S], F32R, R0)
        QL = at("QL", [P, LISTS, S], F32R, R0 + 16384)
        SC = at("SC", [P, NT, LISTS, NK], F32, R0 + 32768)
        cand = at("cand", [P, PH, TOPK, TOPK], F32, R0 + 49152)
        tmp1 = at("tmp1", [P, PH, TOPK, TOPK], F32, R0 + 57344)
        tv = at("tv", [P, LISTS, TOPK], F32, R0)
        ti = at("ti", [P, LISTS, TOPK], U32, R0 + 1024)
        tif = at("tif", [P, LISTS, TOPK], F32, R0 + 2048)
        bv = at("bv", [P, NT, PH, TOPK], F32, R0 + 9216)
        be = at("be", [P, NT, PH, TOPK], F32, R0 + 10240)
        bp = at("bp", [P, PH, TOPK], U32, R0 + 3584)
        bai = at("bai", [P, PH, TOPK], U32, R0 + 4096)
        bbi = at("bbi", [P, PH, TOPK], U32, R0 + 4608)
        baf = at("baf", [P, PH, TOPK], F32, R0 + 5120)
        bbf = at("bbf", [P, PH, TOPK], F32, R0 + 5632)
        ijg = at("ijg", [P, NT, 3, P], F32, R0 + 6144)
        hot_i = at("hot_i", [P, 2, 2, P], F32, C0 + 1024)
        hot_j = at("hot_j", [P, 2, 2, NK // 2], F32, C0 + 3072)
        CH = at("CH", [P, RING, S], F32R, 8192)
        CL = at("CL", [P, RING, S], F32R, 12288)
        LG2 = at("LG2", [P, D], F32, 16384)
        LB2 = at("LB2", [P, D], F32, 20480)

        PS = ctx.enter_context(nc.psum_tensor("PS", [P, 8, 512], F32))

        sems = {}

        def sem(name):
            if name not in sems:
                sems[name] = ctx.enter_context(nc.semaphore(name))
            return sems[name]

        w_landed = [sem(f"w_landed{i}") for i in range(RING)]
        w_hi, w_lo, w_used = sem("w_hi"), sem("w_lo"), sem("w_used")

        def col(name, c):
            k = VEC[name] + c
            return vec[:, k:k + 1]

        def plain(ap):
            return ap.bitcast(F32)

        ALL = {}

        def after(name, n=1):
            ALL[name] = ALL.get(name, 0) + n
            return ALL[name]

        block = ctx.enter_context(nc.Block())

        @block.sync
        def _(sp):
            sp.dma_start(H[:, :, :], x_in.rearrange("(t p) d -> p t d", p=P)).then_inc(sem("x_landed"), 16)
            for n in range(RING):
                sp.dma_start(RAW[:, n, :], weights[n]).then_inc(w_landed[n], 16)
            full = (N_ITEMS // RING) * RING
            with sp.Fori(1, N_ITEMS // RING) as i:
                for slot in range(RING):
                    n = i * RING
                    sp.wait_ge(w_lo, n + (slot + 1 - RING))
                    sp.dma_start(RAW[:, slot, :], weights[bass.ds(n + slot, 1)].rearrange("a p d -> p (a d)")).then_inc(w_landed[slot], 16)
            for n in range(full, N_ITEMS):
                sp.wait_ge(w_lo, n + 1 - RING)
                sp.dma_start(RAW[:, n % RING, :], weights[n]).then_inc(w_landed[n % RING], 16)
            for t in range(NT):
                sp.wait_ge(sem("y_ready"), t + 1)
                sp.dma_start(out[t * P:(t + 1) * P, :], H[:, t, :]).then_inc(sem("y_stored"), 16)
            sp.wait_ge(sem("y_stored"), 16 * NT)

        @block.gpsimd
        def _(pool):
            made = sem("pool_made")
            count = [0]

            def link(ins):
                count[0] += 1
                ins.then_inc(made, 1)
                pool.wait_ge(made, count[0])

            def keep(view, pattern, base, cm, op, fill=0.0):
                link(nc.gpsimd.affine_select(out=view, in_=view, compare_op=op, fill=fill, base=base,
                                             pattern=pattern, channel_multiplier=cm))

            link(nc.gpsimd.memset(ident[:, :], 1.0))
            keep(ident[:, :], [[-1, P]], 0, 1, ALU.is_equal)
            nc.gpsimd.memset(ones_row[:, :], 1.0).then_inc(sem("ident_ready"), 1)
            link(nc.gpsimd.memset(sel4[:, :, :], 1.0))
            keep(sel4[:, :, :], [[-1, MH], [0, P]], 0, 1, ALU.is_equal)
            link(nc.gpsimd.memset(sel8[:, :, :], 1.0))
            keep(sel8[:, :, :], [[-1, FH], [0, P]], 0, 1, ALU.is_equal)
            link(nc.gpsimd.memset(mask_m[:, :, :, :], 1.0))
            for sb in range(NT):
                keep(mask_m[:, 0, sb, :], [[1, S]], -sb * P, -1, ALU.is_ge)
                keep(mask_m[:, 1, sb, :], [[-1, S]], sb * P, 1, ALU.is_ge)
            link(nc.gpsimd.memset(mask_f[:, :], 0.0))
            keep(mask_f[:, :], [[-1, S]], P, 1, ALU.is_ge, NEG)
            link(nc.gpsimd.memset(mask_r[:, :], 1.0))
            for half in range(2):
                v = mask_r[64 * half:64 * half + 64, :]
                keep(v[:, 0:64], [[1, 64]], -1, -1, ALU.is_ge)
                keep(v[:, 64:128], [[1, 64]], 0, -1, ALU.is_ge)
            link(nc.gpsimd.memset(blk_ones[:, :], 0.0))
            link(nc.gpsimd.memset(blk_ones[0:64, 0:64], 1.0))
            link(nc.gpsimd.memset(blk_ones[64:128, 64:128], 1.0))
            link(nc.gpsimd.memset(blk16[:, :], 1.0))
            for half in range(2):
                v = blk16[64 * half:64 * half + 64, :]
                keep(v, [[-BLK, 64 // BLK], [0, BLK]], 0, 1, ALU.is_ge)
                keep(v, [[BLK, 64 // BLK], [0, BLK]], BLK - 1, -1, ALU.is_ge)
            link(nc.gpsimd.memset(resets[:, :], 1.0))
            link(nc.gpsimd.memset(resets[:, :].rearrange("p (c t) -> p c t", t=CH_T)[:, :, 0:1], 0.0))
            link(nc.gpsimd.iota(iota_f[:, :], [[1, P]], base=0, channel_multiplier=0,
                                allow_small_or_imprecise_dtypes=True))
            link(nc.gpsimd.memset(eps_c[:, 1:2], GN_EPS))
            nc.gpsimd.memset(eps_c[:, 0:1], 1.0).then_inc(sem("consts_ready"), 1)

            def split_low(n, slot):
                pool.wait_ge(w_hi, n + 1)
                nc.gpsimd.tensor_tensor(WL[:, slot, :], RAW[:, slot, :], plain(WH[:, slot, :]),
                                        ALU.subtract).then_inc(w_lo, 1)

            full = (N_ITEMS // RING) * RING
            with pool.Fori(0, N_ITEMS // RING) as i:
                for slot in range(RING):
                    split_low(i * RING + slot, slot)
            for n in range(full, N_ITEMS):
                split_low(n, n % RING)

        @block.scalar
        def _(act):
            A = nc.scalar.activation
            feed_at = [0]

            def split_high(n, slot, used=None):
                act.wait_ge(w_landed[slot], landed_value(n))
                if used is not None:
                    act.wait_ge(w_used, used)
                nc.scalar.copy(WH[:, slot, :], RAW[:, slot, :]).then_inc(w_hi, 1)

            def landed_value(n):
                return 16 * (n // RING + 1)

            def feed(last):
                while feed_at[0] <= min(last + RING - 1, N_ITEMS - 1):
                    n = feed_at[0]
                    split_high(n, n % RING, n + 1 - RING if n >= RING else None)
                    feed_at[0] += 1

            def used(n):
                feed(n)
                act.wait_ge(w_used, n + 1)

            act.dma_start(vec[:, :], vec_in).then_inc(sem("vec_landed"), 16)
            act.dma_start(gw[:, :, :], gate_w_in).then_inc(sem("gw_landed"), 16)
            act.dma_start(mbias[:, :], mb_in).then_inc(sem("mb_landed"), 16)
            act.dma_start(fbias[:, :], fb_in).then_inc(sem("fb_landed"), 16)
            act.dma_start(P2[:, :, :], p_in.rearrange("(t p) d -> p t d", p=P)).then_inc(sem("p_landed"), 16)
            act.dma_start(brow[:, :], rows_in[1:2, :]).then_inc(sem("brow_landed"), 16)
            act.dma_start(nfin[:, :], rows_in[0:1, :].broadcast_to([P, D])).then_inc(sem("nfin_landed"), 16)

            def root(r, src, dst, msem):
                act.wait_ge(sem("ms_ready"), msem)
                A(dst, src, ACT.Sqrt).then_inc(sem("sq_ready"), 1)

            def sumsq(r, h_sem, h_val):
                act.wait_ge(sem(h_sem), h_val)
                for t in range(NT):
                    A(XS[:, t, :], H[:, t, :], ACT.Square, accum_out=ST[:, 2 * r + t:2 * r + t + 1]).then_inc(
                        sem("ss_ready"), 1)

            def evac_high(r, gain):
                for c in range(KC):
                    act.wait_ge(sem("tr_ready"), 4 * r + c // 2 + 1)
                    src = PS[:, 4 + c // 2, (c % 2) * S:(c % 2 + 1) * S]
                    A(XH[:, c, :], src, ACT.Copy, scale=col(gain, c) if gain else 1.0).then_inc(sem("xh_ready"), 1)

            feed(0)
            act.wait_ge(sem("gw_landed"), 16)
            nc.scalar.copy(GWH[:, :, :], gw[:, :, :])
            nc.scalar.copy(FWH[:, :, :], gw[:, :, 16:24]).then_inc(sem("gwh_ready"), 1)

            sumsq(0, "x_landed", 16)
            root(0, ST[:, 16:18], ST[:, 16:18], 1)
            act.wait_ge(sem("vec_landed"), 16)
            evac_high(T_MIX, "norm_mix")

            f2 = GR[:, :, :].rearrange("h (d k) s -> h d k s", k=2)[:, :, 1, :]
            act.wait_ge(sem("gr_ready"), 1)
            A(GA[:, 2:4, :], f2, ACT.Abs).then_inc(sem("g_act"), 1)
            act.wait_ge(sem("g_act"), 1)
            A(GA[:, 2:4, :], GA[:, 2:4, :], ACT.Exp, scale=-1.0).then_inc(sem("g_act"), 1)
            act.wait_ge(sem("g_act"), 2)
            act.wait_ge(sem("consts_ready"), 1)
            A(GA[:, 2:4, :], GA[:, 2:4, :], ACT.Ln, bias=eps_c[0:MH, 0:1]).then_inc(sem("g_act"), 1)
            act.wait_ge(sem("m_ready"), 1)
            A(GA[:, 0:2, :], GA[:, 0:2, :], ACT.Exp, scale=-1.0).then_inc(sem("emt_ready"), 1)

            for g in range(2):
                used(FIRST["o"] + 4 * g + 3)
                for t in range(NT):
                    last = A(og[:, t, g * 512:(g + 1) * 512], PS[:, 2 * (g % 2) + t, :], ACT.Sigmoid)
                last.then_inc(sem("o_out"), 1)

            for e in range(2 * MH):
                act.wait_ge(sem("w_ready"), e + 1)
                A(WE[:, e % 2], WE[:, e % 2], ACT.Exp, scale=-1.0).then_inc(sem("e_ready"), 1)
            act.wait_ge(sem("fin_done"), 2 * MH)
            for t in range(NT):
                for h in range(MH):
                    last = A(XS[:, t, h * MDV:(h + 1) * MDV], hacc[:, t, h * MDV:(h + 1) * MDV], ACT.Square,
                             accum_out=ST[:, 24 + 4 * t + h:25 + 4 * t + h])
            last.then_inc(sem("hss_ready"), 1)
            root(0, ST[:, 32:40], ST[:, 32:40], 2)
            evac_high(T_HEADS, "head_norm")

            feed(FIRST["mix_out"] + 7)
            sumsq(1, "h_ready", 1)
            root(1, ST[:, 18:20], ST[:, 18:20], 3)
            evac_high(T_MLP, "norm_mlp")

            def z_high(m):
                act.wait_ge(sem("zf_ready"), m + 1)
                nc.scalar.copy(ZH[:, m, :], ZF[:, m % 4, :]).then_inc(sem("zh_ready"), 1)

            for m in range(32):
                used(FIRST["w1"] + m)
                if m >= 4:
                    act.wait_ge(sem("zf_ready"), m - 3)
                A(RT[:, m % 4, :], PS[:, 4 + m % 4, 0:S], ACT.Relu).then_inc(sem("relu_ready"), 1)
                if m >= 1:
                    z_high(m - 1)
            z_high(31)

            feed(FIRST["w2"] + 31)
            sumsq(2, "h_ready", 2)
            root(2, ST[:, 20:22], ST[:, 20:22], 4)
            evac_high(T_PLE, "norm_ple")
            act.wait_ge(sem("ptr_ready"), 1)
            nc.scalar.copy(PTH[:, :, :], PS[:, 0, :].rearrange("p (c s) -> p c s", c=2)).then_inc(sem("pth_ready"), 1)
            for g in range(2):
                used(FIRST["ple_gate"] + 4 * g + 3)
                for t in range(NT):
                    last = A(SGP[:, t, g * 512:(g + 1) * 512], PS[:, 2 * (g % 2) + t, :], ACT.Sigmoid)
                last.then_inc(sem("sgp_out"), 1)

            feed(FIRST["ple"] + 1)
            sumsq(3, "h_ready", 3)
            root(3, ST[:, 22:24], ST[:, 22:24], 5)
            act.dma_start(lora[:, :, :], lora_in).then_inc(sem("lora_landed"), 16)
            evac_high(T_X1, None)

            for m in range(RW_CHUNKS):
                used(FIRST["rwkv"] + m)
                if m == 0:
                    act.wait_ge(sem("z_zero"), 1)
                nc.scalar.copy(Z[:, m, 1:S + 1], PS[:, 4 + m % 4, 0:S]).then_inc(sem("b2_out"), 1)
            for m in range(8):
                used(FIRST["fox_qk"] + m)
                nc.scalar.copy(fqk[:, m, :], PS[:, 4 + (RW_CHUNKS + m) % 4, 0:S]).then_inc(sem("b2_out"), 1)
            act.wait_ge(sem("sh_ready"), RW_CHUNKS)
            A(LT[0:64, 0, :], SH[0:64, 12, :], ACT.Tanh)
            nc.scalar.copy(LT[64:128, 0, :], SH[64:128, 12, :])
            A(LT[:, 1, :], SH[:, 13, :], ACT.Sigmoid).then_inc(sem("lt_ready"), 1)
            feed(FIRST["fox_v"] + 3)
            act.wait_ge(sem("fr_ready"), 1)
            A(fr[:, 1, :], fr[:, 0, :], ACT.Abs).then_inc(sem("f_act"), 1)
            act.wait_ge(sem("f_act"), 1)
            A(fr[:, 1, :], fr[:, 1, :], ACT.Exp, scale=-1.0).then_inc(sem("f_act"), 1)
            act.wait_ge(sem("f_act"), 2)
            A(fr[:, 1, :], fr[:, 1, :], ACT.Ln, bias=eps_c[0:FH, 0:1]).then_inc(sem("f_act"), 1)
            act.wait_ge(sem("lora_mm"), 1)
            for c in range(4):
                last = A(T[4][:, c, :], PS[:, 4 + c // 2, (c % 2) * S:(c % 2 + 1) * S], ACT.Sigmoid, bias=col("w0", c))
            last.then_inc(sem("sigw_ready"), 1)
            for c in range(4):
                last = A(T[3][:, c, :], PS[:, 6 + c // 2, (c % 2) * S:(c % 2 + 1) * S], ACT.Sigmoid, bias=col("a0", c))
            last.then_inc(sem("aa_ready"), 1)
            act.wait_ge(sem("lora_mm"), 2)
            nc.scalar.copy(GG[:, :, :].rearrange("p c s -> p (c s)"), PS[:, 0:2, :].rearrange("p b n -> p (b n)")).then_inc(
                sem("gg_ready"), 1)
            feed(FIRST["gates"])
            act.wait_ge(sem("lg_ready"), 2)
            A(T[0][:, :, :], T[5][:, :, :], ACT.Exp, scale=-DECAY)
            A(T[1][:, :, :], T[5][:, :, :], ACT.Exp, scale=DECAY)
            A(T[2][:, :, :], T[2][:, :, :], ACT.Exp, scale=-DECAY).then_inc(sem("gdec_ready"), 1)

            def gate_out(g):
                used(FIRST["gates"] + 4 * g + 3)
                for t in range(NT):
                    last = A(SG[:, t, g * 512:(g + 1) * 512], PS[:, 2 * ((g + 1) % 2) + t, :], ACT.Sigmoid)
                last.then_inc(sem("gate_out"), 1)

            gate_out(0)
            root(0, T[7][:, :, :], T[7][:, :, :], 6)
            gate_out(1)
            gate_out(2)
            gate_out(3)

            def f_exp(h):
                act.wait_ge(sem("fmax_ready"), h + 1)
                s0 = 64 + 8 * (h % 2)
                A(fp[:, h % 2, 0:P], fp[:, h % 2, 0:P], ACT.Exp, bias=ST[:, s0 + 2:s0 + 3], scale=FD ** -0.5,
                  accum_out=ST[:, s0 + 4:s0 + 5])
                A(fp[:, h % 2, P:384], fp[:, h % 2, P:384], ACT.Exp, bias=ST[:, s0 + 3:s0 + 4], scale=FD ** -0.5,
                  accum_out=ST[:, s0 + 5:s0 + 6]).then_inc(sem("fexp_ready"), 1)

            def f_pt(h):
                act.wait_ge(sem("fpt_mm"), h + 1)
                if h >= 2:
                    act.wait_ge(sem("fo_mm"), h - 1)
                nc.scalar.copy(fpt[:, h % 2, :], PS[:, 6 + h % 2, 0:384]).then_inc(sem("fpt_ready"), 1)

            for h in range(FH + 1):
                if h < FH:
                    f_exp(h)
                if h >= 1:
                    f_pt(h - 1)
            act.wait_ge(sem("fo_mm"), FH)
            nc.scalar.copy(YFH[:, :, :].rearrange("p c s -> p (c s)"), PS[:, 0:2, :].rearrange("p b n -> p (b n)")).then_inc(
                sem("yfh_ready"), 1)

            act.wait_ge(sem("bkt_mm"), 1)
            nc.scalar.copy(BKT[:, :, :, :].rearrange("p c q n -> p (c q n)"),
                           PS[:, 0:4, :].rearrange("p b n -> p (b n)")).then_inc(sem("bkt_ready"), 1)
            act.wait_ge(sem("uv_mm"), 1)
            nc.scalar.copy(UV[:, :, :, :].rearrange("p c q n -> p (c q n)"),
                           PS[:, 4:8, :].rearrange("p b n -> p (b n)")).then_inc(sem("uv_ready"), 1)
            for k, (_, _, dst, adds, _) in enumerate(INVERSE):
                if adds:
                    continue
                for half in range(2):
                    act.wait_ge(sem(f"inv_mm{half}"), k + 1)
                    b = 4 * half + 2 * (k % 2)
                    nc.scalar.copy(inv[half][dst][:, :, :].rearrange("p u n -> p (u n)"),
                                   PS[:, b:b + 2, :].rearrange("p b n -> p (b n)")).then_inc(
                                       sem(f"inv_copied{half}"), 1)
            feed(FIRST["p_fox"])
            for c in range(NCH):
                act.wait_ge(sem("u_mm"), c + 1)
                for h2 in range(2):
                    rows = slice(64 * h2, 64 * h2 + 64)
                    last = nc.scalar.copy(UV[rows, c, :, rows], PS[rows, 1, 0:S].rearrange("p (q n) -> p q n", n=RN))
                last.then_inc(sem("u_ready"), 1)
                feed(FIRST["p_fox"] + c)
                act.wait_ge(sem("y_mm"), c + 1)
                nc.scalar.copy(YT[:, :, c * CH_T:(c + 1) * CH_T],
                               PS[:, 2, 0:S].rearrange("p (q t) -> p q t", q=NPAIR)).then_inc(sem("yt_ready"), 1)
            for b in range(2):
                act.wait_ge(sem("gn_mm"), 3 + b)
                var = T[2][:, 2 * b:2 * b + 2, :].rearrange("p c s -> p (c s)")
                A(var, PS[:, 6 + b, :], ACT.Ln, bias=eps_c[:, 1:2], scale=1.0 / RN).then_inc(sem("gn_act"), 1)
            act.wait_ge(sem("gn_act"), 2)
            for b in range(2):
                var = T[2][:, 2 * b:2 * b + 2, :]
                A(var, var, ACT.Exp, scale=-0.5).then_inc(sem("rstd_ready"), 1)
            for b in range(2):
                act.wait_ge(sem("yr_ready"), b + 1)
                nc.scalar.copy(YRH[:, 2 * b:2 * b + 2, :], YC[:, 2 * b:2 * b + 2, :]).then_inc(sem("yrh_ready"), 1)
            feed(FIRST["p_rwkv"] + 3)
            act.wait_ge(w_used, FIRST["p_rwkv"])
            act.dma_start(LG1[:, :], rows_in[2:3, :].broadcast_to([P, D])).then_inc(sem("ln1_landed"), 16)
            act.dma_start(LB1[:, :], rows_in[3:4, :].broadcast_to([P, D])).then_inc(sem("ln1_landed"), 16)
            evac_high(T_MERGED, None)
            feed(FIRST["w_o"] + 7)

            def layer_norm(k, h_val, ms_val):
                act.wait_ge(sem("h_ready"), h_val)
                for t in range(NT):
                    A(XS[:, t, :], H[:, t, :], ACT.Copy, accum_out=ST[:, 80 + 2 * k + t:81 + 2 * k + t]).then_inc(
                        sem("sum_ready"), 1)
                for t in range(NT):
                    act.wait_ge(sem("xc_ready"), 2 * k + t + 1)
                    A(XS[:, t, :], H[:, t, :], ACT.Square, accum_out=ST[:, 88 + 2 * k + t:89 + 2 * k + t]).then_inc(
                        sem("var_ready"), 1)
                root(0, ST[:, 96 + 2 * k:98 + 2 * k], ST[:, 96 + 2 * k:98 + 2 * k], ms_val)

            layer_norm(0, 5, 7)
            evac_high(T_X2, None)
            for m in range(LISTS):
                used(FIRST["peer_q"] + m)
                nc.scalar.copy(QH[:, m, :], PS[:, 4 + m % 4, 0:S]).then_inc(sem("qh_ready"), 1)
            used(FIRST["keys"] + 1)
            for t in range(NT):
                nc.scalar.copy(SC[:, t, :, :].rearrange("p l k -> p (l k)"),
                               PS[:, 4 * t:4 * t + 4, :].rearrange("p b n -> p (b n)")).then_inc(sem("u_bank_free"), 1)

            U0 = FIRST["u"]
            feed(U0 - 1 + 1)
            assert feed_at[0] == U0 + RING

            def u_evac(i, half, static):
                act.wait_ge(w_used, U0 + 4 * i + 2 * half + 2)
                A(HS[:, bass.ds(4 * i + 2 * half, 2), :], PS[:, half, :].rearrange("p (j s) -> p j s", j=2),
                  ACT.Gelu).then_inc(sem("u_bank_free"), 1)

            def u_body(i):
                for half in range(2):
                    for c in (2 * half, 2 * half + 1):
                        n = 4 * i + RING + c
                        split_high_dyn(U0, n, c)
                    u_evac(i, half, False)

            def split_high_dyn(first, rel, c):
                slot = (first + c) % RING
                act.wait_ge(w_landed[slot], 16 * ((first + c) // RING + 1) + 4 * (rel - c))
                act.wait_ge(w_used, rel + (first + 1 - RING))
                nc.scalar.copy(WH[:, slot, :], RAW[:, slot, :]).then_inc(w_hi, 1)

            with act.Fori(0, NK // 8) as i:
                u_body(i)
            act.wait_ge(sem("bv_ready"), 1)
            A(be[:, :, :, :], be[:, :, :, :], ACT.Exp).then_inc(sem("bexp_ready"), 1)
            act.wait_ge(sem("ijg_ready"), 1)
            act.wait_ge(sem("ijg_mm"), 1)
            nc.scalar.copy(IT[:, :], PS[:, 2, 0:S])
            nc.scalar.copy(JT[:, :], PS[:, 2, S:2 * S])
            nc.scalar.copy(GT[:, :], PS[:, 3, 0:S]).then_inc(sem("ijgT_ready"), 1)
            with act.Fori(NK // 8, NK // 4) as i:
                u_body(i)
            feed_at[0] = FIRST["v_table"] + RING

            act.wait_ge(w_used, FIRST["v_table"])
            act.dma_start(LG2[:, :], rows_in[4:5, :].broadcast_to([P, D])).then_inc(sem("ln2_landed"), 16)
            act.dma_start(LB2[:, :], rows_in[5:6, :].broadcast_to([P, D])).then_inc(sem("ln2_landed"), 16)

            V0 = FIRST["v_table"]

            def c_high(j, slot, first=False):
                if not first:
                    act.wait_ge(w_used, j + (V0 + 1 - RING))
                nc.scalar.copy(CH[:, slot, :], HS[:, j, :] if isinstance(j, int) else HS[:, bass.ds(j, 1), :].rearrange(
                    "p a s -> p (a s)")).then_inc(sem("ch_ready"), 1)

            act.wait_ge(sem("gated"), S // 8)
            for c in range(RING):
                c_high(c, c, True)
            with act.Fori(0, NK // 8 - 1) as i:
                for c in range(4):
                    split_high_dyn(V0, 4 * i + RING + c, c)
                    c_high(4 * i + RING + c, c)
            for c in range(4):
                split_high_dyn(V0, NK // 2 + c, c)
            act.wait_ge(sem("gated"), 2 * S // 8)
            for c in range(4):
                c_high(NK // 2 + c, c)
            with act.Fori(NK // 8, NK // 4 - 1) as i:
                for c in range(4):
                    split_high_dyn(V0, 4 * i + RING + c, c)
                    c_high(4 * i + RING + c, c)
            layer_norm(1, 7, 8)

        @block.tensor
        def _(pe):
            mm = nc.tensor.matmul
            tp = nc.tensor.transpose

            def transposes(r, src, name, value):
                if value is not None:
                    pe.wait_ge(sem(name), value)
                for c in range(KC):
                    for t in range(NT):
                        last = tp(PS[:, 4 + c // 2, (c % 2) * S + t * P:(c % 2) * S + (t + 1) * P],
                                  src[:, t, c * P:(c + 1) * P], ident[:, :])
                    if c % 2:
                        last.then_inc(sem("tr_ready"), 1)

            def split(pairs, dst, start, stop):
                for k, (a, b) in enumerate(pairs):
                    last = mm(dst, a, b, start=start and k == 0, stop=stop and k == len(pairs) - 1)
                return last

            def form_a(first, groups, per_group, xh, xl, bank=lambda g: 2 * (g % 2), free=None, seed=None, ready=None):
                n = first
                for g in range(groups):
                    if free:
                        free(g)
                    if seed:
                        seed(g)
                    for i in range(per_group):
                        if ready and g == 0:
                            ready(i)
                        pe.wait_ge(w_lo, n + 1)
                        for kk in range(2):
                            k = 2 * i + kk
                            wh = WH[:, n % RING, kk * 512:(kk + 1) * 512]
                            wl = WL[:, n % RING, kk * 512:(kk + 1) * 512]
                            for t in range(NT):
                                h, l = xh[:, k, t * P:(t + 1) * P], xl[:, k, t * P:(t + 1) * P]
                                last = split([(h, wh), (h, wl), (l, wh)], PS[:, bank(g) + t, :],
                                             k == 0 and not seed, k == 2 * per_group - 1)
                        last.then_inc(w_used, 1)
                        n += 1

            def form_b(first, count, place, free):
                for m in range(count):
                    n = first + m
                    free(m)
                    pe.wait_ge(w_lo, n + 1)
                    for k in range(KC):
                        wh, wl = WH[:, n % RING, k * P:(k + 1) * P], WL[:, n % RING, k * P:(k + 1) * P]
                        last = split([(wh, XH[:, k, :]), (wh, XL[:, k, :]), (wl, XH[:, k, :])], place(m),
                                     k == 0, k == KC - 1)
                    last.then_inc(w_used, 1)

            def wait(name, value):
                if value > 0:
                    pe.wait_ge(sem(name), value)

            def small_gates(bank, wh, wl, n):
                for t in range(NT):
                    for k in range(KC):
                        h, l = XH[:, k, t * P:(t + 1) * P], XL[:, k, t * P:(t + 1) * P]
                        last = split([(h, wh[:, k]), (h, wl[:, k]), (l, wh[:, k])], PS[:, bank, t * n:(t + 1) * n],
                                     k == 0, k == KC - 1)
                return last

            pe.wait_ge(sem("ident_ready"), 1)
            transposes(T_MIX, XS, "xs_ready", 2)
            wait("xl_ready", 8)
            wait("gwl_ready", 1)
            small_gates(3, GWH[:, :, 0:16], GWL[:, :, 0:16], 16).then_inc(sem("gates_mm"), 1)
            wait("gtok_ready", 1)
            for c in range(4):
                for t in range(NT):
                    last = tp(PS[0:MH, 1 + c // 2, (c % 2) * S + t * P:(c % 2) * S + (t + 1) * P],
                              gtok[:, t, 4 * c:4 * c + 4], ident[:, :])
            last.then_inc(sem("grow_mm"), 1)
            form_b(FIRST["qk"], 8, lambda m: PS[:, 4 + m % 4, 0:S], lambda m: wait("qk_out", m - 3))
            wait("gr_ready", 1)
            form_a(FIRST["v"], 2, 4, XH, XL)
            form_a(FIRST["o"], 2, 4, XH, XL, free=lambda g: wait("v_out", g + 1))

            wait("m_ready", 1)
            wait("emt_ready", 1)
            wait("qk_out", 8)
            for k in range(2):
                for d in range(2):
                    for t in range(NT):
                        j = 4 * k + 2 * d + t
                        row = (4 if k == 0 else 0) + d
                        last = tp(PS[:, 7, 4 * j:4 * j + 4], GA[:, row, t * P:(t + 1) * P], ident[0:MH, 0:MH])
            last.then_inc(sem("at_mm"), 1)
            wait("at_ready_m", 1)
            wait("consts_ready", 1)

            def scores(h):
                wait("sm_ready", 2 * h - 2)
                for sb in range(NT):
                    last = mm(PS[:, 4 + h % 2, sb * S:(sb + 1) * S], qkT[:, MH + h, sb * P:(sb + 1) * P],
                              qkT[:, h, :], start=True, stop=True)
                last.then_inc(sem("st_mm"), 1)
                wait("w_ready", 2 * h - 2)
                for d in range(2):
                    last = mm(PS[:, 6 + h % 2, d * S:(d + 1) * S], sel4[:, h, :], GA[:, 6 + d, :], start=True,
                              stop=True)
                last.then_inc(sem("mb_mm"), 1)

            def numerators(e):
                h, d = e // 2, e % 2
                wait("p_ready", e + 1)
                if e < 2:
                    wait("o_out", 2)
                wait("fin_done", e - 1)
                for t in range(NT):
                    sources = range(0, t + 1) if d == 0 else range(t, NT)
                    for sb in sources:
                        last = mm(PS[:, 2 * (e % 2) + t, 0:MDV + 1], SM[:, e % 2, sb, t * P:(t + 1) * P],
                                  v1[:, sb, h, :], start=(sb == sources[0]), stop=(sb == sources[-1]))
                last.then_inc(sem("num_mm"), 1)

            scores(0)
            for e in range(2 * MH):
                if e % 2 == 0 and e + 2 < 2 * MH:
                    scores(e // 2 + 1)
                numerators(e)
            transposes(T_HEADS, XS, "xs_ready", 4)
            wait("xl_ready", 16)
            form_a(FIRST["mix_out"], 2, 4, XH, XL)

            transposes(T_MLP, XS, "xs_ready", 6)
            wait("xl_ready", 24)
            form_b(FIRST["w1"], 32, lambda m: PS[:, 4 + m % 4, 0:S], lambda m: wait("relu_ready", m - 3))
            form_a(FIRST["w2"], 2, 16, ZH, ZL, ready=lambda i: wait("zl_ready", 2 * i + 2))

            transposes(T_PLE, XS, "xs_ready", 8)
            wait("p_landed", 16)
            for c in range(2):
                for t in range(NT):
                    last = tp(PS[:, 0, c * S + t * P:c * S + (t + 1) * P], P2[:, t, c * P:(c + 1) * P], ident[:, :])
            last.then_inc(sem("ptr_ready"), 1)
            wait("xl_ready", 32)
            wait("ptl_ready", 1)
            wait("brow_landed", 16)

            def bias(g):
                for t in range(NT):
                    mm(PS[:, 2 * (g % 2) + t, :], ones_row[0:1, :], brow[0:1, g * 512:(g + 1) * 512], start=True,
                       stop=False)

            form_a(FIRST["ple_gate"], 2, 4, XH, XL, seed=bias)
            form_a(FIRST["ple"], 2, 1, PTH, PTL, free=lambda g: wait("sgp_out", g + 1))

            transposes(T_X1, H, "h_ready", 4)
            wait("xl_ready", 40)
            form_b(FIRST["rwkv"], RW_CHUNKS, lambda m: PS[:, 4 + m % 4, 0:S], lambda m: wait("b2_out", m - 3))
            form_b(FIRST["fox_qk"], 8, lambda m: PS[:, 4 + (RW_CHUNKS + m) % 4, 0:S],
                   lambda m: wait("b2_out", RW_CHUNKS + m - 3))
            small_gates(3, FWH, FWL, 8).then_inc(sem("f_mm"), 1)
            form_a(FIRST["fox_v"], 1, 4, XH, XL)
            wait("ftok_ready", 1)
            for t in range(NT):
                last = tp(PS[0:FH, 2, t * P:(t + 1) * P], ftok[:, t, :], ident[:, :])
            last.then_inc(sem("frow_mm"), 1)
            wait("lt_ready", 1)
            wait("lora_landed", 16)
            wait("b2_out", RW_CHUNKS + 8)
            for c in range(4):
                mm(PS[:, 4 + c // 2, (c % 2) * S:(c % 2 + 1) * S], lora[0:64, 0, c * P:(c + 1) * P], LT[0:64, 0, :],
                   start=True, stop=True)
            for c in range(4):
                last = mm(PS[:, 6 + c // 2, (c % 2) * S:(c % 2 + 1) * S], lora[64:128, 0, c * P:(c + 1) * P],
                          LT[64:128, 0, :], start=True, stop=True)
            last.then_inc(sem("lora_mm"), 1)
            wait("fv_ready", 1)
            for c in range(4):
                last = mm(PS[:, c // 2, (c % 2) * S:(c % 2 + 1) * S], lora[:, 1, c * P:(c + 1) * P], LT[:, 1, :],
                          start=True, stop=True)
            last.then_inc(sem("lora_mm"), 1)
            wait("fr_ready", 1)

            def gates(g, free=None):
                form_a(FIRST["gates"] + 4 * g, 1, 4, XH, XL, bank=lambda _: 2 * ((g + 1) % 2), free=free)

            gates(0)
            wait("kksq_ready", 1)
            wait("sigw_ready", 1)
            for b in range(2):
                last = mm(PS[:, 4 + b, :], blk_ones[:, :], T[7][:, 2 * b:2 * b + 2, :], start=True, stop=True)
            last.then_inc(sem("kkss_mm"), 1)
            gates(1, lambda _: wait("gg_ready", 1))
            wait("bonp_ready", 1)
            wait("aa_ready", 1)
            for b in range(2):
                last = mm(PS[:, 6 + b, :], blk_ones[:, :], T[7][:, 2 * b:2 * b + 2, :], start=True, stop=True)
            last.then_inc(sem("bon_mm"), 1)
            gates(2, lambda _: wait("gate_out", 1))
            gates(3, lambda _: wait("gate_out", 2))

            wait("nc8_ready", 1)
            wait("nk_ready", 1)
            wait("bon_ready", 1)
            wait("gate_out", 4)

            def f_scores(h):
                b = 64 * (h % 2)
                wait("fmax_ready", h - 1)
                for t in range(NT):
                    n = (t + 1) * P
                    dst = PS[:, 4 + h % 2, t * P:t * P + n]
                    mm(dst, fqk[b:b + 64, h // 2, t * P:(t + 1) * P], fqk[b:b + 64, 4 + h // 2, 0:n], start=True,
                       stop=False)
                    last = mm(dst, sel8[:, h, :], fr[:, 2, 0:n], start=False, stop=True)
                last.then_inc(sem("fs_mm"), 1)

            def f_transposes(h):
                wait("fnorm_ready", h + 1)
                wait("fpt_ready", h - 1)
                for k in range(3):
                    last = tp(PS[:, 6 + h % 2, k * P:(k + 1) * P], fp[:, h % 2, k * P:(k + 1) * P], ident[:, :])
                last.then_inc(sem("fpt_mm"), 1)

            def f_values(h):
                wait("fpt_ready", h + 1)
                b = 64 * (h % 2)
                for t in range(NT):
                    for sb in range(t + 1):
                        k = 0 if t == 0 else 1 + sb
                        last = mm(PS[b:b + 64, h // 4, (h // 2 % 2) * S + t * P:(h // 2 % 2) * S + (t + 1) * P],
                                  fv[:, sb, h * FD:(h + 1) * FD], fpt[:, h % 2, k * P:(k + 1) * P], start=(sb == 0),
                                  stop=(sb == t))
                last.then_inc(sem("fo_mm"), 1)

            f_scores(0)
            f_scores(1)
            for h in range(FH):
                f_transposes(h)
                if h + 2 < FH:
                    f_scores(h + 2)
                f_values(h)

            wait("bk_ready", 1)
            wait("yfh_ready", 1)
            wait("yfl_ready", 1)
            for c in range(NCH):
                for q in range(NPAIR):
                    last = tp(PS[:, c, q * P:(q + 1) * P], BK[:, q, c, :, :].rearrange("p a t -> p (a t)"), ident[:, :])
            last.then_inc(sem("bkt_mm"), 1)
            wait("bkt_ready", 1)
            for c in range(NCH):
                for h2 in range(2):
                    b = 64 * h2
                    for q in range(NPAIR):
                        last = mm(PS[:, 2 * c + h2, q * P:(q + 1) * P],
                                  BK[b:b + 64, q, c, :, :].rearrange("p a t -> p (a t)"),
                                  CR[b:b + 64, q, c, :, :].rearrange("p a t -> p (a t)"), start=True, stop=True)
                    last.then_inc(sem("sc_mm"), 1)
            wait("vp_ready", 1)
            for c in range(NCH):
                for q in range(NPAIR):
                    last = tp(PS[:, 4 + c, q * P:(q + 1) * P], BK[:, q, c, :, :].rearrange("p a t -> p (a t)"),
                              ident[:, :])
            last.then_inc(sem("uv_mm"), 1)
            wait("uv_ready", 1)

            for k, (a, b, dst, adds, need) in enumerate(INVERSE):
                for half in range(2):
                    if k == 0:
                        wait("inv_in", half + 1)
                    upto = max(need, k - 2)
                    wait(f"inv_added{half}", evacuated(upto, True))
                    wait(f"inv_copied{half}", evacuated(upto, False))
                    bank = 4 * half + 2 * (k % 2)
                    for u in range(8):
                        dst = PS[:, bank + u // 4, (u % 4) * P:(u % 4 + 1) * P]
                        left = inv[half][a][:, u, :]
                        if b == "I":
                            last = tp(dst, left, ident[:, :])
                        else:
                            last = mm(dst, left, inv[half][b][:, u, :], start=True, stop=True)
                    last.then_inc(sem(f"inv_mm{half}"), 1)
            for half in range(2):
                wait(f"inv_added{half}", evacuated(len(INVERSE) - 1, True))

            def fox_part(c, t):
                n = FIRST["p_fox"] + c
                pe.wait_ge(w_lo, n + 1)
                for kk in range(2):
                    k = 2 * (c % 2) + kk
                    wh = WH[:, n % RING, kk * 512:(kk + 1) * 512]
                    wl = WL[:, n % RING, kk * 512:(kk + 1) * 512]
                    h, l = YFH[:, k, t * P:(t + 1) * P], YFL[:, k, t * P:(t + 1) * P]
                    last = split([(h, wh), (h, wl), (l, wh)], PS[:, 4 + 2 * (c // 2) + t, :], k == 0, k == 3)
                if t:
                    last.then_inc(w_used, 1)

            for c in range(NCH):
                wait("s_ready", c)
                for q in range(NPAIR):
                    for h2 in range(2):
                        rows = slice(64 * h2, 64 * h2 + 64)
                        dst = PS[rows, 0, q * 64:(q + 1) * 64]
                        if c:
                            mm(dst, CR[:, q, c, 0, :], S2[:, q, rows], start=True, stop=True)
                        last = mm(dst, PK[:, c, h2, q, 0:64], UV[:, c, q, rows], start=(c == 0), stop=True,
                                  skip_group_check=True)
                last.then_inc(sem("z_mm"), 1)
                fox_part(c, 0)
                wait("zs_ready", c + 1)
                for q in range(NPAIR):
                    last = mm(PS[:, 1, q * 64:(q + 1) * 64], MINV[:, c, q, :], ZS[:, q, :], start=True, stop=True)
                last.then_inc(sem("u_mm"), 1)
                wait("u_ready", c + 1)
                for q in range(NPAIR):
                    last = mm(PS[:, 3, q * P:(q + 1) * P], BKT[:, c, q, :], UV[:, c, q, :], start=True, stop=True)
                last.then_inc(sem("su_mm"), 1)
                wait("yt_ready", c)
                for q in range(NPAIR):
                    if c:
                        mm(PS[:, 2, q * 64:(q + 1) * 64], S2[:, q, :], CR[:, q, c, 1, :], start=True, stop=True)
                    for h2 in range(2):
                        rows = slice(64 * h2, 64 * h2 + 64)
                        last = mm(PS[rows, 2, q * 64:(q + 1) * 64], UV[:, c, q, rows], PK[:, c, h2, q, 64:128],
                                  start=(c == 0), stop=True, skip_group_check=True)
                last.then_inc(sem("y_mm"), 1)
                fox_part(c, 1)
            wait("yt_ready", NCH)
            for b in range(2):
                wait("pf_out", b + 1)
                mm(PS[:, 4 + b, :], blk_ones[:, :], YT[:, 2 * b:2 * b + 2, :], start=True, stop=True).then_inc(
                    sem("gn_mm"), 1)
            for b in range(2):
                wait("ysq_ready", b + 1)
                mm(PS[:, 6 + b, :], blk_ones[:, :], T[0][:, 2 * b:2 * b + 2, :], start=True, stop=True).then_inc(
                    sem("gn_mm"), 1)

            form_a(FIRST["p_rwkv"], 2, 2, YRH, YRL, ready=lambda i: wait("yrl_ready", i + 1))
            transposes(T_MERGED, XS, "xs_ready", 10)
            wait("xl_ready", 48)
            form_a(FIRST["w_o"], 2, 4, XH, XL)

            transposes(T_X2, H, "h_ready", 6)
            wait("xl_ready", 56)
            form_b(FIRST["peer_q"], LISTS, lambda m: PS[:, 4 + m % 4, 0:S], lambda m: wait("ql_ready", m - 3))
            wait("ql_ready", LISTS)
            for i in range(2):
                n = FIRST["keys"] + i
                pe.wait_ge(w_lo, n + 1)
                for j in range(LISTS // 2):
                    l = i * (LISTS // 2) + j
                    wh, wl = WH[:, n % RING, j * NK:(j + 1) * NK], WL[:, n % RING, j * NK:(j + 1) * NK]
                    for t in range(NT):
                        h, lo = QH[:, l, t * P:(t + 1) * P], QL[:, l, t * P:(t + 1) * P]
                        last = split([(h, wh), (h, wl), (lo, wh)], PS[:, 4 * t + l // 4, (l % 4) * NK:(l % 4 + 1) * NK],
                                     True, True)
                last.then_inc(w_used, 1)

            U0 = FIRST["u"]

            def gates_of(phase, i, c, first=False):
                for g in range(2):
                    pair = 8 * i + (2 * c + g)
                    if c % 2 == 0 and g == 0 and not first:
                        pe.wait_ge(sem("gated"), 2 * i + (c // 2 - 1 + phase * (S // 8)))
                    pe.wait_ge(sem("hot_ready"), pair + (1 + phase * (S // 2)))
                    for a in range(2):
                        k = 4 * (c % 2) + 2 * g + a
                        last = mm(PS[:, 4 + c // 2, k * 64:(k + 1) * 64], hot_i[:, g, a, :], hot_j[:, g, a, :],
                                  start=True, stop=True)
                    last.then_inc(sem("gates_mm2"), 1)

            def u_body(i, phase=None, first=False):
                for c in range(4):
                    slot = (U0 + c) % RING
                    if c % 2 == 0:
                        pe.wait_ge(sem("u_bank_free"), 2 * i + (c // 2 + 1))
                    pe.wait_ge(w_lo, 4 * i + (U0 + c + 1))
                    for k in range(KC):
                        wh, wl = WH[:, slot, k * P:(k + 1) * P], WL[:, slot, k * P:(k + 1) * P]
                        last = split([(wh, XH[:, k, :]), (wh, XL[:, k, :]), (wl, XH[:, k, :])],
                                     PS[:, c // 2, (c % 2) * S:(c % 2 + 1) * S], k == 0, k == KC - 1)
                    last.then_inc(w_used, 1)
                    if phase is not None:
                        gates_of(phase, 0 if first else i - NK // 8, c, first)

            with pe.Fori(0, NK // 8) as i:
                u_body(i)
            wait("ijg_ready", 1)
            for a in range(3):
                for t in range(NT):
                    k = a * S + t * P
                    last = tp(PS[:, 2 + a // 2, (a % 2) * S + t * P:(a % 2) * S + (t + 1) * P], ijg[:, t, a, :],
                              ident[:, :])
            last.then_inc(sem("ijg_mm"), 1)
            u_body(NK // 8, 0, first=True)
            with pe.Fori(NK // 8 + 1, NK // 4) as i:
                u_body(i, 0)

            V0 = FIRST["v_table"]

            def v_item(j, c, start=False, stop=False):
                slot = (V0 + c) % RING
                pe.wait_ge(w_lo, j + (V0 + 1))
                pe.wait_ge(sem("cl_ready"), j + 1)
                for t in range(NT):
                    h, l = CH[:, c, t * P:(t + 1) * P], CL[:, c, t * P:(t + 1) * P]
                    for half in range(2):
                        wh = WH[:, slot, half * 512:(half + 1) * 512]
                        wl = WL[:, slot, half * 512:(half + 1) * 512]
                        last = split([(h, wh), (h, wl), (l, wh)], PS[:, 2 * t + half, :], start, stop)
                last.then_inc(w_used, 1)

            for c in range(4):
                v_item(c, c, start=(c == 0))
                gates_of(1, 0, c)
            with pe.Fori(1, NK // 8) as i:
                for c in range(4):
                    v_item(4 * i + c, c)
                    gates_of(1, i, c)
            with pe.Fori(NK // 8, NK // 4 - 1) as i:
                for c in range(4):
                    v_item(4 * i + c, c)
            for c in range(4):
                v_item(NK - 4 + c, c, stop=(c == 3))

        @block.vector
        def _(dve):
            V = nc.vector
            step = sem("dve_step")
            steps = [0]

            def link(ins):
                steps[0] += 1
                ins.then_inc(step, 1)
                dve.wait_ge(step, steps[0])

            def wait(name, value):
                if value > 0:
                    dve.wait_ge(sem(name), value)

            def used(n):
                dve.wait_ge(w_used, n + 1)

            def mean_eps(dst, src, scale, eps):
                V.tensor_scalar(dst, src, scale, eps, ALU.mult, ALU.add).then_inc(sem("ms_ready"), 1)

            def normed(r, ss_val, root_val):
                wait("ss_ready", ss_val)
                rs = ST[:, 16 + 2 * r:18 + 2 * r]
                mean_eps(rs, ST[:, 2 * r:2 * r + 2], 1.0 / D, EPS)
                wait("sq_ready", root_val)
                link(V.reciprocal(rs, rs))

            def low_half(r, gain):
                for c in range(KC):
                    wait("xh_ready", 8 * r + c // 2 * 2 + 2)
                    V.scalar_tensor_tensor(XL[:, c, :], PS[:, 4 + c // 2, (c % 2) * S:(c % 2 + 1) * S],
                                           col(gain, c) if gain else 1.0, plain(XH[:, c, :]), ALU.mult,
                                           ALU.subtract).then_inc(sem("xl_ready"), 1)

            def scale_xs(r):
                for t in range(NT):
                    V.tensor_scalar(XS[:, t, :], H[:, t, :], ST[:, 16 + 2 * r + t:17 + 2 * r + t], None,
                                    ALU.mult).then_inc(sem("xs_ready"), 1)

            wait("consts_ready", 1)
            V.memset(v1[:, :, :, MDV:MDV + 1], 1.0)
            normed(0, 2, 1)
            scale_xs(0)
            wait("gwh_ready", 1)
            V.tensor_tensor(FWL[:, :, :], gw[:, :, 16:24], plain(FWH[:, :, :]), ALU.subtract)
            V.tensor_tensor(GWL[:, :, :], gw[:, :, :], plain(GWH[:, :, :]), ALU.subtract).then_inc(sem("gwl_ready"), 1)
            wait("vec_landed", 16)
            low_half(T_MIX, "norm_mix")

            wait("gates_mm", 1)
            V.tensor_copy(gtok[:, :, :].rearrange("p t g -> p (t g)"), PS[:, 3, 0:32]).then_inc(sem("gtok_ready"), 1)
            wait("grow_mm", 1)
            wait("mb_landed", 16)
            for k in range(4):
                last = V.tensor_scalar(GR[:, k, :], PS[0:MH, 1 + k // 2, (k % 2) * S:(k % 2 + 1) * S],
                                       mbias[:, k:k + 1], None, ALU.add)
            last.then_inc(sem("gr_ready"), 1)
            wait("gr_ready", 1)

            def qk_copy(m):
                used(FIRST["qk"] + m)
                V.tensor_copy(qkT[:, m, :], PS[:, 4 + m % 4, 0:S]).then_inc(sem("qk_out"), 1)

            for m in range(4):
                qk_copy(m)
            wait("g_act", 3)
            for d in range(2):
                f, i_ = GR[:, 2 * d + 1, :], GR[:, 2 * d, :]
                link(V.scalar_tensor_tensor(GA[:, 0, :], f, 0.0, GA[:, 2 + d, :], ALU.min, ALU.subtract))
                order = slice(None) if d == 0 else slice(None, None, -1)
                link(V.tensor_tensor_scan(GA[:, 2 + d, order], GA[:, 0, order], GA[:, 0, order], 0.0, ALU.add,
                                          ALU.bypass))
                link(V.tensor_tensor(GA[:, 4 + d, :], i_, GA[:, 2 + d, :], ALU.subtract))
                link(V.tensor_tensor_scan(GA[:, 6 + d, order], GA[:, 4 + d, order], GA[:, 4 + d, order], 0.0, ALU.max,
                                          ALU.bypass))
            V.tensor_tensor(GA[:, 0:2, :], GA[:, 2:4, :], GA[:, 6:8, :], ALU.add).then_inc(sem("m_ready"), 1)
            for m in range(4, 8):
                qk_copy(m)
            for g in range(2):
                used(FIRST["v"] + 4 * g + 3)
                for t in range(NT):
                    last = V.tensor_copy(v1[:, t, 2 * g:2 * g + 2, 0:MDV],
                                         PS[:, 2 * g + t, :].rearrange("p (h v) -> p h v", h=2))
                last.then_inc(sem("v_out"), 1)
            wait("at_mm", 1)
            V.tensor_copy(AT[:, :, :].rearrange("p j h -> p (j h)"), PS[:, 7, 0:32]).then_inc(sem("at_ready_m"), 1)
            wait("at_ready_m", 1)

            def exponents(e):
                h, d = e // 2, e % 2
                wait("mb_mm", h + 1)
                wait("p_ready", e - 1)
                for sb in range(NT):
                    a = AT[:, 2 * d + sb, h:h + 1]
                    last = V.tensor_scalar(WE[:, e % 2, sb, :], PS[:, 6 + h % 2, d * S:(d + 1) * S], a, 0.0,
                                           ALU.subtract, ALU.max)
                last.then_inc(sem("w_ready"), 1)

            def masked_scores(e):
                h, d = e // 2, e % 2
                wait("st_mm", h + 1)
                wait("num_mm", e - 1)
                V.scalar_tensor_tensor(SM[:, e % 2].rearrange("p a s -> p (a s)"), PS[:, 4 + h % 2, :], MDK ** -0.5,
                                       mask_m[:, d].rearrange("p a s -> p (a s)"), ALU.mult,
                                       ALU.mult).then_inc(sem("sm_ready"), 1)

            def weights_of(e):
                wait("e_ready", e + 1)
                wait("sm_ready", e + 1)
                V.tensor_tensor(SM[:, e % 2], SM[:, e % 2], WE[:, e % 2], ALU.mult).then_inc(sem("p_ready"), 1)

            def finish(e):
                h, d = e // 2, e % 2
                wait("num_mm", e + 1)
                wait("emt_ready", 1)
                den = [ST[:, 44 + 2 * (e % 2) + t:45 + 2 * (e % 2) + t] for t in range(NT)]
                raw = [PS[:, 2 * (e % 2) + t, MDV:MDV + 1] for t in range(NT)]
                least = [AT[:, 4 + 2 * d + t, h:h + 1] for t in range(NT)]
                for t in range(NT):
                    ins = V.tensor_scalar(den[t], raw[t], -1.0, least[t], ALU.mult, ALU.max)
                link(ins)
                for t in range(NT):
                    ins = V.scalar_tensor_tensor(den[t], raw[t], least[t], den[t], ALU.max, ALU.max)
                link(ins)
                both = ST[:, 44 + 2 * (e % 2):46 + 2 * (e % 2)]
                link(V.reciprocal(both, both))
                wait("fin_done", e)
                for t in range(NT):
                    num, acc = PS[:, 2 * (e % 2) + t, 0:MDV], hacc[:, t, h * MDV:(h + 1) * MDV]
                    if d == 0:
                        last = V.tensor_scalar(acc, num, den[t], None, ALU.mult)
                    else:
                        last = V.scalar_tensor_tensor(acc, num, den[t], acc, ALU.mult, ALU.add)
                last.then_inc(sem("fin_done"), 1)

            for e in range(2 * MH + 2):
                if e < 2 * MH:
                    exponents(e)
                    masked_scores(e)
                if 1 <= e <= 2 * MH:
                    weights_of(e - 1)
                if e >= 2:
                    finish(e - 2)
            wait("hss_ready", 1)
            mean_eps(ST[:, 32:40], ST[:, 24:32], 1.0 / MDV, EPS)
            wait("sq_ready", 2)
            link(V.reciprocal(ST[:, 32:40], ST[:, 32:40]))
            wait("o_out", 2)
            for t in range(NT):
                for h in range(MH):
                    k = slice(h * MDV, (h + 1) * MDV)
                    last = V.scalar_tensor_tensor(XS[:, t, k], hacc[:, t, k], ST[:, 32 + 4 * t + h:33 + 4 * t + h],
                                                  og[:, t, k], ALU.mult, ALU.mult)
                last.then_inc(sem("xs_ready"), 1)
            low_half(T_HEADS, "head_norm")

            def add_to_h(first, per_group, alpha=None):
                for g in range(2):
                    used(first + per_group * (g + 1) - 1)
                    for t in range(NT):
                        k = slice(g * 512, (g + 1) * 512)
                        src = PS[:, 2 * (g % 2) + t, :]
                        if alpha is None:
                            last = V.tensor_tensor(H[:, t, k], H[:, t, k], src, ALU.add)
                        else:
                            last = V.scalar_tensor_tensor(H[:, t, k], H[:, t, k], alpha, src, ALU.mult, ALU.add)
                return last

            add_to_h(FIRST["mix_out"], 4).then_inc(sem("h_ready"), 1)

            normed(1, 4, 3)
            scale_xs(1)
            low_half(T_MLP, "norm_mlp")

            def z_low(m):
                wait("zh_ready", m + 1)
                V.tensor_tensor(ZL[:, m, :], ZF[:, m % 4, :], plain(ZH[:, m, :]), ALU.subtract).then_inc(
                    sem("zl_ready"), 1)

            for m in range(32):
                wait("relu_ready", m + 1)
                wait("zl_ready", m - 3)
                V.tensor_tensor(ZF[:, m % 4, :], RT[:, m % 4, :], RT[:, m % 4, :], ALU.mult).then_inc(
                    sem("zf_ready"), 1)
                if m >= 1:
                    z_low(m - 1)
            z_low(31)
            add_to_h(FIRST["w2"], 16).then_inc(sem("h_ready"), 1)

            normed(2, 6, 4)
            scale_xs(2)
            low_half(T_PLE, "norm_ple")
            wait("pth_ready", 1)
            V.tensor_tensor(PTL[:, :, :], PS[:, 0, :].rearrange("p (c s) -> p c s", c=2), plain(PTH[:, :, :]),
                            ALU.subtract).then_inc(sem("ptl_ready"), 1)
            wait("sgp_out", 2)
            for g in range(2):
                used(FIRST["ple"] + g)
                k = slice(g * 512, (g + 1) * 512)
                for t in range(NT):
                    ins = V.tensor_tensor(XS[:, t, k], PS[:, 2 * g + t, :], SGP[:, t, k], ALU.mult)
                link(ins)
                for t in range(NT):
                    last = V.tensor_tensor(H[:, t, k], H[:, t, k], XS[:, t, k], ALU.add)
            last.then_inc(sem("h_ready"), 1)
            normed(3, 8, 5)
            wait("nfin_landed", 16)
            for t in range(NT):
                last = V.scalar_tensor_tensor(H[:, t, :], H[:, t, :], ST[:, 22 + t:23 + t], nfin[:, :], ALU.mult,
                                              ALU.mult)
            last.then_inc(sem("h_ready"), 1)
            V.memset(Z[:, :, 0:1], 0.0).then_inc(sem("z_zero"), 1)
            low_half(T_X1, None)

            wait("z_zero", 1)
            for m in range(RW_CHUNKS):
                wait("b2_out", m + 1)
                link(V.tensor_tensor(T[4][:, m % 4, :], Z[:, m, 0:S], Z[:, m, 1:S + 1], ALU.subtract))
                V.scalar_tensor_tensor(SH[:, m, :], T[4][:, m % 4, :], col("mu", m), Z[:, m, 1:S + 1], ALU.mult,
                                       ALU.add).then_inc(sem("sh_ready"), 1)
            wait("f_mm", 1)
            V.tensor_copy(ftok[:, :, :].rearrange("p t g -> p (t g)"), PS[:, 3, 0:16]).then_inc(sem("ftok_ready"), 1)
            used(FIRST["fox_v"] + 3)
            for t in range(NT):
                last = V.tensor_copy(fv[:, t, :], PS[:, t, :])
            last.then_inc(sem("fv_ready"), 1)
            wait("frow_mm", 1)
            wait("fb_landed", 16)
            V.tensor_scalar(fr[:, 0, :], PS[0:FH, 2, 0:S], fbias[:, 0:1], None, ALU.add).then_inc(sem("fr_ready"), 1)
            wait("sh_ready", RW_CHUNKS)
            for c in range(4):
                ins = V.tensor_scalar(T[6][:, c, :], SH[:, 4 + c, :], col("k_k", c), None, ALU.mult)
            link(ins)
            V.tensor_tensor(T[7][:, :, :], T[6][:, :, :], T[6][:, :, :], ALU.mult).then_inc(sem("kksq_ready"), 1)
            wait("f_act", 3)
            link(V.scalar_tensor_tensor(fr[:, 0, :], fr[:, 0, :], 0.0, fr[:, 1, :], ALU.min, ALU.subtract))
            link(V.tensor_tensor_scan(fr[:, 1, :], fr[:, 0, :], fr[:, 0, :], 0.0, ALU.add, ALU.bypass))
            V.tensor_scalar(fr[:, 2, :], fr[:, 1, :], -float(FD) ** 0.5, None, ALU.mult).then_inc(sem("nc8_ready"), 1)
            wait("sigw_ready", 1)
            flat = lambda x: x.rearrange("p c s -> p (c s)")
            link(V.tensor_tensor_scan(flat(T[5][:, :, :]), resets[:, :], flat(T[4][:, :, :]), 0.0, ALU.mult, ALU.add))
            V.tensor_tensor(T[2][:, :, :], T[5][:, :, :], T[4][:, :, :], ALU.subtract).then_inc(sem("lg_ready"), 2)
            wait("kkss_mm", 1)
            V.tensor_scalar(flat(T[7][:, :, :]), PS[:, 4:6, :].rearrange("p b n -> p (b n)"), 1e-24, None,
                            ALU.max).then_inc(sem("ms_ready"), 1)
            wait("gdec_ready", 1)
            V.tensor_copy(GL[:, :, :], T[0][:, :, :].rearrange("p q (c t) -> p q c t", t=CH_T)[:, :, :, CH_T - 1])
            wait("aa_ready", 1)
            for c in range(4):
                ins = V.tensor_scalar(T[5][:, c, :], T[3][:, c, :], 1.0, col("k_a", c), ALU.subtract, ALU.mult)
            link(ins)
            link(V.scalar_tensor_tensor(T[5][:, :, :], T[5][:, :, :], 1.0, SH[:, 4:8, :], ALU.add, ALU.mult))
            wait("sq_ready", 6)
            link(V.reciprocal(T[7][:, :, :], T[7][:, :, :]))
            V.tensor_tensor(T[6][:, :, :], T[6][:, :, :], T[7][:, :, :], ALU.mult).then_inc(sem("nk_ready"), 1)
            wait("nk_ready", 1)
            link(V.tensor_tensor(T[7][:, :, :], SH[:, 0:4, :], T[5][:, :, :], ALU.mult))
            for c in range(4):
                last = V.tensor_scalar(T[7][:, c, :], T[7][:, c, :], col("r_k", c), None, ALU.mult)
            last.then_inc(sem("bonp_ready"), 1)
            link(V.tensor_tensor(T[4][:, :, :], T[6][:, :, :], T[3][:, :, :], ALU.mult))
            chunked = lambda x: x.rearrange("p c (n t) -> p (c n) t", t=CH_T)
            part = lambda x, k: x[:, :, :, k, :].rearrange("p q c t -> p (q c) t")
            for h2 in range(2):
                rows = slice(64 * h2, 64 * h2 + 64)
                for k, src in ((h2, T[4]), (1 - h2, T[5])):
                    V.tensor_tensor(part(BK[rows], k), chunked(src[rows]), chunked(T[1][rows]), ALU.mult)
            V.tensor_tensor(part(CR, 0), chunked(T[6][:, :, :]), chunked(T[2][:, :, :]), ALU.mult)
            V.tensor_tensor(part(CR, 1), chunked(SH[:, 0:4, :]), chunked(T[0][:, :, :]), ALU.mult).then_inc(
                sem("bk_ready"), 1)
            wait("bon_mm", 1)
            V.tensor_tensor(flat(BON[:, :, :]), PS[:, 6:8, :].rearrange("p b n -> p (b n)"), flat(SH[:, 8:12, :]),
                            ALU.mult).then_inc(sem("bon_ready"), 1)
            wait("bon_ready", 1)
            for c in range(4):
                ins = V.tensor_scalar(BON[:, c, :], BON[:, c, :], col("ln_b", c), None, ALU.add)
            link(ins)

            def f_max(h):
                wait("fs_mm", h + 1)
                wait("fpt_mm", h - 1)
                s0 = 64 + 8 * (h % 2)
                V.tensor_tensor_reduce(out=fp[:, h % 2, 0:P], in0=PS[:, 4 + h % 2, 0:P], in1=mask_f[:, P:S], scale=1.0,
                                       scalar=3.0 * NEG, op0=ALU.add, op1=ALU.max, accum_out=ST[:, s0:s0 + 1])
                link(V.tensor_tensor_reduce(out=fp[:, h % 2, P:384], in0=PS[:, 4 + h % 2, P:384], in1=mask_f[:, :],
                                            scale=1.0, scalar=3.0 * NEG, op0=ALU.add, op1=ALU.max,
                                            accum_out=ST[:, s0 + 1:s0 + 2]))
                V.tensor_scalar(ST[:, s0 + 2:s0 + 4], ST[:, s0:s0 + 2], -float(FD) ** -0.5, None, ALU.mult).then_inc(
                    sem("fmax_ready"), 1)

            def f_norm(h):
                wait("fexp_ready", h + 1)
                s0 = 64 + 8 * (h % 2)
                link(V.reciprocal(ST[:, s0 + 4:s0 + 6], ST[:, s0 + 4:s0 + 6]))
                V.tensor_scalar(fp[:, h % 2, 0:P], fp[:, h % 2, 0:P], ST[:, s0 + 4:s0 + 5], None, ALU.mult)
                V.tensor_scalar(fp[:, h % 2, P:384], fp[:, h % 2, P:384], ST[:, s0 + 5:s0 + 6], None,
                                ALU.mult).then_inc(sem("fnorm_ready"), 1)

            f_max(0)
            for h in range(FH):
                if h + 1 < FH:
                    f_max(h + 1)
                f_norm(h)
            wait("yfh_ready", 1)
            V.tensor_tensor(flat(YFL[:, :, :]), PS[:, 0:2, :].rearrange("p b n -> p (b n)"),
                            flat(plain(YFH[:, :, :])), ALU.subtract).then_inc(sem("yfl_ready"), 1)

            V.memset(MINV[:, :, :, :], 0.0)
            for half in range(2):
                V.memset(inv[half]["P0"][:, :, :], 0.0)
                ins = V.memset(inv[half]["NO"][:, :, :], 0.0)
            link(ins)

            for c in range(NCH):
                for h2 in range(2):
                    wait("sc_mm", 2 * c + h2 + 1)
                    last = V.tensor_tensor(PK[:, c, h2, :, :], PS[:, 2 * c + h2, :].rearrange("p (q n) -> p q n", n=P),
                                           mask_r[:, :].unsqueeze(1).broadcast_to([P, NPAIR, P]), ALU.mult)
            link(last)
            for h2 in range(2):
                rows = slice(64 * h2, 64 * h2 + 64)
                V.memset(part(BK[rows], h2), 0.0)
                last = V.tensor_copy(part(BK[rows], 1 - h2), chunked(SH[rows, 8:12, :]))
            last.then_inc(sem("vp_ready"), 1)
            wait("uv_mm", 1)

            for half in range(2):
                I = inv[half]
                blocks = [(c, slice(NPAIR * c, NPAIR * c + NPAIR), h2, slice(64 * h2, 64 * h2 + 64))
                          for c in range(2) for h2 in range(2)]
                A_ = lambda c, h2, r: PK[r, 2 * half + c, h2, :, 0:64]
                for c, q, h2, r in blocks:
                    diag = blk16[r, :].unsqueeze(1).broadcast_to([64, NPAIR, 64])
                    ins = V.scalar_tensor_tensor(I["P0"][r, q, r], A_(c, h2, r), -1.0, diag, ALU.mult, ALU.mult)
                link(ins)
                for c, q, h2, r in blocks:
                    V.scalar_tensor_tensor(I["NO"][r, q, r], A_(c, h2, r), -1.0, I["P0"][r, q, r], ALU.mult,
                                           ALU.subtract)
                for c, q, h2, r in blocks:
                    eye = ident[r, r].unsqueeze(1).broadcast_to([64, NPAIR, 64])
                    last = V.tensor_tensor(I["X"][r, q, r], I["P0"][r, q, r], eye, ALU.add)
                last.then_inc(sem("inv_in"), 1)
            wait("inv_in", 2)
            for k, (_, _, dst, adds, _) in enumerate(INVERSE):
                if not adds:
                    continue
                for half in range(2):
                    wait(f"inv_mm{half}", k + 1)
                    b = 4 * half + 2 * (k % 2)
                    X = inv[half]["X"].rearrange("p u n -> p (u n)")
                    wait(f"inv_added{half}", evacuated(k - 1, True))
                    V.tensor_tensor(X, X, PS[:, b:b + 2, :].rearrange("p b n -> p (b n)"), ALU.add).then_inc(
                        sem(f"inv_added{half}"), 1)

            for c in range(NCH):
                wait("z_mm", c + 1)
                V.tensor_scalar(ZS[:, :, :].rearrange("p q n -> p (q n)"), PS[:, 0, 0:S], -1.0, None, ALU.mult).then_inc(sem("zs_ready"), 1)
                wait("su_mm", c + 1)
                src = PS[:, 3, :].rearrange("p (q n) -> p q n", n=P)
                if c:
                    link(V.tensor_tensor(S2T[:, :, :], S2[:, :, :], src, ALU.add))
                    src = S2T[:, :, :]
                    wait("y_mm", c + 1)
                for q in range(NPAIR):
                    last = V.scalar_tensor_tensor(S2[:, q, :], src[:, q, :], GL[:, q, c:c + 1], blk_ones[:, :],
                                                  ALU.mult, ALU.mult)
                last.then_inc(sem("s_ready"), 1)
                wait("s_ready", c + 1)
                if c % 2:
                    g = c // 2
                    used(FIRST["p_fox"] + c)
                    k = slice(g * 512, (g + 1) * 512)
                    for t in range(NT):
                        last = V.tensor_tensor(FY[:, t, k], PS[:, 4 + 2 * g + t, :], SG[:, t, k], ALU.mult)
                    last.then_inc(sem("pf_out"), 1)

            two = lambda x, b: flat(x[:, 2 * b:2 * b + 2, :])
            for b in range(2):
                wait("gn_mm", b + 1)
                link(V.scalar_tensor_tensor(two(YC, b), PS[:, 4 + b, :], -1.0 / RN, two(YT, b), ALU.mult, ALU.add))
                V.tensor_tensor(two(T[0], b), two(YC, b), two(YC, b), ALU.mult).then_inc(sem("ysq_ready"), 1)
            for b in range(2):
                wait("rstd_ready", b + 1)
                link(V.tensor_tensor(two(YC, b), two(YC, b), two(T[2], b), ALU.mult))
                for c in (2 * b, 2 * b + 1):
                    ins = V.scalar_tensor_tensor(YC[:, c, :], YC[:, c, :], col("ln_g", c), BON[:, c, :], ALU.mult,
                                                 ALU.add)
                link(ins)
                V.tensor_tensor(two(YC, b), two(YC, b), two(GG, b), ALU.mult).then_inc(sem("yr_ready"), 1)
            for b in range(2):
                wait("yrh_ready", b + 1)
                V.tensor_tensor(two(YRL, b), two(YC, b), two(plain(YRH), b), ALU.subtract).then_inc(
                    sem("yrl_ready"), 1)

            wait("pf_out", 2)
            for g in range(2):
                wait("xs_ready", 8 + g)
                used(FIRST["p_rwkv"] + 2 * g + 1)
                k = slice(g * 512, (g + 1) * 512)
                for t in range(NT):
                    ins = V.tensor_tensor(flat(T[3][:, 2 * t:2 * t + 2, :]), PS[:, 2 * g + t, :],
                                          SG[:, t, D + g * 512:D + (g + 1) * 512], ALU.mult)
                link(ins)
                for t in range(NT):
                    last = V.tensor_tensor(XS[:, t, k], FY[:, t, k], flat(T[3][:, 2 * t:2 * t + 2, :]), ALU.add)
                last.then_inc(sem("xs_ready"), 1)
            low_half(T_MERGED, None)
            add_to_h(FIRST["w_o"], 4, DN_ALPHA).then_inc(sem("h_ready"), 1)

            def layer_norm(k, gain, shift, landed, root_val, ready):
                for t in range(NT):
                    wait("sum_ready", 2 * k + t + 1)
                    m = ST[:, 80 + 2 * k + t:81 + 2 * k + t]
                    link(V.tensor_scalar(m, m, 1.0 / D, None, ALU.mult))
                    V.tensor_scalar(H[:, t, :], H[:, t, :], m, None, ALU.subtract).then_inc(sem("xc_ready"), 1)
                wait("var_ready", 2 * k + 2)
                r = ST[:, 96 + 2 * k:98 + 2 * k]
                mean_eps(r, ST[:, 88 + 2 * k:90 + 2 * k], 1.0 / D, LN_EPS)
                wait("sq_ready", root_val)
                link(V.reciprocal(r, r))
                wait(landed, 32)
                for t in range(NT):
                    link(V.scalar_tensor_tensor(H[:, t, :], H[:, t, :], r[:, t:t + 1], gain[:, :], ALU.mult, ALU.mult))
                    ins = V.tensor_tensor(H[:, t, :], H[:, t, :], shift[:, :], ALU.add)
                    if ready == "y_ready" or t == NT - 1:
                        ins.then_inc(sem(ready), 1)

            layer_norm(0, LG1, LB1, "ln1_landed", 7, "h_ready")
            low_half(T_X2, None)

            for m in range(LISTS):
                wait("qh_ready", m + 1)
                V.tensor_tensor(QL[:, m, :], PS[:, 4 + m % 4, 0:S], plain(QH[:, m, :]), ALU.subtract).then_inc(
                    sem("ql_ready"), 1)

            wait("u_bank_free", NT)
            for t in range(NT):
                def best(values, top, index, lists, n):
                    for r in range(2):
                        for l in range(lists):
                            ins = V.max(top(l)[:, 8 * r:8 * r + 8], values(l))
                        link(ins)
                        for l in range(lists):
                            ins = V.max_index(index(l)[:, 8 * r:8 * r + 8], top(l)[:, 8 * r:8 * r + 8], values(l))
                        link(ins)
                        if r == 0:
                            for l in range(lists):
                                ins = V.match_replace(values(l), top(l)[:, 0:8], values(l), -3.0e38)
                            link(ins)

                best(lambda l: SC[:, t, l, :], lambda l: tv[:, l, :], lambda l: ti[:, l, :], LISTS, NK)
                V.tensor_copy(tif[:, :, :], ti[:, :, :])
                pair = tv[:, :, :].rearrange("p (h two) k -> p h two k", two=2)
                shape = [P, PH, TOPK, TOPK]
                link(V.tensor_tensor(cand[:, :, :, :], pair[:, :, 0, :].unsqueeze(3).broadcast_to(shape),
                                     pair[:, :, 1, :].unsqueeze(2).broadcast_to(shape), ALU.add))
                best(lambda l: cand[:, l, :, :].rearrange("p a b -> p (a b)"), lambda l: bv[:, t, l, :],
                     lambda l: bp[:, l, :], PH, TOPK * TOPK)
                V.tensor_scalar(bai[:, :, :], bp[:, :, :], 4, None, ALU.logical_shift_right)
                link(V.tensor_scalar(bbi[:, :, :], bp[:, :, :], TOPK - 1, None, ALU.bitwise_and))
                V.tensor_copy(baf[:, :, :], bai[:, :, :])
                link(V.tensor_copy(bbf[:, :, :], bbi[:, :, :]))
                keys = tif[:, :, :].rearrange("p (h two) k -> p h two k", two=2)
                for which, place in ((0, baf), (1, bbf)):
                    flat3 = tmp1[:, :, :, :].rearrange("p h k a -> p (h k) a")
                    link(V.tensor_tensor(flat3, iota_f[:, 0:TOPK].unsqueeze(1).broadcast_to([P, P, TOPK]),
                                         place[:, :, :].rearrange("p h k -> p (h k)").unsqueeze(2).broadcast_to(
                                             [P, P, TOPK]), ALU.is_equal))
                    link(V.tensor_tensor(tmp1[:, :, :, :], tmp1[:, :, :, :],
                                         keys[:, :, which, :].unsqueeze(2).broadcast_to(shape), ALU.mult))
                    link(V.tensor_reduce(ijg[:, t, which, :], flat3, AX_X, ALU.add))
                last = V.tensor_tensor(be[:, t], bv[:, t], bv[:, t, :, 0:1].broadcast_to([P, PH, TOPK]), ALU.subtract)
            last.then_inc(sem("bv_ready"), 1)
            wait("bexp_ready", 1)
            both = be[:, :, :, :].rearrange("p t h k -> p (t h) k")
            link(V.tensor_reduce(ST[:, 112:128], both, AX_X, ALU.add))
            link(V.reciprocal(ST[:, 112:128], ST[:, 112:128]))
            for t in range(NT):
                last = V.tensor_tensor(ijg[:, t, 2, :].rearrange("p (h k) -> p h k", h=PH), be[:, t],
                                       ST[:, 112 + 8 * t:120 + 8 * t].unsqueeze(2).broadcast_to([P, PH, TOPK]),
                                       ALU.mult)
            last.then_inc(sem("ijg_ready"), 1)

            wait("ijgT_ready", 1)

            def at_token(x, t):
                return x[:, t:t + 1] if isinstance(t, int) else x[:, bass.ds(t, 1)]

            def one_hots(phase, i, c, first=False):
                half = iota_f[:, phase * (NK // 2):(phase + 1) * (NK // 2)]
                for g in range(2):
                    if not first:
                        dve.wait_ge(sem("gates_mm2"), 8 * i + (2 * c + g - 1 + phase * (S // 2)))
                    for a in range(2):
                        t = 16 * i + (4 * c + 2 * g + a)
                        V.tensor_scalar(hot_i[:, g, a, :], iota_f[:, :], at_token(IT, t), None, ALU.is_equal)
                        last = V.tensor_scalar(hot_j[:, g, a, :], half, at_token(JT, t), at_token(GT, t), ALU.is_equal,
                                               ALU.mult)
                    last.then_inc(sem("hot_ready"), 1)

            def gate(phase, i, b):
                dve.wait_ge(sem("gates_mm2"), 8 * i + (4 * b + 4 + phase * (S // 2)))
                t = 16 * i + 8 * b
                tokens = slice(t, t + 8) if isinstance(t, int) else bass.ds(t, 8)
                hs = HS[:, phase * (NK // 2):(phase + 1) * (NK // 2), tokens]
                V.tensor_tensor(hs, hs, PS[:, 4 + b, :].rearrange("p (a j) -> p j a", a=8), ALU.mult).then_inc(
                    sem("gated"), 1)

            def c_low(j, c):
                dve.wait_ge(sem("ch_ready"), j + 1)
                hs = HS[:, j, :] if isinstance(j, int) else HS[:, bass.ds(j, 1), :].rearrange("p a s -> p (a s)")
                V.tensor_tensor(CL[:, c, :], hs, plain(CH[:, c, :]), ALU.subtract).then_inc(sem("cl_ready"), 1)

            wait("u_bank_free", NT + NK // 4)
            for c in range(4):
                one_hots(0, 0, c, first=(c == 0))
                if c % 2:
                    gate(0, 0, c // 2)
            with dve.Fori(1, S // 16) as i:
                for c in range(4):
                    one_hots(0, i, c)
                    if c % 2:
                        gate(0, i, c // 2)
            wait("u_bank_free", NT + NK // 2)
            for c in range(4):
                c_low(c, c)
            with dve.Fori(0, S // 16 - 1) as i:
                for c in range(4):
                    one_hots(1, i, c)
                    if c % 2:
                        gate(1, i, c // 2)
                    c_low(4 * i + RING + c, c)
            for c in range(4):
                one_hots(1, S // 16 - 1, c)
                if c % 2:
                    gate(1, S // 16 - 1, c // 2)
            with dve.Fori(S // 16, NK // 4) as i:
                for c in range(4):
                    c_low(4 * i + c, c)
            used(N_ITEMS - 1)
            for t in range(NT):
                last = V.scalar_tensor_tensor(H[:, t, :], H[:, t, :], DN_ALPHA,
                                              PS[:, 2 * t:2 * t + 2, :].rearrange("p b n -> p (b n)"), ALU.mult, ALU.add)
            last.then_inc(sem("h_ready"), 1)
            layer_norm(1, LG2, LB2, "ln2_landed", 8, "y_ready")


def kernel(**inputs):
    import numpy as np
    import concourse.bacc as bacc
    from concourse.bass_utils import run_bass_kernel_spmd

    a = {k: np.asarray(v) for k, v in inputs.items()}

    def form_a(w):
        k, n = w.shape
        return w.reshape(k // 256, 2, P, n // 512, 512).transpose(3, 0, 2, 1, 4).reshape(-1, P, D)

    def form_b(w):
        return w.reshape(KC, P, -1, P).transpose(2, 1, 0, 3).reshape(-1, P, D)

    w1 = a["mlstm_w_in"][0]
    w2 = a["w_in_2"][0]
    fox = 3 * FH * FD + FH
    rw = fox + RW_CHUNKS * P
    parts = {
        "qk": form_b(w1[:, :1024]),
        "v": form_a(w1[:, 1024:2048]),
        "o": form_a(w1[:, 2048:3072]),
        "mix_out": form_a(a["mlstm_w_out"][0]),
        "w1": form_b(a["mlp_w1"][0]),
        "w2": form_a(a["mlp_w2"][0]),
        "ple_gate": form_a(a["ple_gate_w"][0]),
        "ple": form_a(a["ple_w"][0]),
        "rwkv": form_b(w2[:, fox:rw]),
        "fox_qk": form_b(w2[:, :1024]),
        "fox_v": form_a(w2[:, 1024:1536]),
        "gates": form_a(w2[:, rw:]),
        "p_fox": form_a(a["p_fox_2"][0]),
        "p_rwkv": form_a(a["p_rwkv_2"][0]),
        "w_o": form_a(a["w_o_2"][0]),
        "peer_q": form_b(a["peer_w_q_2"][0]),
        "keys": a["peer_sub_keys_2"][0].reshape(2, PH, NK, P).transpose(0, 3, 1, 2).reshape(2, P, D),
        "u": a["peer_u_2"][0].reshape(NK, NK, KC, P).transpose(1, 3, 2, 0).reshape(NK, P, D),
        "v_table": a["peer_v_2"][0].reshape(NK, NK, D).transpose(1, 0, 2),
    }
    for name, n in COUNTS:
        assert parts[name].shape == (n, P, D), name
    vectors = [a["norm_mix"], a["norm_mlp"], a["norm_ple"], a["mlstm_head_norm"], a["rwkv_mu_2"], a["rwkv_w0_2"],
               a["rwkv_a0_2"], a["rwkv_k_k_2"], a["rwkv_k_a_2"], a["rwkv_r_k_2"], a["rwkv_ln_g_2"], a["rwkv_ln_b_2"]]
    columns = lambda w: w.reshape(KC, P, -1).transpose(1, 0, 2)
    arrays = {
        "weights": np.concatenate([parts[name] for name, _ in COUNTS]),
        "x": a["x"][0],
        "p": a["p"][0, 0],
        "vectors": np.concatenate([v[0].reshape(-1, P).T for v in vectors], axis=1),
        "rows": np.stack([a["norm_final"], a["ple_gate_b"][0], a["ln1_g_2"][0], a["ln1_b_2"][0], a["ln2_g_2"][0],
                          a["ln2_b_2"][0]]),
        "gate_weights": np.concatenate([columns(w1[:, 3072:]), columns(w2[:, 1536:fox])], axis=2),
        "low_rank": np.stack([np.concatenate([a["rwkv_w2_2"][0], a["rwkv_a2_2"][0]]), a["rwkv_g2_2"][0]], axis=1),
        "gate_bias": a["mlstm_b_gates"][0].T,
        "fox_bias": a["fox_f_bias_2"][0].reshape(FH, 1),
    }
    arrays = {k: np.ascontiguousarray(v) for k, v in arrays.items()}
    nc = bacc.Bacc("TRN2", target_bir_lowering=False, num_devices=1)
    args = [nc.dram_tensor(k, v.shape, mybir.dt.from_np(v.dtype), kind="ExternalInput").ap() for k, v in arrays.items()]
    out = nc.dram_tensor("y", (S, D), F32, kind="ExternalOutput").ap()
    bass_blocks(nc, *args, out)
    r = run_bass_kernel_spmd(nc, [arrays], core_ids=[0])
    return r.results[0]["y"].reshape(1, S, D)
```

```python
from contextlib import ExitStack

import concourse.bass as bass
from concourse import mybir

ALU = mybir.AluOpType
ACT = mybir.ActivationFunctionType
F32 = mybir.dt.float32
F32R = mybir.dt.float32r
BF16 = mybir.dt.bfloat16
U32 = mybir.dt.uint32
AX_X = mybir.AxisListType.X

P = 128
S = 256
NT = S // P
D = 1024
KC = D // P
EPS = 1e-6
LN_EPS = 1e-5
GN_EPS = 64e-5
DN_ALPHA = 2.0 ** 0.25

MH, MDK, MDV = 4, 128, 256
FH, FD = 8, 64
RH, RN = 8, 64
CH_T = 64
NCH = S // CH_T
NPAIR = RH // 2
RW_CHUNKS = (3 * RH * RN + 64 + 64 + 128) // P
DECAY = 0.6065306597126334
NEG = -1.0e30
BLK = 16
PH, NK, TOPK = 8, 128, 16
LISTS = 2 * PH
IJG_AT = NK // 8 - 2

COUNTS = [
    ("qk", 8), ("v", 8), ("o", 8), ("mix_out", 8), ("w1", 32), ("w2", 32), ("ple_gate", 8), ("ple", 2),
    ("rwkv", RW_CHUNKS), ("fox_qk", 8), ("fox_v", 4), ("gates", 16), ("p_fox", 4), ("p_rwkv", 4), ("w_o", 8),
    ("peer_q", 16), ("keys", 2), ("u", NK), ("v_table", NK),
]
FIRST = {}
_at = 0
for _name, _n in COUNTS:
    FIRST[_name] = _at
    _at += _n
N_ITEMS = _at
RING = 4

VEC = {}
_at = 0
for _name, _n in [("norm_mix", 8), ("norm_mlp", 8), ("norm_ple", 8), ("head_norm", 8), ("mu", RW_CHUNKS), ("w0", 4),
                  ("a0", 4), ("k_k", 4), ("k_a", 4), ("r_k", 4), ("ln_g", 4), ("ln_b", 4)]:
    VEC[_name] = _at
    _at += _n
N_VEC = _at

T_MIX, T_HEADS, T_MLP, T_PLE, T_X1, T_MERGED, T_X2 = range(7)

INVERSE = [
    ("P0", "I", "T0", False, -1),
    ("T0", "P0", "P1", False, 0), ("P0", "T0", "T1", False, 0),
    ("T1", "X", "X", True, 2), ("T1", "P1", "P0", False, 2),
    ("P1", "T1", "T0", False, 2), ("T0", "X", "X", True, 5),
    ("P0", "T0", "T1", False, 5), ("T1", "X", "X", True, 7),
    ("X", "I", "T0", False, 8),
    ("T0", "NO", "P0", False, 9), ("NO", "T0", "P1", False, 9),
    ("P0", "P1", "T1", False, 11), ("T1", "X", "X", True, 12),
    ("P1", "X", "X", True, 13),
]


def evacuated(upto, adds):
    return sum(r[3] == adds for r in INVERSE[:upto + 1])


def bass_blocks(nc, weights, x_in, p_in, vec_in, rows_in, gate_w_in, lora_in, mb_in, fb_in, out, rest_dram, x2_dram):
    with ExitStack() as ctx:
        base = 16512
        slab = ctx.enter_context(nc.sbuf_tensor("slab", [P, 53208], F32))

        def at(name, shape, dt, offset):
            return nc.alloc_sbuf_tensor_at(name, shape, dt, offset=base + offset)

        H = at("H", [P, NT, D], F32, 0)
        XH = at("XH", [P, KC, S], F32R, 8192)
        XL = at("XL", [P, KC, S], F32R, 16384)
        RAW = at("RAW", [P, RING, D], F32, 24576)
        WH = at("WH", [P, RING, D], F32R, 40960)
        WL = at("WL", [P, RING, D], F32R, 57344)
        C0 = 73728
        iota_f = at("iota_f", [P, P], F32, C0)
        ST = at("ST", [P, P], F32, C0 + 512)
        ident = at("ident", [P, P], F32, C0 + 1024)
        vec = at("vec", [P, N_VEC], F32, C0 + 1536)
        ones_row = at("ones_row", [1, P], F32, C0 + 1856)
        IT = at("IT", [P, S], F32, C0 + 4160)
        JT = at("JT", [P, S], F32, C0 + 5184)
        GT = at("GT", [P, S], F32, C0 + 6208)
        fbias = at("fbias", [FH, 1], F32, C0 + 7232)
        mbias = at("mbias", [MH, 4], F32, C0 + 7264)
        eps_c = at("eps_c", [P, 4], F32, C0 + 7296)
        A0 = 81664
        M0 = A0 + 114688
        mask_m = at("mask_m", [P, 2, 2, S], F32, M0)
        fpt = at("fpt", [P, 2, 384], F32, M0)
        mask_f = at("mask_f", [P, S], F32, M0 + 4096)
        mask_r = at("mask_r", [P, P], F32, M0 + 5120)
        blk_ones = at("blk_ones", [P, P], F32, M0 + 5632)
        blk16 = at("blk16", [P, 64], F32, M0 + 6144)
        resets = at("resets", [P, D], BF16, M0 + 6400)
        sel4 = at("sel4", [MH, MH, P], F32, M0 + 8448)
        sel8 = at("sel8", [FH, FH, P], F32, M0 + 10496)
        XS = at("XS", [P, NT, D], F32, A0)
        LNS = at("LNS", [P, NT, D], F32, A0 + 8192)
        qkT = at("qkT", [P, 2 * MH, S], F32, A0 + 8192)
        v1 = at("v1", [P, NT, MH, MDV + 1], F32, A0 + 16384)
        og = at("og", [P, NT, D], F32, A0 + 24640)
        hacc = at("hacc", [P, NT, D], F32, A0 + 32832)
        WE = at("WE", [P, 2, 2, S], F32, A0 + 41024)
        SM = at("SM", [P, 2, 2, S], F32, A0 + 45120)
        GR = at("GR", [MH, 4, S], F32, A0 + 49216)
        GA = at("GA", [MH, 8, S], F32, A0 + 53312)
        AT = at("AT", [P, 8, MH], F32, A0 + 61504)
        grow = at("grow", [16, S], F32, A0 + 64512)
        GWH = at("GWH", [P, KC, 24], F32R, A0 + 62208)
        GWL = at("GWL", [P, KC, 24], F32R, A0 + 62976)
        gw = at("gw", [P, KC, 24], F32, A0 + 63744)
        ZH = at("ZH", [P, 32, S], F32R, A0 + 8192)
        ZL = at("ZL", [P, 32, S], F32R, A0 + 40960)
        RT = at("RT", [P, 4, S], F32, A0 + 73728)
        ZF = at("ZF", [P, 4, S], F32, A0 + 77824)
        P2 = at("P2", [P, NT, S], F32, A0 + 81920)
        PTH = at("PTH", [P, 2, S], F32R, A0 + 83968)
        PTL = at("PTL", [P, 2, S], F32R, A0 + 86016)
        SGP = at("SGP", [P, NT, D], F32, A0 + 88064)
        brow = at("brow", [1, D], F32, A0 + 96256)
        nfin = at("nfin", [P, D], F32, A0 + 100352)
        FWH = at("FWH", [P, KC, 8], F32R, A0 + 104448)
        FWL = at("FWL", [P, KC, 8], F32R, A0 + 104704)
        SG = at("SG", [P, NT, 2 * D], F32, A0 + 8192)
        YFH = at("YFH", [P, 4, S], F32R, A0 + 24576)
        YFL = at("YFL", [P, 4, S], F32R, A0 + 28672)
        YRH = at("YRH", [P, 4, S], F32R, A0 + 32768)
        YRL = at("YRL", [P, 4, S], F32R, A0 + 36864)
        fqk = at("fqk", [P, 8, S], F32, A0)
        fv = at("fv", [P, NT, 512], F32, A0 + 32768)
        fp = at("fp", [P, 2, 384], F32, A0 + 36864)
        fr = at("fr", [FH, 3, S], F32, C0 + 4160)
        lora = at("lora", [P, 2, 512], F32, A0 + 24576)
        BK = at("BK", [P, NPAIR, NCH, 2, CH_T], F32, A0 + 40960)
        CR = at("CR", [P, NPAIR, NCH, 2, CH_T], F32, A0 + 49152)
        PK = at("PK", [P, NCH, 2, NPAIR, P], F32, A0 + 57344)
        BKT = at("BKT", [P, NCH, NPAIR, P], F32, A0 + 73728)
        UV = at("UV", [P, NCH, NPAIR, P], F32, A0 + 81920)
        SH = at("SH", [P, RW_CHUNKS, S], F32, A0 + 90112)
        Z = at("Z", [P, RW_CHUNKS, S + 1], F32, A0 + 57344)
        T = [at(f"T{k}", [P, 4, S], F32, A0 + 57344 + 4096 * k) for k in range(8)]
        GG = at("GG", [P, 4, S], F32, A0 + 104448)
        BON = at("BON", [P, 4, S], F32, A0 + 108544)
        GL = at("GL", [P, NPAIR, NCH], F32, C0 + 7328)
        LT = at("LT", [P, 2, S], F32, A0 + 112640)
        MINV = at("MINV", [P, NCH, NPAIR, P], F32, 8192)
        INV_AT = [{"T0": A0, "P0": 16384, "P1": A0 + 4096, "T1": A0 + 32768, "NO": A0 + 90112},
                  {"T0": A0 + 40960, "P0": 20480, "P1": A0 + 45056, "T1": A0 + 36864, "NO": A0 + 94208}]
        inv = [{k: at(f"inv_{k}_{half}", [P, 8, P], F32, v) for k, v in INV_AT[half].items()} for half in range(2)]
        for half in range(2):
            inv[half]["X"] = MINV[:, 2 * half:2 * half + 2, :, :].rearrange("p c q n -> p (c q) n")
        VZ = at("VZ", [P, NPAIR, NCH, 2, CH_T], F32, A0 + 90112)
        ZS = at("ZS", [P, NPAIR, RN], F32, A0 + 45056)
        S2 = at("S2", [P, NPAIR, P], F32, A0 + 47104)
        YT = at("YT", [P, 4, S], F32, A0 + 90112)
        YC = at("YC", [P, 4, S], F32, A0 + 94208)
        S2T = at("S2T", [P, NPAIR, P], F32, A0 + 102400)
        LG1 = at("LG1", [P, D], F32, A0 + 24576)
        LB1 = at("LB1", [P, D], F32, A0 + 28672)
        HS = at("HS", [P, NK, S], F32, A0)
        R0 = A0 + 65536
        QH = at("QH", [P, LISTS, S], F32R, R0)
        QL = at("QL", [P, LISTS, S], F32R, R0 + 16384)
        SC = at("SC", [P, NT, LISTS, NK], F32, R0 + 32768)
        cand = at("cand", [P, PH, TOPK, TOPK], F32, R0 + 49152)
        tmp1 = at("tmp1", [P, PH, TOPK, TOPK], F32, R0 + 57344)
        tv = at("tv", [P, LISTS, TOPK], F32, R0)
        ti = at("ti", [P, LISTS, TOPK], U32, R0 + 1024)
        tif = at("tif", [P, LISTS, TOPK], F32, R0 + 2048)
        bv = at("bv", [P, NT, PH, TOPK], F32, R0 + 9216)
        be = at("be", [P, NT, PH, TOPK], F32, R0 + 10240)
        bp = at("bp", [P, PH, TOPK], U32, R0 + 3584)
        bai = at("bai", [P, PH, TOPK], U32, R0 + 4096)
        bbi = at("bbi", [P, PH, TOPK], U32, R0 + 4608)
        baf = at("baf", [P, PH, TOPK], F32, R0 + 5120)
        bbf = at("bbf", [P, PH, TOPK], F32, R0 + 5632)
        ijg = at("ijg", [P, NT, 3, P], F32, R0 + 6144)
        DG = at("DG", [P, NT, P], F32, C0 + 2560)
        hot_i = at("hot_i", [P, 2, 2, P], F32, C0 + 1024)
        hot_j = at("hot_j", [P, 2, 2, NK], F32, 0)
        stage = at("stage", [P, 2, NK // 2, 8], F32, 2048)
        CH = at("CH", [P, RING, S], F32R, 8192)
        CL = at("CL", [P, RING, S], F32R, 12288)
        LG2 = at("LG2", [P, D], F32, 16384)
        LB2 = at("LB2", [P, D], F32, 20480)

        PS = ctx.enter_context(nc.psum_tensor("PS", [P, 8, 512], F32))

        sems = {}

        def sem(name):
            if name not in sems:
                sems[name] = ctx.enter_context(nc.semaphore(name))
            return sems[name]

        w_landed = [sem(f"w_landed{i}") for i in range(RING)]
        w_hi, w_lo, w_used = sem("w_hi"), sem("w_lo"), sem("w_used")

        def col(name, c):
            k = VEC[name] + c
            return vec[:, k:k + 1]

        def plain(ap):
            return ap.bitcast(F32)

        block = ctx.enter_context(nc.Block())

        @block.sync
        def _(sp):
            sp.dma_start(H[:, :, :], x_in.rearrange("(t p) d -> p t d", p=P)).then_inc(sem("x_landed"), 16)
            for n in range(RING):
                sp.dma_start(RAW[:, n, :], weights[n]).then_inc(w_landed[n], 16)
            full = (N_ITEMS // RING) * RING
            with sp.Fori(1, N_ITEMS // RING) as i:
                for slot in range(RING):
                    n = i * RING
                    sp.wait_ge(w_lo, n + (slot + 1 - RING))
                    sp.dma_start(RAW[:, slot, :], weights[bass.ds(n + slot, 1)].rearrange("a p d -> p (a d)")).then_inc(w_landed[slot], 16)
            for n in range(full, N_ITEMS):
                sp.wait_ge(w_lo, n + 1 - RING)
                sp.dma_start(RAW[:, n % RING, :], weights[n]).then_inc(w_landed[n % RING], 16)
            for t in range(NT):
                sp.wait_ge(sem("y_ready"), t + 1)
                sp.dma_start(out[t * P:(t + 1) * P, :], H[:, t, :]).then_inc(sem("y_stored"), 16)
            sp.wait_ge(sem("y_stored"), 16 * NT)

        @block.gpsimd
        def _(pool):
            made = sem("pool_made")
            count = [0]

            def link(ins):
                count[0] += 1
                ins.then_inc(made, 1)
                pool.wait_ge(made, count[0])

            def keep(view, pattern, base, cm, op, fill=0.0):
                link(nc.gpsimd.affine_select(out=view, in_=view, compare_op=op, fill=fill, base=base,
                                             pattern=pattern, channel_multiplier=cm))

            link(nc.gpsimd.memset(ident[:, :], 1.0))
            keep(ident[:, :], [[-1, P]], 0, 1, ALU.is_equal)
            nc.gpsimd.memset(ones_row[:, :], 1.0).then_inc(sem("ident_ready"), 1)
            link(nc.gpsimd.memset(sel4[:, :, :], 1.0))
            keep(sel4[:, :, :], [[-1, MH], [0, P]], 0, 1, ALU.is_equal)
            link(nc.gpsimd.memset(sel8[:, :, :], 1.0))
            keep(sel8[:, :, :], [[-1, FH], [0, P]], 0, 1, ALU.is_equal)
            link(nc.gpsimd.memset(mask_m[:, :, :, :], 1.0))
            for sb in range(NT):
                keep(mask_m[:, 0, sb, :], [[1, S]], -sb * P, -1, ALU.is_ge)
                keep(mask_m[:, 1, sb, :], [[-1, S]], sb * P, 1, ALU.is_ge)
            link(nc.gpsimd.memset(mask_f[:, :], 0.0))
            keep(mask_f[:, :], [[-1, S]], P, 1, ALU.is_ge, NEG)
            link(nc.gpsimd.memset(mask_r[:, :], 1.0))
            for half in range(2):
                v = mask_r[64 * half:64 * half + 64, :]
                keep(v[:, 0:64], [[1, 64]], -1, -1, ALU.is_ge)
                keep(v[:, 64:128], [[1, 64]], 0, -1, ALU.is_ge)
            link(nc.gpsimd.memset(blk_ones[:, :], 0.0))
            link(nc.gpsimd.memset(blk_ones[0:64, 0:64], 1.0))
            link(nc.gpsimd.memset(blk_ones[64:128, 64:128], 1.0))
            link(nc.gpsimd.memset(blk16[:, :], 1.0))
            for half in range(2):
                v = blk16[64 * half:64 * half + 64, :]
                keep(v, [[-BLK, 64 // BLK], [0, BLK]], 0, 1, ALU.is_ge)
                keep(v, [[BLK, 64 // BLK], [0, BLK]], BLK - 1, -1, ALU.is_ge)
            link(nc.gpsimd.memset(resets[:, :], 1.0))
            link(nc.gpsimd.memset(resets[:, :].rearrange("p (c t) -> p c t", t=CH_T)[:, :, 0:1], 0.0))
            link(nc.gpsimd.iota(iota_f[:, :], [[1, P]], base=0, channel_multiplier=0,
                                allow_small_or_imprecise_dtypes=True))
            link(nc.gpsimd.memset(eps_c[:, 1:2], GN_EPS))
            nc.gpsimd.memset(eps_c[:, 0:1], 1.0).then_inc(sem("consts_ready"), 1)

            def split_low(n, slot):
                pool.wait_ge(w_hi, n + 1)
                nc.gpsimd.tensor_tensor(WL[:, slot, :], RAW[:, slot, :], plain(WH[:, slot, :]),
                                        ALU.subtract).then_inc(w_lo, 1)

            full = (N_ITEMS // RING) * RING
            with pool.Fori(0, N_ITEMS // RING) as i:
                for slot in range(RING):
                    split_low(i * RING + slot, slot)
            for n in range(full, N_ITEMS):
                split_low(n, n % RING)

        @block.scalar
        def _(act):
            A = nc.scalar.activation
            feed_at = [0]

            def split_high(n, slot, used=None):
                act.wait_ge(w_landed[slot], landed_value(n))
                if used is not None:
                    act.wait_ge(w_used, used)
                nc.scalar.copy(WH[:, slot, :], RAW[:, slot, :]).then_inc(w_hi, 1)

            def landed_value(n):
                return 16 * (n // RING + 1)

            def feed(last):
                while feed_at[0] <= min(last + RING - 1, N_ITEMS - 1):
                    n = feed_at[0]
                    split_high(n, n % RING, n + 1 - RING if n >= RING else None)
                    feed_at[0] += 1

            def used(n):
                feed(n)
                act.wait_ge(w_used, n + 1)

            act.dma_start(vec[:, :], vec_in).then_inc(sem("vec_landed"), 16)
            act.dma_start(gw[:, :, :], gate_w_in).then_inc(sem("gw_landed"), 16)
            act.dma_start(mbias[:, :], mb_in).then_inc(sem("mb_landed"), 16)
            act.dma_start(fbias[:, :], fb_in).then_inc(sem("fb_landed"), 16)
            act.dma_start(P2[:, :, :], p_in.rearrange("(t p) d -> p t d", p=P)).then_inc(sem("p_landed"), 16)
            act.dma_start(brow[:, :], rows_in[1:2, :]).then_inc(sem("brow_landed"), 16)
            act.dma_start(nfin[:, :], rows_in[0:1, :].broadcast_to([P, D])).then_inc(sem("nfin_landed"), 16)

            def root(src, dst, msem):
                act.wait_ge(sem("ms_ready"), msem)
                A(dst, src, ACT.Sqrt).then_inc(sem("sq_ready"), 1)

            def sumsq(r, name, value):
                for g in range(2):
                    act.wait_ge(sem(name), value if name == "x_landed" else value + g)
                    for t in range(NT):
                        k = slice(g * 512, (g + 1) * 512)
                        at_ = 8 * g + 2 * r + t
                        last = A(XS[:, t, k], H[:, t, k], ACT.Square, accum_out=ST[:, at_:at_ + 1])
                    last.then_inc(sem("ss_ready"), 1)

            def evac_high(r, gain):
                for c in range(KC):
                    act.wait_ge(sem("tr_ready"), 4 * r + c // 2 + 1)
                    src = PS[:, 4 + c // 2, (c % 2) * S:(c % 2 + 1) * S]
                    A(XH[:, c, :], src, ACT.Copy, scale=col(gain, c) if gain else 1.0).then_inc(sem("xh_ready"), 1)

            sumsq(0, "x_landed", 16)
            root(ST[:, 16:18], ST[:, 16:18], 1)
            act.wait_ge(sem("gw_landed"), 16)
            nc.scalar.copy(GWH[:, :, :], gw[:, :, :])
            nc.scalar.copy(FWH[:, :, :], gw[:, :, 16:24]).then_inc(sem("gwh_ready"), 1)
            feed(0)
            act.wait_ge(sem("vec_landed"), 16)
            evac_high(T_MIX, "norm_mix")

            f2 = GR[:, :, :].rearrange("h (d k) s -> h d k s", k=2)[:, :, 1, :]
            act.wait_ge(sem("gr_ready"), 1)
            A(GA[:, 2:4, :], f2, ACT.Abs).then_inc(sem("g_act"), 1)
            act.wait_ge(sem("g_act"), 1)
            A(GA[:, 2:4, :], GA[:, 2:4, :], ACT.Exp, scale=-1.0).then_inc(sem("g_act"), 1)
            act.wait_ge(sem("g_act"), 2)
            act.wait_ge(sem("consts_ready"), 1)
            A(GA[:, 2:4, :], GA[:, 2:4, :], ACT.Ln, bias=eps_c[0:MH, 0:1]).then_inc(sem("g_act"), 1)
            feed(FIRST["qk"] + 4)
            act.wait_ge(sem("m_ready"), 1)
            A(GA[:, 0:2, :], GA[:, 0:2, :], ACT.Exp, scale=-1.0).then_inc(sem("emt_ready"), 1)

            for g in range(2):
                used(FIRST["o"] + 4 * g + 3)
                for t in range(NT):
                    last = A(og[:, t, g * 512:(g + 1) * 512], PS[:, 2 * (g % 2) + t, :], ACT.Sigmoid)
                last.then_inc(sem("o_out"), 1)

            def head_squares(h):
                act.wait_ge(sem("fin_done"), 2 * h + 2)
                for t in range(NT):
                    A(XS[:, t, h * MDV:(h + 1) * MDV], hacc[:, t, h * MDV:(h + 1) * MDV], ACT.Square,
                      accum_out=ST[:, 24 + 4 * t + h:25 + 4 * t + h]).then_inc(sem("hss_ready"), 1)

            act.wait_ge(sem("at_ready_m"), 1)
            for e in range(2 * MH):
                h, d = e // 2, e % 2
                act.wait_ge(sem("mb_mm"), h + 1)
                if e >= 2:
                    act.wait_ge(sem("p_ready"), e - 1)
                for sb in range(NT):
                    last = A(WE[:, e % 2, sb, :], PS[:, 6 + h % 2, d * S:(d + 1) * S], ACT.Relu,
                             bias=AT[:, 2 * d + sb, h:h + 1])
                last.then_inc(sem("w_ready"), 1)
                act.wait_ge(sem("w_ready"), e + 1)
                A(WE[:, e % 2], WE[:, e % 2], ACT.Exp, scale=-1.0).then_inc(sem("e_ready"), 1)
                if e >= 3 and e % 2:
                    head_squares((e - 3) // 2)
            head_squares(MH - 1)
            root(ST[:, 32:40], ST[:, 32:40], 2)
            evac_high(T_HEADS, "head_norm")

            feed(FIRST["mix_out"] + 7)
            sumsq(1, "h_half", 1)
            root(ST[:, 18:20], ST[:, 18:20], 3)
            evac_high(T_MLP, "norm_mlp")

            def z_high(m):
                act.wait_ge(sem("zf_ready"), m + 1)
                nc.scalar.copy(ZH[:, m, :], ZF[:, m % 4, :]).then_inc(sem("zh_ready"), 1)

            for m in range(32):
                used(FIRST["w1"] + m)
                if m >= 4:
                    act.wait_ge(sem("zf_ready"), m - 3)
                A(RT[:, m % 4, :], PS[:, 4 + m % 4, 0:S], ACT.Relu).then_inc(sem("relu_ready"), 1)
                if m >= 1:
                    z_high(m - 1)
            z_high(31)

            feed(FIRST["w2"] + 31)
            sumsq(2, "h_half", 3)
            root(ST[:, 20:22], ST[:, 20:22], 4)
            evac_high(T_PLE, "norm_ple")
            act.wait_ge(sem("ptr_ready"), 1)
            nc.scalar.copy(PTH[:, :, :], PS[:, 0, :].rearrange("p (c s) -> p c s", c=2)).then_inc(sem("pth_ready"), 1)
            for g in range(2):
                used(FIRST["ple_gate"] + 4 * g + 3)
                for t in range(NT):
                    last = A(SGP[:, t, g * 512:(g + 1) * 512], PS[:, 2 * (g % 2) + t, :], ACT.Sigmoid)
                last.then_inc(sem("sgp_out"), 1)

            feed(FIRST["ple"] + 1)
            sumsq(3, "h_half", 5)
            root(ST[:, 22:24], ST[:, 22:24], 5)
            act.dma_start(lora[:, :, :], lora_in).then_inc(sem("lora_landed"), 16)
            evac_high(T_X1, None)

            for m in range(RW_CHUNKS):
                used(FIRST["rwkv"] + m)
                if m == 0:
                    act.wait_ge(sem("z_zero"), 1)
                nc.scalar.copy(Z[:, m, 1:S + 1], PS[:, 4 + m % 4, 0:S]).then_inc(sem("b2_out"), 1)
            for m in range(8):
                used(FIRST["fox_qk"] + m)
                nc.scalar.copy(fqk[:, m, :], PS[:, 4 + (RW_CHUNKS + m) % 4, 0:S]).then_inc(sem("b2_out"), 1)
            act.wait_ge(sem("sh_ready"), RW_CHUNKS)
            A(LT[0:64, 0, :], SH[0:64, 12, :], ACT.Tanh)
            nc.scalar.copy(LT[64:128, 0, :], SH[64:128, 12, :])
            A(LT[:, 1, :], SH[:, 13, :], ACT.Sigmoid).then_inc(sem("lt_ready"), 1)
            feed(FIRST["fox_v"] + 3)
            act.wait_ge(sem("fr_ready"), 1)
            A(fr[:, 1, :], fr[:, 0, :], ACT.Abs).then_inc(sem("f_act"), 1)
            act.wait_ge(sem("f_act"), 1)
            A(fr[:, 1, :], fr[:, 1, :], ACT.Exp, scale=-1.0).then_inc(sem("f_act"), 1)
            act.wait_ge(sem("f_act"), 2)
            A(fr[:, 1, :], fr[:, 1, :], ACT.Ln, bias=eps_c[0:FH, 0:1]).then_inc(sem("f_act"), 1)
            act.wait_ge(sem("lora_mm"), 1)
            for c in range(4):
                last = A(T[4][:, c, :], PS[:, 4 + c // 2, (c % 2) * S:(c % 2 + 1) * S], ACT.Sigmoid, bias=col("w0", c))
            last.then_inc(sem("sigw_ready"), 1)
            for c in range(4):
                last = A(T[3][:, c, :], PS[:, 6 + c // 2, (c % 2) * S:(c % 2 + 1) * S], ACT.Sigmoid, bias=col("a0", c))
            last.then_inc(sem("aa_ready"), 1)
            act.wait_ge(sem("lora_mm"), 2)
            nc.scalar.copy(GG[:, :, :].rearrange("p c s -> p (c s)"), PS[:, 0:2, :].rearrange("p b n -> p (b n)")).then_inc(
                sem("gg_ready"), 1)
            feed(FIRST["gates"])
            act.wait_ge(sem("lg_ready"), 2)
            A(T[0][:, :, :], T[5][:, :, :], ACT.Exp, scale=-DECAY)
            A(T[1][:, :, :], T[5][:, :, :], ACT.Exp, scale=DECAY)
            A(T[2][:, :, :], T[2][:, :, :], ACT.Exp, scale=-DECAY).then_inc(sem("gdec_ready"), 1)

            def gate_out(g):
                used(FIRST["gates"] + 4 * g + 3)
                for t in range(NT):
                    last = A(SG[:, t, g * 512:(g + 1) * 512], PS[:, 2 * ((g + 1) % 2) + t, :], ACT.Sigmoid)
                last.then_inc(sem("gate_out"), 1)

            gate_out(0)
            root(T[7][:, :, :], T[7][:, :, :], 6)
            gate_out(1)
            gate_out(2)
            gate_out(3)

            def f_exp(h):
                act.wait_ge(sem("fmax_ready"), h + 1)
                s0 = 64 + 8 * (h % 2)
                A(fp[:, h % 2, 0:P], fp[:, h % 2, 0:P], ACT.Exp, bias=ST[:, s0 + 2:s0 + 3], scale=FD ** -0.5,
                  accum_out=ST[:, s0 + 4:s0 + 5])
                A(fp[:, h % 2, P:384], fp[:, h % 2, P:384], ACT.Exp, bias=ST[:, s0 + 3:s0 + 4], scale=FD ** -0.5,
                  accum_out=ST[:, s0 + 5:s0 + 6]).then_inc(sem("fexp_ready"), 1)

            def f_pt(h):
                act.wait_ge(sem("fpt_mm"), h + 1)
                if h >= 2:
                    act.wait_ge(sem("fo_mm"), h - 1)
                nc.scalar.copy(fpt[:, h % 2, :], PS[:, 6 + h % 2, 0:384]).then_inc(sem("fpt_ready"), 1)

            def by_token(n):
                act.wait_ge(sem("tok_mm"), n + 1)
                dst = UV[:, n] if n < NCH else BKT[:, n - NCH]
                nc.scalar.copy(dst.rearrange("p q n -> p (q n)"), PS[:, 2, :]).then_inc(sem("tok_ready"), 1)

            for h in range(FH + 1):
                if h < FH:
                    f_exp(h)
                if h >= 1:
                    f_pt(h - 1)
                    by_token(h - 1)
            act.wait_ge(sem("fo_mm"), FH)
            nc.scalar.copy(YFH[:, :, :].rearrange("p c s -> p (c s)"), PS[:, 0:2, :].rearrange("p b n -> p (b n)")).then_inc(
                sem("yfh_ready"), 1)

            for k, (_, _, dst, adds, _) in enumerate(INVERSE):
                if adds:
                    continue
                for half in range(2):
                    act.wait_ge(sem(f"inv_mm{half}"), k + 1)
                    b = 4 * (1 - half) + 2 * (k % 2)
                    nc.scalar.copy(inv[half][dst][:, :, :].rearrange("p u n -> p (u n)"),
                                   PS[:, b:b + 2, :].rearrange("p b n -> p (b n)")).then_inc(
                                       sem(f"inv_copied{half}"), 1)
            feed(FIRST["p_fox"])
            for c in range(NCH):
                act.wait_ge(sem("u_mm"), c + 1)
                for h2 in range(2):
                    rows = slice(64 * h2, 64 * h2 + 64)
                    last = nc.scalar.copy(UV[rows, c, :, rows], PS[rows, 1, 0:S].rearrange("p (q n) -> p q n", n=RN))
                last.then_inc(sem("u_ready"), 1)
                feed(FIRST["p_fox"] + c)
                act.wait_ge(sem("y_mm"), c + 1)
                nc.scalar.copy(YT[:, :, c * CH_T:(c + 1) * CH_T],
                               PS[:, 2, 0:S].rearrange("p (q t) -> p q t", q=NPAIR)).then_inc(sem("yt_ready"), 1)
            for b in range(2):
                act.wait_ge(sem("gn_mm"), 3 + b)
                var = T[2][:, 2 * b:2 * b + 2, :].rearrange("p c s -> p (c s)")
                A(var, PS[:, 6 + b, :], ACT.Ln, bias=eps_c[:, 1:2], scale=1.0 / RN).then_inc(sem("gn_act"), 1)
            act.wait_ge(sem("gn_act"), 2)
            for b in range(2):
                var = T[2][:, 2 * b:2 * b + 2, :]
                A(var, var, ACT.Exp, scale=-0.5).then_inc(sem("rstd_ready"), 1)
            for b in range(2):
                act.wait_ge(sem("yr_ready"), b + 1)
                nc.scalar.copy(YRH[:, 2 * b:2 * b + 2, :], YC[:, 2 * b:2 * b + 2, :]).then_inc(sem("yrh_ready"), 1)
            feed(FIRST["p_rwkv"] + 3)
            act.wait_ge(w_used, FIRST["p_rwkv"])
            act.dma_start(LG1[:, :], rows_in[2:3, :].broadcast_to([P, D])).then_inc(sem("ln1_landed"), 16)
            act.dma_start(LB1[:, :], rows_in[3:4, :].broadcast_to([P, D])).then_inc(sem("ln1_landed"), 16)
            evac_high(T_MERGED, None)
            feed(FIRST["w_o"] + 7)

            def layer_norm(k, ms_val):
                act.wait_ge(sem("mean_ready"), k + 1)
                for t in range(NT):
                    last = A(LNS[:, t, :], H[:, t, :], ACT.Square, bias=ST[:, 88 + 2 * k + t:89 + 2 * k + t],
                             accum_out=ST[:, 92 + 2 * k + t:93 + 2 * k + t])
                last.then_inc(sem("var_ready"), 1)
                root(ST[:, 96 + 2 * k:98 + 2 * k], ST[:, 96 + 2 * k:98 + 2 * k], ms_val)

            layer_norm(0, 7)
            evac_high(T_X2, None)
            act.wait_ge(sem("x2_ready"), NT)
            act.dma_start(x2_dram, H[:, :, :].rearrange("p t d -> p (t d)")).then_inc(sem("x2_stored"), 16)
            for m in range(LISTS):
                used(FIRST["peer_q"] + m)
                nc.scalar.copy(QH[:, m, :], PS[:, 4 + m % 4, 0:S]).then_inc(sem("qh_ready"), 1)
            used(FIRST["keys"] + 1)
            for t in range(NT):
                nc.scalar.copy(SC[:, t, :, :].rearrange("p l k -> p (l k)"),
                               PS[:, 4 * t:4 * t + 4, :].rearrange("p b n -> p (b n)")).then_inc(sem("u_bank_free"), 1)

            U0 = FIRST["u"]
            feed(U0)
            assert feed_at[0] == U0 + RING

            def u_evac(i, half):
                act.wait_ge(w_used, U0 + 4 * i + 2 * half + 2)
                A(HS[:, bass.ds(4 * i + 2 * half, 2), :], PS[:, half, :].rearrange("p (j s) -> p j s", j=2),
                  ACT.Gelu).then_inc(sem("u_bank_free"), 1)

            def park(i, b):
                act.wait_ge(sem("gated"), 4 * i + (2 * b + 2))
                block_ = 2 * i + b
                act.dma_start(rest_dram[bass.ds(block_, 1)].rearrange("a p n -> p (a n)"),
                              stage[:, b, :, :].rearrange("p j a -> p (j a)")).then_inc(sem(f"parked{b}"), 16)

            def u_body(i, parks=None):
                for half in range(2):
                    for c in (2 * half, 2 * half + 1):
                        n = 4 * i + RING + c
                        split_high_dyn(U0, n, c)
                    u_evac(i, half)
                    if parks is not None and half == 1:
                        park(i - NK // 8, 0)
                    elif parks:
                        park(i - (NK // 8 + 1), 1)

            def split_high_dyn(first, rel, c):
                slot = (first + c) % RING
                act.wait_ge(w_landed[slot], 16 * ((first + c) // RING + 1) + 4 * (rel - c))
                act.wait_ge(w_used, rel + (first + 1 - RING))
                nc.scalar.copy(WH[:, slot, :], RAW[:, slot, :]).then_inc(w_hi, 1)

            with act.Fori(0, IJG_AT - 2) as i:
                u_body(i)
            act.wait_ge(sem("bv_ready"), 1)
            A(be[:, :, :, :], be[:, :, :, :], ACT.Exp).then_inc(sem("bexp_ready"), 1)
            with act.Fori(IJG_AT - 2, IJG_AT) as i:
                u_body(i)
            act.wait_ge(sem("ijg_ready"), 1)
            act.wait_ge(sem("ijg_mm"), 1)
            nc.scalar.copy(IT[:, :], PS[:, 2, 0:S])
            nc.scalar.copy(JT[:, :], PS[:, 2, S:2 * S])
            nc.scalar.copy(GT[:, :], PS[:, 3, 0:S]).then_inc(sem("ijgT_ready"), 1)
            with act.Fori(IJG_AT, NK // 8) as i:
                u_body(i)
            u_body(NK // 8, parks=0)
            with act.Fori(NK // 8 + 1, NK // 4) as i:
                u_body(i, parks=1)
            park(S // 16 - 1, 1)
            feed_at[0] = FIRST["v_table"] + RING

            act.wait_ge(sem("x2_stored"), 16)
            act.wait_ge(w_used, FIRST["v_table"])
            act.dma_start(LG2[:, :], rows_in[4:5, :].broadcast_to([P, D])).then_inc(sem("ln2_landed"), 16)
            act.dma_start(LB2[:, :], rows_in[5:6, :].broadcast_to([P, D])).then_inc(sem("ln2_landed"), 16)

            V0 = FIRST["v_table"]

            def c_high(j, slot, first=False):
                if not first:
                    act.wait_ge(w_used, j + (V0 + 1 - RING))
                nc.scalar.copy(CH[:, slot, :], HS[:, j, :] if isinstance(j, int) else HS[:, bass.ds(j, 1), :].rearrange(
                    "p a s -> p (a s)")).then_inc(sem("ch_ready"), 1)

            def fetch(block_, b):
                src = rest_dram[block_] if isinstance(block_, int) else \
                    rest_dram[bass.ds(block_, 1)].rearrange("a p n -> p (a n)")
                act.dma_start(stage[:, b, :, :].rearrange("p j a -> p (j a)"), src).then_inc(sem(f"fetched{b}"), 16)

            act.wait_ge(sem("gated"), S // 4)
            for c in range(RING):
                c_high(c, c, True)
            for b in range(2):
                act.wait_ge(sem(f"parked{b}"), 16 * (S // 16))
            for b in range(2):
                fetch(b, b)
            with act.Fori(0, NK // 8 - 1) as i:
                for c in range(4):
                    split_high_dyn(V0, 4 * i + RING + c, c)
                    c_high(4 * i + RING + c, c)
                    if c % 2:
                        act.wait_ge(sem("rest_gated"), 2 * i + (c // 2 + 1))
                        fetch(2 * i + (c // 2 + 2), c // 2)
            for c in range(4):
                split_high_dyn(V0, NK // 2 + c, c)
            act.wait_ge(sem("rest_gated"), S // 8)
            act.dma_start(H[:, :, :].rearrange("p t d -> p (t d)"), x2_dram).then_inc(sem("x2_back"), 16)
            for c in range(4):
                c_high(NK // 2 + c, c)
            with act.Fori(NK // 8, NK // 4 - 1) as i:
                for c in range(4):
                    split_high_dyn(V0, 4 * i + RING + c, c)
                    c_high(4 * i + RING + c, c)
            layer_norm(1, 8)

        @block.tensor
        def _(pe):
            mm = nc.tensor.matmul
            tp = nc.tensor.transpose

            def transposes(r, src, name, value, scale=None):
                pe.wait_ge(sem(name), value)
                for c in range(KC):
                    for t in range(NT):
                        dst = PS[:, 4 + c // 2, (c % 2) * S + t * P:(c % 2) * S + (t + 1) * P]
                        part = src[:, t, c * P:(c + 1) * P]
                        if scale is None:
                            last = tp(dst, part, ident[:, :])
                        else:
                            last = mm(dst, part, scale[:, t, :], start=True, stop=True)
                    if c % 2:
                        last.then_inc(sem("tr_ready"), 1)

            def activations(r):
                return lambda k: wait("xl_ready", KC * r + k + 1)

            def split(pairs, dst, start, stop):
                for k, (a, b) in enumerate(pairs):
                    last = mm(dst, a, b, start=start and k == 0, stop=stop and k == len(pairs) - 1)
                return last

            def form_a(first, groups, per_group, xh, xl, bank=lambda g: 2 * (g % 2), free=None, seed=None, ready=None):
                n = first
                for g in range(groups):
                    if free:
                        free(g)
                    if seed:
                        seed(g)
                    for i in range(per_group):
                        if ready and g == 0:
                            ready(i)
                        pe.wait_ge(w_lo, n + 1)
                        for kk in range(2):
                            k = 2 * i + kk
                            wh = WH[:, n % RING, kk * 512:(kk + 1) * 512]
                            wl = WL[:, n % RING, kk * 512:(kk + 1) * 512]
                            for t in range(NT):
                                h, l = xh[:, k, t * P:(t + 1) * P], xl[:, k, t * P:(t + 1) * P]
                                last = split([(h, wh), (h, wl), (l, wh)], PS[:, bank(g) + t, :],
                                             k == 0 and not seed, k == 2 * per_group - 1)
                        last.then_inc(w_used, 1)
                        n += 1

            def form_b(first, count, place, free, ready=None):
                for m in range(count):
                    n = first + m
                    free(m)
                    pe.wait_ge(w_lo, n + 1)
                    for k in range(KC):
                        if ready and m == 0:
                            ready(k // 2 * 2 + 1)
                        wh, wl = WH[:, n % RING, k * P:(k + 1) * P], WL[:, n % RING, k * P:(k + 1) * P]
                        last = split([(wh, XH[:, k, :]), (wh, XL[:, k, :]), (wl, XH[:, k, :])], place(m),
                                     k == 0, k == KC - 1)
                    last.then_inc(w_used, 1)

            def wait(name, value):
                if value > 0:
                    pe.wait_ge(sem(name), value)

            def small_gates(dst, wh, wl):
                for k in range(KC):
                    last = split([(wh[:, k], XH[:, k, :]), (wh[:, k], XL[:, k, :]), (wl[:, k], XH[:, k, :])], dst,
                                 k == 0, k == KC - 1)
                return last

            pe.wait_ge(sem("ident_ready"), 1)
            transposes(T_MIX, H, "xs_ready", 1, DG)
            wait("xl_ready", 8)
            wait("gwl_ready", 1)
            small_gates(PS[0:16, 3, 0:S], GWH[:, :, 0:16], GWL[:, :, 0:16]).then_inc(sem("gates_mm"), 1)

            def gate_rows(m):
                wait("qk_out", m - 3)
                if m == 1:
                    wait("grow_ready", 1)
                    for c in range(4):
                        last = mm(PS[0:MH, 1 + c // 2, (c % 2) * S:(c % 2 + 1) * S], ident[0:16, 4 * c:4 * c + 4],
                                  grow[:, :], start=True, stop=True)
                    last.then_inc(sem("grow_mm"), 1)

            form_b(FIRST["qk"], 8, lambda m: PS[:, 4 + m % 4, 0:S], gate_rows)
            form_a(FIRST["v"], 2, 4, XH, XL, bank=lambda g: 2 * g, free=lambda g: wait("gr_ready", 1) if g == 0 else None)
            form_a(FIRST["o"], 2, 4, XH, XL, free=lambda g: wait("v_out", g + 1))

            wait("m_ready", 1)
            wait("emt_ready", 1)
            wait("qk_out", 8)
            for k in range(2):
                for d in range(2):
                    for t in range(NT):
                        j = 4 * k + 2 * d + t
                        row = (4 if k == 0 else 0) + d
                        last = tp(PS[:, 7, 4 * j:4 * j + 4], GA[:, row, t * P:(t + 1) * P], ident[0:MH, 0:MH])
            last.then_inc(sem("at_mm"), 1)
            wait("at_ready_m", 1)
            wait("consts_ready", 1)

            def scores(h):
                wait("sm_ready", 2 * h - 2)
                for sb in range(NT):
                    last = mm(PS[:, 4 + h % 2, sb * S:(sb + 1) * S], qkT[:, MH + h, sb * P:(sb + 1) * P],
                              qkT[:, h, :], start=True, stop=True)
                last.then_inc(sem("st_mm"), 1)
                wait("w_ready", 2 * h - 2)
                for d in range(2):
                    last = mm(PS[:, 6 + h % 2, d * S:(d + 1) * S], sel4[:, h, :], GA[:, 6 + d, :], start=True,
                              stop=True)
                last.then_inc(sem("mb_mm"), 1)

            def numerators(e):
                h, d = e // 2, e % 2
                wait("p_ready", e + 1)
                if e < 2:
                    wait("o_out", 2)
                wait("fin_done", e - 1)
                for t in range(NT):
                    sources = range(0, t + 1) if d == 0 else range(t, NT)
                    for sb in sources:
                        last = mm(PS[:, 2 * (e % 2) + t, 0:MDV + 1], SM[:, e % 2, sb, t * P:(t + 1) * P],
                                  v1[:, sb, h, :], start=(sb == sources[0]), stop=(sb == sources[-1]))
                last.then_inc(sem("num_mm"), 1)

            scores(0)
            for e in range(2 * MH):
                if e % 2 == 0 and e + 2 < 2 * MH:
                    scores(e // 2 + 1)
                numerators(e)
            transposes(T_HEADS, XS, "xs_ready", 2)
            form_a(FIRST["mix_out"], 2, 4, XH, XL, ready=lambda i: activations(T_HEADS)(2 * i + 1))

            transposes(T_MLP, H, "xs_ready", 3, DG)
            form_b(FIRST["w1"], 32, lambda m: PS[:, 4 + m % 4, 0:S], lambda m: wait("relu_ready", m - 3),
                   ready=activations(T_MLP))
            form_a(FIRST["w2"], 2, 16, ZH, ZL, ready=lambda i: wait("zl_ready", 2 * i + 2))

            transposes(T_PLE, H, "xs_ready", 4, DG)
            wait("p_landed", 16)
            for c in range(2):
                for t in range(NT):
                    last = tp(PS[:, 0, c * S + t * P:c * S + (t + 1) * P], P2[:, t, c * P:(c + 1) * P], ident[:, :])
            last.then_inc(sem("ptr_ready"), 1)
            wait("ptl_ready", 1)
            wait("brow_landed", 16)

            def bias(g):
                for t in range(NT):
                    mm(PS[:, 2 * (g % 2) + t, :], ones_row[0:1, :], brow[0:1, g * 512:(g + 1) * 512], start=True,
                       stop=False)

            form_a(FIRST["ple_gate"], 2, 4, XH, XL, seed=bias,
                   ready=lambda i: activations(T_PLE)(2 * i + 1))
            form_a(FIRST["ple"], 2, 1, PTH, PTL, free=lambda g: wait("sgp_out", g + 1))

            transposes(T_X1, H, "x1_ready", 1)
            form_b(FIRST["rwkv"], RW_CHUNKS, lambda m: PS[:, 4 + m % 4, 0:S], lambda m: wait("b2_out", m - 3),
                   ready=activations(T_X1))
            form_b(FIRST["fox_qk"], 8, lambda m: PS[:, 4 + (RW_CHUNKS + m) % 4, 0:S],
                   lambda m: wait("b2_out", RW_CHUNKS + m - 3))
            small_gates(PS[0:FH, 3, 0:S], FWH, FWL).then_inc(sem("f_mm"), 1)
            form_a(FIRST["fox_v"], 1, 4, XH, XL)
            wait("lt_ready", 1)
            wait("lora_landed", 16)
            wait("b2_out", RW_CHUNKS + 8)
            for c in range(4):
                mm(PS[:, 4 + c // 2, (c % 2) * S:(c % 2 + 1) * S], lora[0:64, 0, c * P:(c + 1) * P], LT[0:64, 0, :],
                   start=True, stop=True)
            for c in range(4):
                last = mm(PS[:, 6 + c // 2, (c % 2) * S:(c % 2 + 1) * S], lora[64:128, 0, c * P:(c + 1) * P],
                          LT[64:128, 0, :], start=True, stop=True)
            last.then_inc(sem("lora_mm"), 1)
            wait("fv_ready", 1)
            for c in range(4):
                last = mm(PS[:, c // 2, (c % 2) * S:(c % 2 + 1) * S], lora[:, 1, c * P:(c + 1) * P], LT[:, 1, :],
                          start=True, stop=True)
            last.then_inc(sem("lora_mm"), 1)
            wait("fr_ready", 1)

            def gates(g, free=None):
                form_a(FIRST["gates"] + 4 * g, 1, 4, XH, XL, bank=lambda _: 2 * ((g + 1) % 2), free=free)

            gates(0)
            wait("kksq_ready", 1)
            wait("sigw_ready", 1)
            for b in range(2):
                last = mm(PS[:, 4 + b, :], blk_ones[:, :], T[7][:, 2 * b:2 * b + 2, :], start=True, stop=True)
            last.then_inc(sem("kkss_mm"), 1)
            gates(1, lambda _: wait("gg_ready", 1))
            gates(2, lambda _: wait("gate_out", 1))
            wait("bonp_ready", 1)
            wait("aa_ready", 1)
            for b in range(2):
                last = mm(PS[:, 6 + b, :], blk_ones[:, :], T[7][:, 2 * b:2 * b + 2, :], start=True, stop=True)
            last.then_inc(sem("bon_mm"), 1)
            gates(3, lambda _: wait("gate_out", 2))

            wait("nc8_ready", 1)
            wait("nk_ready", 1)
            wait("bon_ready", 1)
            wait("gate_out", 4)
            wait("bk_ready", 1)
            wait("vz_ready", 1)

            def by_token(n):
                wait("tok_ready", n)
                src, c = (VZ, n) if n < NCH else (BK, n - NCH)
                for q in range(NPAIR):
                    last = tp(PS[:, 2, q * P:(q + 1) * P], src[:, q, c, :, :].rearrange("p a t -> p (a t)"), ident[:, :])
                last.then_inc(sem("tok_mm"), 1)

            def r_scores(n):
                wait("pk_ready", n)
                b = 64 * (n % 2)
                for q in range(NPAIR):
                    last = mm(PS[:, 3, q * P:(q + 1) * P], BK[b:b + 64, q, n // 2, :, :].rearrange("p a t -> p (a t)"),
                              CR[b:b + 64, q, n // 2, :, :].rearrange("p a t -> p (a t)"), start=True, stop=True)
                last.then_inc(sem("sc_mm"), 1)

            def f_scores(h):
                b = 64 * (h % 2)
                wait("fmax_ready", h - 1)
                for t in range(NT):
                    n = (t + 1) * P
                    dst = PS[:, 4 + h % 2, t * P:t * P + n]
                    mm(dst, fqk[b:b + 64, h // 2, t * P:(t + 1) * P], fqk[b:b + 64, 4 + h // 2, 0:n], start=True,
                       stop=False)
                    last = mm(dst, sel8[:, h, :], fr[:, 2, 0:n], start=False, stop=True)
                last.then_inc(sem("fs_mm"), 1)

            def f_transposes(h):
                wait("fnorm_ready", h + 1)
                wait("fpt_ready", h - 1)
                for k in range(3):
                    last = tp(PS[:, 6 + h % 2, k * P:(k + 1) * P], fp[:, h % 2, k * P:(k + 1) * P], ident[:, :])
                last.then_inc(sem("fpt_mm"), 1)

            def f_values(h):
                wait("fpt_ready", h + 1)
                b = 64 * (h % 2)
                for t in range(NT):
                    for sb in range(t + 1):
                        k = 0 if t == 0 else 1 + sb
                        last = mm(PS[b:b + 64, h // 4, (h // 2 % 2) * S + t * P:(h // 2 % 2) * S + (t + 1) * P],
                                  fv[:, sb, h * FD:(h + 1) * FD], fpt[:, h % 2, k * P:(k + 1) * P], start=(sb == 0),
                                  stop=(sb == t))
                last.then_inc(sem("fo_mm"), 1)

            f_scores(0)
            f_scores(1)
            for h in range(FH):
                f_transposes(h)
                by_token(h)
                r_scores(h)
                if h + 2 < FH:
                    f_scores(h + 2)
                f_values(h)

            for k, (a, b, dst, adds, need) in enumerate(INVERSE):
                for half in range(2):
                    if k == 0:
                        wait("inv_in", half + 1)
                        if half:
                            wait("yfl_ready", 1)
                            wait("tok_ready", 2 * NCH)
                    upto = max(need, k - 2)
                    wait(f"inv_added{half}", evacuated(upto, True))
                    wait(f"inv_copied{half}", evacuated(upto, False))
                    bank = 4 * (1 - half) + 2 * (k % 2)
                    for u in range(8):
                        dst = PS[:, bank + u // 4, (u % 4) * P:(u % 4 + 1) * P]
                        left = inv[half][a][:, u, :]
                        if b == "I":
                            last = tp(dst, left, ident[:, :])
                        else:
                            last = mm(dst, left, inv[half][b][:, u, :], start=True, stop=True)
                    last.then_inc(sem(f"inv_mm{half}"), 1)
            for half in range(2):
                wait(f"inv_added{half}", evacuated(len(INVERSE) - 1, True))

            def fox_part(c, t):
                n = FIRST["p_fox"] + c
                pe.wait_ge(w_lo, n + 1)
                for kk in range(2):
                    k = 2 * (c % 2) + kk
                    wh = WH[:, n % RING, kk * 512:(kk + 1) * 512]
                    wl = WL[:, n % RING, kk * 512:(kk + 1) * 512]
                    h, l = YFH[:, k, t * P:(t + 1) * P], YFL[:, k, t * P:(t + 1) * P]
                    last = split([(h, wh), (h, wl), (l, wh)], PS[:, 4 + 2 * (c // 2) + t, :], k == 0, k == 3)
                if t:
                    last.then_inc(w_used, 1)

            for c in range(NCH):
                wait("s_ready", c)
                for q in range(NPAIR):
                    for h2 in range(2):
                        rows = slice(64 * h2, 64 * h2 + 64)
                        dst = PS[rows, 0, q * 64:(q + 1) * 64]
                        if c:
                            mm(dst, CR[:, q, c, 0, :], S2[:, q, rows], start=True, stop=True)
                        last = mm(dst, PK[:, c, h2, q, 0:64], UV[:, c, q, rows], start=(c == 0), stop=True,
                                  skip_group_check=True)
                last.then_inc(sem("z_mm"), 1)
                fox_part(c, 0)
                wait("zs_ready", c + 1)
                for q in range(NPAIR):
                    last = mm(PS[:, 1, q * 64:(q + 1) * 64], MINV[:, c, q, :], ZS[:, q, :], start=True, stop=True)
                last.then_inc(sem("u_mm"), 1)
                wait("u_ready", c + 1)
                if c < NCH - 1:
                    for q in range(NPAIR):
                        last = mm(PS[:, 3, q * P:(q + 1) * P], BKT[:, c, q, :], UV[:, c, q, :], start=True, stop=True)
                    last.then_inc(sem("su_mm"), 1)
                wait("yt_ready", c)
                for q in range(NPAIR):
                    if c:
                        mm(PS[:, 2, q * 64:(q + 1) * 64], S2[:, q, :], CR[:, q, c, 1, :], start=True, stop=True)
                    for h2 in range(2):
                        rows = slice(64 * h2, 64 * h2 + 64)
                        last = mm(PS[rows, 2, q * 64:(q + 1) * 64], UV[:, c, q, rows], PK[:, c, h2, q, 64:128],
                                  start=(c == 0), stop=True, skip_group_check=True)
                last.then_inc(sem("y_mm"), 1)
                fox_part(c, 1)
            wait("yt_ready", NCH)
            for b in range(2):
                wait("pf_out", b + 1)
                mm(PS[:, 4 + b, :], blk_ones[:, :], YT[:, 2 * b:2 * b + 2, :], start=True, stop=True).then_inc(
                    sem("gn_mm"), 1)
            for b in range(2):
                wait("ysq_ready", b + 1)
                mm(PS[:, 6 + b, :], blk_ones[:, :], T[0][:, 2 * b:2 * b + 2, :], start=True, stop=True).then_inc(
                    sem("gn_mm"), 1)

            form_a(FIRST["p_rwkv"], 2, 2, YRH, YRL, ready=lambda i: wait("yrl_ready", i + 1))
            transposes(T_MERGED, XS, "xs_ready", 5)
            form_a(FIRST["w_o"], 2, 4, XH, XL, ready=lambda i: activations(T_MERGED)(2 * i + 1))

            transposes(T_X2, H, "x2_ready", 2)
            form_b(FIRST["peer_q"], LISTS, lambda m: PS[:, 4 + m % 4, 0:S], lambda m: wait("ql_ready", m - 3),
                   ready=activations(T_X2))
            wait("ql_ready", LISTS)
            for i in range(2):
                n = FIRST["keys"] + i
                pe.wait_ge(w_lo, n + 1)
                for j in range(LISTS // 2):
                    l = i * (LISTS // 2) + j
                    wh, wl = WH[:, n % RING, j * NK:(j + 1) * NK], WL[:, n % RING, j * NK:(j + 1) * NK]
                    for t in range(NT):
                        h, lo = QH[:, l, t * P:(t + 1) * P], QL[:, l, t * P:(t + 1) * P]
                        last = split([(h, wh), (h, wl), (lo, wh)], PS[:, 4 * t + l // 4, (l % 4) * NK:(l % 4 + 1) * NK],
                                     True, True)
                last.then_inc(w_used, 1)

            U0 = FIRST["u"]

            def gates_of(i, c, first=False):
                if not first:
                    pe.wait_ge(sem("gated"), 4 * i + (c - 3))
                for g in range(2):
                    pe.wait_ge(sem("hot_ready"), 8 * i + (2 * c + g + 1))
                    for a in range(2):
                        k = 2 * g + a
                        last = mm(PS[:, 4 + c, k * NK:(k + 1) * NK], hot_i[:, g, a, :], hot_j[:, g, a, :], start=True,
                                  stop=True)
                    last.then_inc(sem("hot_used"), 1)

            def u_body(i, gates=False, first=False):
                for c in range(4):
                    slot = (U0 + c) % RING
                    if c % 2 == 0:
                        pe.wait_ge(sem("u_bank_free"), 2 * i + (c // 2 + 1))
                    pe.wait_ge(w_lo, 4 * i + (U0 + c + 1))
                    for k in range(KC):
                        wh, wl = WH[:, slot, k * P:(k + 1) * P], WL[:, slot, k * P:(k + 1) * P]
                        last = split([(wh, XH[:, k, :]), (wh, XL[:, k, :]), (wl, XH[:, k, :])],
                                     PS[:, c // 2, (c % 2) * S:(c % 2 + 1) * S], k == 0, k == KC - 1)
                    last.then_inc(w_used, 1)
                    if gates:
                        gates_of(i - NK // 8, c, first)

            with pe.Fori(0, IJG_AT) as i:
                u_body(i)
            wait("ijg_ready", 1)
            for a in range(3):
                for t in range(NT):
                    k = a * S + t * P
                    last = tp(PS[:, 2 + a // 2, (a % 2) * S + t * P:(a % 2) * S + (t + 1) * P], ijg[:, t, a, :],
                              ident[:, :])
            last.then_inc(sem("ijg_mm"), 1)
            with pe.Fori(IJG_AT, NK // 8) as i:
                u_body(i)
            u_body(NK // 8, gates=True, first=True)
            with pe.Fori(NK // 8 + 1, NK // 4) as i:
                u_body(i, gates=True)

            V0 = FIRST["v_table"]

            def v_item(j, c, start=False, stop=False):
                slot = (V0 + c) % RING
                pe.wait_ge(w_lo, j + (V0 + 1))
                pe.wait_ge(sem("cl_ready"), j + 1)
                for t in range(NT):
                    h, l = CH[:, c, t * P:(t + 1) * P], CL[:, c, t * P:(t + 1) * P]
                    for half in range(2):
                        wh = WH[:, slot, half * 512:(half + 1) * 512]
                        wl = WL[:, slot, half * 512:(half + 1) * 512]
                        last = split([(h, wh), (h, wl), (l, wh)], PS[:, 2 * t + half, :], start, stop)
                last.then_inc(w_used, 1)

            for c in range(4):
                v_item(c, c, start=(c == 0))
            with pe.Fori(1, NK // 4 - 1) as i:
                for c in range(4):
                    v_item(4 * i + c, c)
            for c in range(4):
                v_item(NK - 4 + c, c, stop=(c == 3))

        @block.vector
        def _(dve):
            V = nc.vector
            step = sem("dve_step")
            steps = [0]

            def link(ins):
                steps[0] += 1
                ins.then_inc(step, 1)
                dve.wait_ge(step, steps[0])

            def wait(name, value):
                if value > 0:
                    dve.wait_ge(sem(name), value)

            def used(n):
                dve.wait_ge(w_used, n + 1)

            def mean_eps(dst, src, scale, eps):
                V.tensor_scalar(dst, src, scale, eps, ALU.mult, ALU.add).then_inc(sem("ms_ready"), 1)

            def root_mean(r):
                rs = ST[:, 16 + 2 * r:18 + 2 * r]
                wait("ss_ready", 2 * r + 1)
                link(V.tensor_scalar(rs, ST[:, 2 * r:2 * r + 2], 1.0 / D, EPS, ALU.mult, ALU.add))
                wait("ss_ready", 2 * r + 2)
                V.scalar_tensor_tensor(rs, ST[:, 8 + 2 * r:10 + 2 * r], 1.0 / D, rs, ALU.mult, ALU.add).then_inc(
                    sem("ms_ready"), 1)
                wait("sq_ready", r + 1 if r == 0 else r + 2)
                link(V.reciprocal(rs, rs))

            def normed(r):
                root_mean(r)
                for t in range(NT):
                    last = V.tensor_scalar(DG[:, t, :], ident[:, :], ST[:, 16 + 2 * r + t:17 + 2 * r + t], None,
                                           ALU.mult)
                last.then_inc(sem("xs_ready"), 1)

            def low_half(r, gain):
                for c in range(KC):
                    wait("xh_ready", 8 * r + c // 2 * 2 + 2)
                    V.scalar_tensor_tensor(XL[:, c, :], PS[:, 4 + c // 2, (c % 2) * S:(c % 2 + 1) * S],
                                           col(gain, c) if gain else 1.0, plain(XH[:, c, :]), ALU.mult,
                                           ALU.subtract).then_inc(sem("xl_ready"), 1)

            V.memset(v1[:, :, :, MDV:MDV + 1], 1.0)
            wait("ident_ready", 1)
            normed(0)
            wait("gwh_ready", 1)
            V.tensor_tensor(FWL[:, :, :], gw[:, :, 16:24], plain(FWH[:, :, :]), ALU.subtract)
            V.tensor_tensor(GWL[:, :, :], gw[:, :, :], plain(GWH[:, :, :]), ALU.subtract).then_inc(sem("gwl_ready"), 1)
            wait("vec_landed", 16)
            low_half(T_MIX, "norm_mix")

            wait("consts_ready", 1)

            wait("gates_mm", 1)
            V.tensor_copy(grow[:, :], PS[0:16, 3, 0:S]).then_inc(sem("grow_ready"), 1)
            wait("grow_mm", 1)
            wait("mb_landed", 16)
            for k in range(4):
                last = V.tensor_scalar(GR[:, k, :], PS[0:MH, 1 + k // 2, (k % 2) * S:(k % 2 + 1) * S],
                                       mbias[:, k:k + 1], None, ALU.add)
            last.then_inc(sem("gr_ready"), 1)
            wait("gr_ready", 1)

            def qk_copy(m):
                used(FIRST["qk"] + m)
                V.tensor_copy(qkT[:, m, :], PS[:, 4 + m % 4, 0:S]).then_inc(sem("qk_out"), 1)

            for m in range(4):
                qk_copy(m)
            wait("g_act", 3)
            for d in range(2):
                f, i_ = GR[:, 2 * d + 1, :], GR[:, 2 * d, :]
                link(V.scalar_tensor_tensor(GA[:, 0, :], f, 0.0, GA[:, 2 + d, :], ALU.min, ALU.subtract))
                order = slice(None) if d == 0 else slice(None, None, -1)
                link(V.tensor_tensor_scan(GA[:, 2 + d, order], GA[:, 0, order], GA[:, 0, order], 0.0, ALU.add,
                                          ALU.bypass))
                link(V.tensor_tensor(GA[:, 4 + d, :], i_, GA[:, 2 + d, :], ALU.subtract))
                link(V.tensor_tensor_scan(GA[:, 6 + d, order], GA[:, 4 + d, order], GA[:, 4 + d, order], 0.0, ALU.max,
                                          ALU.bypass))
            V.tensor_tensor(GA[:, 0:2, :], GA[:, 2:4, :], GA[:, 6:8, :], ALU.add).then_inc(sem("m_ready"), 1)
            for m in range(4, 8):
                qk_copy(m)
            for g in range(2):
                used(FIRST["v"] + 4 * g + 3)
                for t in range(NT):
                    last = V.tensor_copy(v1[:, t, 2 * g:2 * g + 2, 0:MDV],
                                         PS[:, 2 * g + t, :].rearrange("p (h v) -> p h v", h=2))
                last.then_inc(sem("v_out"), 1)
            wait("at_mm", 1)
            V.tensor_scalar(AT[:, 0:4, :].rearrange("p j h -> p (j h)"), PS[:, 7, 0:16], -1.0, None, ALU.mult)
            V.tensor_copy(AT[:, 4:8, :].rearrange("p j h -> p (j h)"), PS[:, 7, 16:32]).then_inc(sem("at_ready_m"), 1)
            wait("at_ready_m", 1)

            def masked_scores(e):
                h, d = e // 2, e % 2
                wait("st_mm", h + 1)
                wait("num_mm", e - 1)
                V.scalar_tensor_tensor(SM[:, e % 2].rearrange("p a s -> p (a s)"), PS[:, 4 + h % 2, :], MDK ** -0.5,
                                       mask_m[:, d].rearrange("p a s -> p (a s)"), ALU.mult,
                                       ALU.mult).then_inc(sem("sm_ready"), 1)

            def weights_of(e):
                wait("e_ready", e + 1)
                wait("sm_ready", e + 1)
                V.tensor_tensor(SM[:, e % 2], SM[:, e % 2], WE[:, e % 2], ALU.mult).then_inc(sem("p_ready"), 1)

            def finish(e):
                h, d = e // 2, e % 2
                wait("num_mm", e + 1)
                wait("emt_ready", 1)
                den = [ST[:, 44 + 2 * (e % 2) + t:45 + 2 * (e % 2) + t] for t in range(NT)]
                raw = [PS[:, 2 * (e % 2) + t, MDV:MDV + 1] for t in range(NT)]
                least = [AT[:, 4 + 2 * d + t, h:h + 1] for t in range(NT)]
                for t in range(NT):
                    ins = V.tensor_scalar(den[t], raw[t], -1.0, least[t], ALU.mult, ALU.max)
                link(ins)
                for t in range(NT):
                    ins = V.scalar_tensor_tensor(den[t], raw[t], least[t], den[t], ALU.max, ALU.max)
                link(ins)
                both = ST[:, 44 + 2 * (e % 2):46 + 2 * (e % 2)]
                link(V.reciprocal(both, both))
                wait("fin_done", e)
                for t in range(NT):
                    num, acc = PS[:, 2 * (e % 2) + t, 0:MDV], hacc[:, t, h * MDV:(h + 1) * MDV]
                    if d == 0:
                        last = V.tensor_scalar(acc, num, den[t], None, ALU.mult)
                    else:
                        last = V.scalar_tensor_tensor(acc, num, den[t], acc, ALU.mult, ALU.add)
                last.then_inc(sem("fin_done"), 1)

            for e in range(2 * MH + 2):
                if e < 2 * MH:
                    masked_scores(e)
                if 1 <= e <= 2 * MH:
                    weights_of(e - 1)
                if e >= 2:
                    finish(e - 2)
            wait("hss_ready", NT * MH)
            mean_eps(ST[:, 32:40], ST[:, 24:32], 1.0 / MDV, EPS)
            wait("sq_ready", 2)
            link(V.reciprocal(ST[:, 32:40], ST[:, 32:40]))
            wait("o_out", 2)
            for t in range(NT):
                for h in range(MH):
                    k = slice(h * MDV, (h + 1) * MDV)
                    last = V.scalar_tensor_tensor(XS[:, t, k], hacc[:, t, k], ST[:, 32 + 4 * t + h:33 + 4 * t + h],
                                                  og[:, t, k], ALU.mult, ALU.mult)
            last.then_inc(sem("xs_ready"), 1)
            low_half(T_HEADS, "head_norm")

            def add_to_h(first, per_group, alpha=None, half=None):
                for g in range(2):
                    used(first + per_group * (g + 1) - 1)
                    for t in range(NT):
                        k = slice(g * 512, (g + 1) * 512)
                        src = PS[:, 2 * (g % 2) + t, :]
                        if alpha is None:
                            last = V.tensor_tensor(H[:, t, k], H[:, t, k], src, ALU.add)
                        else:
                            sums = ST[:, 80 + 2 * g + t:81 + 2 * g + t]
                            last = V.scalar_tensor_tensor(H[:, t, k], H[:, t, k], alpha, src, ALU.mult, ALU.add,
                                                          accum_out=sums)
                    last.then_inc(sem("h_sum" if half is None else half), 1)

            add_to_h(FIRST["mix_out"], 4, half="h_half")

            normed(1)
            low_half(T_MLP, "norm_mlp")

            def z_low(m):
                wait("zh_ready", m + 1)
                V.tensor_tensor(ZL[:, m, :], ZF[:, m % 4, :], plain(ZH[:, m, :]), ALU.subtract).then_inc(
                    sem("zl_ready"), 1)

            for m in range(32):
                wait("relu_ready", m + 1)
                wait("zl_ready", m - 3)
                V.tensor_tensor(ZF[:, m % 4, :], RT[:, m % 4, :], RT[:, m % 4, :], ALU.mult).then_inc(
                    sem("zf_ready"), 1)
                if m >= 1:
                    z_low(m - 1)
            z_low(31)
            add_to_h(FIRST["w2"], 16, half="h_half")

            normed(2)
            low_half(T_PLE, "norm_ple")
            wait("pth_ready", 1)
            V.tensor_tensor(PTL[:, :, :], PS[:, 0, :].rearrange("p (c s) -> p c s", c=2), plain(PTH[:, :, :]),
                            ALU.subtract).then_inc(sem("ptl_ready"), 1)
            wait("sgp_out", 2)
            for g in range(2):
                used(FIRST["ple"] + g)
                k = slice(g * 512, (g + 1) * 512)
                for t in range(NT):
                    ins = V.tensor_tensor(XS[:, t, k], PS[:, 2 * g + t, :], SGP[:, t, k], ALU.mult)
                link(ins)
                for t in range(NT):
                    last = V.tensor_tensor(H[:, t, k], H[:, t, k], XS[:, t, k], ALU.add)
                last.then_inc(sem("h_half"), 1)
            root_mean(3)
            wait("nfin_landed", 16)
            for t in range(NT):
                last = V.scalar_tensor_tensor(H[:, t, :], H[:, t, :], ST[:, 22 + t:23 + t], nfin[:, :], ALU.mult,
                                              ALU.mult)
            last.then_inc(sem("x1_ready"), 1)
            V.memset(Z[:, :, 0:1], 0.0).then_inc(sem("z_zero"), 1)
            low_half(T_X1, None)

            wait("z_zero", 1)
            for m in range(RW_CHUNKS):
                wait("b2_out", m + 1)
                link(V.tensor_tensor(T[4][:, m % 4, :], Z[:, m, 0:S], Z[:, m, 1:S + 1], ALU.subtract))
                V.scalar_tensor_tensor(SH[:, m, :], T[4][:, m % 4, :], col("mu", m), Z[:, m, 1:S + 1], ALU.mult,
                                       ALU.add).then_inc(sem("sh_ready"), 1)
            used(FIRST["fox_v"] + 3)
            for t in range(NT):
                last = V.tensor_copy(fv[:, t, :], PS[:, t, :])
            last.then_inc(sem("fv_ready"), 1)
            wait("f_mm", 1)
            wait("fb_landed", 16)
            V.tensor_scalar(fr[:, 0, :], PS[0:FH, 3, 0:S], fbias[:, 0:1], None, ALU.add).then_inc(sem("fr_ready"), 1)
            wait("sh_ready", RW_CHUNKS)
            for c in range(4):
                ins = V.tensor_scalar(T[6][:, c, :], SH[:, 4 + c, :], col("k_k", c), None, ALU.mult)
            link(ins)
            V.tensor_tensor(T[7][:, :, :], T[6][:, :, :], T[6][:, :, :], ALU.mult).then_inc(sem("kksq_ready"), 1)
            wait("f_act", 3)
            link(V.scalar_tensor_tensor(fr[:, 0, :], fr[:, 0, :], 0.0, fr[:, 1, :], ALU.min, ALU.subtract))
            link(V.tensor_tensor_scan(fr[:, 1, :], fr[:, 0, :], fr[:, 0, :], 0.0, ALU.add, ALU.bypass))
            V.tensor_scalar(fr[:, 2, :], fr[:, 1, :], -float(FD) ** 0.5, None, ALU.mult).then_inc(sem("nc8_ready"), 1)
            wait("sigw_ready", 1)
            flat = lambda x: x.rearrange("p c s -> p (c s)")
            link(V.tensor_tensor_scan(flat(T[5][:, :, :]), resets[:, :], flat(T[4][:, :, :]), 0.0, ALU.mult, ALU.add))
            V.tensor_tensor(T[2][:, :, :], T[5][:, :, :], T[4][:, :, :], ALU.subtract).then_inc(sem("lg_ready"), 2)
            wait("kkss_mm", 1)
            V.tensor_scalar(flat(T[7][:, :, :]), PS[:, 4:6, :].rearrange("p b n -> p (b n)"), 1e-24, None,
                            ALU.max).then_inc(sem("ms_ready"), 1)
            wait("gdec_ready", 1)
            V.tensor_copy(GL[:, :, :], T[0][:, :, :].rearrange("p q (c t) -> p q c t", t=CH_T)[:, :, :, CH_T - 1])
            wait("aa_ready", 1)
            for c in range(4):
                ins = V.tensor_scalar(T[5][:, c, :], T[3][:, c, :], 1.0, col("k_a", c), ALU.subtract, ALU.mult)
            link(ins)
            link(V.scalar_tensor_tensor(T[5][:, :, :], T[5][:, :, :], 1.0, SH[:, 4:8, :], ALU.add, ALU.mult))
            wait("sq_ready", 6)
            link(V.reciprocal(T[7][:, :, :], T[7][:, :, :]))
            V.tensor_tensor(T[6][:, :, :], T[6][:, :, :], T[7][:, :, :], ALU.mult).then_inc(sem("nk_ready"), 1)
            wait("nk_ready", 1)
            link(V.tensor_tensor(T[7][:, :, :], SH[:, 0:4, :], T[5][:, :, :], ALU.mult))
            for c in range(4):
                last = V.tensor_scalar(T[7][:, c, :], T[7][:, c, :], col("r_k", c), None, ALU.mult)
            last.then_inc(sem("bonp_ready"), 1)
            link(V.tensor_tensor(T[4][:, :, :], T[6][:, :, :], T[3][:, :, :], ALU.mult))
            chunked = lambda x: x.rearrange("p c (n t) -> p (c n) t", t=CH_T)
            part = lambda x, k: x[:, :, :, k, :].rearrange("p q c t -> p (q c) t")
            for h2 in range(2):
                rows = slice(64 * h2, 64 * h2 + 64)
                for k, src in ((h2, T[4]), (1 - h2, T[5])):
                    V.tensor_tensor(part(BK[rows], k), chunked(src[rows]), chunked(T[1][rows]), ALU.mult)
            V.tensor_tensor(part(CR, 0), chunked(T[6][:, :, :]), chunked(T[2][:, :, :]), ALU.mult)
            V.tensor_tensor(part(CR, 1), chunked(SH[:, 0:4, :]), chunked(T[0][:, :, :]), ALU.mult).then_inc(
                sem("bk_ready"), 1)
            wait("bk_ready", 1)
            for h2 in range(2):
                rows = slice(64 * h2, 64 * h2 + 64)
                V.memset(part(VZ[rows], h2), 0.0)
                last = V.tensor_copy(part(VZ[rows], 1 - h2), chunked(SH[rows, 8:12, :]))
            last.then_inc(sem("vz_ready"), 1)
            wait("bon_mm", 1)
            V.tensor_tensor(flat(BON[:, :, :]), PS[:, 6:8, :].rearrange("p b n -> p (b n)"), flat(SH[:, 8:12, :]),
                            ALU.mult).then_inc(sem("bon_ready"), 1)
            wait("bon_ready", 1)
            for c in range(4):
                ins = V.tensor_scalar(BON[:, c, :], BON[:, c, :], col("ln_b", c), None, ALU.add)
            link(ins)

            def f_max(h):
                wait("fs_mm", h + 1)
                wait("fpt_mm", h - 1)
                s0 = 64 + 8 * (h % 2)
                V.tensor_tensor_reduce(out=fp[:, h % 2, 0:P], in0=PS[:, 4 + h % 2, 0:P], in1=mask_f[:, P:S], scale=1.0,
                                       scalar=3.0 * NEG, op0=ALU.add, op1=ALU.max, accum_out=ST[:, s0:s0 + 1])
                link(V.tensor_tensor_reduce(out=fp[:, h % 2, P:384], in0=PS[:, 4 + h % 2, P:384], in1=mask_f[:, :],
                                            scale=1.0, scalar=3.0 * NEG, op0=ALU.add, op1=ALU.max,
                                            accum_out=ST[:, s0 + 1:s0 + 2]))
                V.tensor_scalar(ST[:, s0 + 2:s0 + 4], ST[:, s0:s0 + 2], -float(FD) ** -0.5, None, ALU.mult).then_inc(
                    sem("fmax_ready"), 1)

            def f_norm(h):
                wait("fexp_ready", h + 1)
                s0 = 64 + 8 * (h % 2)
                link(V.reciprocal(ST[:, s0 + 4:s0 + 6], ST[:, s0 + 4:s0 + 6]))
                V.tensor_scalar(fp[:, h % 2, 0:P], fp[:, h % 2, 0:P], ST[:, s0 + 4:s0 + 5], None, ALU.mult)
                V.tensor_scalar(fp[:, h % 2, P:384], fp[:, h % 2, P:384], ST[:, s0 + 5:s0 + 6], None,
                                ALU.mult).then_inc(sem("fnorm_ready"), 1)

            def masked_rwkv(n):
                wait("sc_mm", n + 1)
                V.tensor_tensor(PK[:, n // 2, n % 2, :, :], PS[:, 3, :].rearrange("p (q n) -> p q n", n=P),
                                mask_r[:, :].unsqueeze(1).broadcast_to([P, NPAIR, P]), ALU.mult).then_inc(
                                    sem("pk_ready"), 1)

            def zeros(n):
                if n == 0:
                    used(FIRST["gates"] + 15)
                if n == 4:
                    wait("tok_mm", NCH)
                if n in (0, 1):
                    V.memset(inv[n]["X"], 0.0)
                elif n in (2, 3):
                    V.memset(inv[n - 2]["P0"][:, :, :], 0.0)
                elif n in (4, 5):
                    V.memset(inv[n - 4]["NO"][:, :, :], 0.0).then_inc(sem("zeros_ready"), 1)

            def inverse_inputs(half):
                wait("pk_ready", NCH * (half + 1))
                wait("zeros_ready", 2)
                I = inv[half]
                blocks = [(c, slice(NPAIR * c, NPAIR * c + NPAIR), h2, slice(64 * h2, 64 * h2 + 64))
                          for c in range(2) for h2 in range(2)]
                A_ = lambda c, h2, r: PK[r, 2 * half + c, h2, :, 0:64]
                for c, q, h2, r in blocks:
                    diag = blk16[r, :].unsqueeze(1).broadcast_to([64, NPAIR, 64])
                    ins = V.scalar_tensor_tensor(I["P0"][r, q, r], A_(c, h2, r), -1.0, diag, ALU.mult, ALU.mult)
                link(ins)
                for c, q, h2, r in blocks:
                    V.scalar_tensor_tensor(I["NO"][r, q, r], A_(c, h2, r), -1.0, I["P0"][r, q, r], ALU.mult,
                                           ALU.subtract)
                for c, q, h2, r in blocks:
                    eye = ident[r, r].unsqueeze(1).broadcast_to([64, NPAIR, 64])
                    last = V.tensor_tensor(I["X"][r, q, r], I["P0"][r, q, r], eye, ALU.add)
                last.then_inc(sem("inv_in"), 1)

            f_max(0)
            for h in range(FH):
                if h + 1 < FH:
                    f_max(h + 1)
                f_norm(h)
                if h >= 1:
                    masked_rwkv(h - 1)
                    zeros(h - 1)
                if h == FH - 1:
                    inverse_inputs(0)
            masked_rwkv(FH - 1)

            inverse_inputs(1)
            wait("inv_in", 2)
            wait("yfh_ready", 1)
            V.tensor_tensor(flat(YFL[:, :, :]), PS[:, 0:2, :].rearrange("p b n -> p (b n)"),
                            flat(plain(YFH[:, :, :])), ALU.subtract).then_inc(sem("yfl_ready"), 1)
            for k, (_, _, dst, adds, _) in enumerate(INVERSE):
                if not adds:
                    continue
                for half in range(2):
                    wait(f"inv_mm{half}", k + 1)
                    b = 4 * (1 - half) + 2 * (k % 2)
                    X = inv[half]["X"].rearrange("p u n -> p (u n)")
                    wait(f"inv_added{half}", evacuated(k - 1, True))
                    V.tensor_tensor(X, X, PS[:, b:b + 2, :].rearrange("p b n -> p (b n)"), ALU.add).then_inc(
                        sem(f"inv_added{half}"), 1)

            for c in range(NCH):
                wait("z_mm", c + 1)
                V.tensor_scalar(ZS[:, :, :].rearrange("p q n -> p (q n)"), PS[:, 0, 0:S], -1.0, None, ALU.mult).then_inc(sem("zs_ready"), 1)
                if c < NCH - 1:
                    wait("su_mm", c + 1)
                    src = PS[:, 3, :].rearrange("p (q n) -> p q n", n=P)
                    if c:
                        link(V.tensor_tensor(S2T[:, :, :], S2[:, :, :], src, ALU.add))
                        src = S2T[:, :, :]
                        wait("y_mm", c + 1)
                    for q in range(NPAIR):
                        last = V.scalar_tensor_tensor(S2[:, q, :], src[:, q, :], GL[:, q, c:c + 1], blk_ones[:, :],
                                                      ALU.mult, ALU.mult)
                    last.then_inc(sem("s_ready"), 1)
                    wait("s_ready", c + 1)
                if c % 2:
                    g = c // 2
                    used(FIRST["p_fox"] + c)
                    k = slice(g * 512, (g + 1) * 512)
                    for t in range(NT):
                        last = V.tensor_tensor(XS[:, t, k], PS[:, 4 + 2 * g + t, :], SG[:, t, k], ALU.mult)
                    last.then_inc(sem("pf_out"), 1)

            two = lambda x, b: flat(x[:, 2 * b:2 * b + 2, :])
            for b in range(2):
                wait("gn_mm", b + 1)
                link(V.scalar_tensor_tensor(two(YC, b), PS[:, 4 + b, :], -1.0 / RN, two(YT, b), ALU.mult, ALU.add))
                V.tensor_tensor(two(T[0], b), two(YC, b), two(YC, b), ALU.mult).then_inc(sem("ysq_ready"), 1)
            for b in range(2):
                wait("rstd_ready", b + 1)
                link(V.tensor_tensor(two(YC, b), two(YC, b), two(T[2], b), ALU.mult))
                for c in (2 * b, 2 * b + 1):
                    ins = V.scalar_tensor_tensor(YC[:, c, :], YC[:, c, :], col("ln_g", c), BON[:, c, :], ALU.mult,
                                                 ALU.add)
                link(ins)
                V.tensor_tensor(two(YC, b), two(YC, b), two(GG, b), ALU.mult).then_inc(sem("yr_ready"), 1)
            for b in range(2):
                wait("yrh_ready", b + 1)
                V.tensor_tensor(two(YRL, b), two(YC, b), two(plain(YRH), b), ALU.subtract).then_inc(
                    sem("yrl_ready"), 1)

            wait("pf_out", 2)
            for g in range(2):
                used(FIRST["p_rwkv"] + 2 * g + 1)
                k = slice(g * 512, (g + 1) * 512)
                for t in range(NT):
                    ins = V.tensor_tensor(flat(T[3 - 2 * g][:, 2 * t:2 * t + 2, :]), PS[:, 2 * g + t, :],
                                          SG[:, t, D + g * 512:D + (g + 1) * 512], ALU.mult)
                link(ins)
                for t in range(NT):
                    last = V.tensor_tensor(XS[:, t, k], XS[:, t, k], flat(T[3 - 2 * g][:, 2 * t:2 * t + 2, :]), ALU.add)
            last.then_inc(sem("xs_ready"), 1)
            low_half(T_MERGED, None)
            add_to_h(FIRST["w_o"], 4, DN_ALPHA)

            def layer_norm(k, gain, shift, landed, ready):
                s, m, r = ST[:, 80:84], ST[:, 88 + 2 * k:90 + 2 * k], ST[:, 96 + 2 * k:98 + 2 * k]
                wait("h_sum", 2 * k + 2)
                link(V.tensor_tensor(m, s[:, 0:2], s[:, 2:4], ALU.add))
                V.tensor_scalar(m, m, -1.0 / D, None, ALU.mult).then_inc(sem("mean_ready"), 1)
                wait("mean_ready", k + 1)
                wait(landed, 32)
                for t in range(NT):
                    ins = V.scalar_tensor_tensor(XS[:, t, :], H[:, t, :], m[:, t:t + 1], gain[:, :], ALU.add, ALU.mult)
                link(ins)
                wait("var_ready", k + 1)
                mean_eps(r, ST[:, 92 + 2 * k:94 + 2 * k], 1.0 / D, LN_EPS)
                wait("sq_ready", 7 + k)
                link(V.reciprocal(r, r))
                for t in range(NT):
                    V.scalar_tensor_tensor(H[:, t, :], XS[:, t, :], r[:, t:t + 1], shift[:, :], ALU.mult,
                                           ALU.add).then_inc(sem(ready), 1)

            layer_norm(0, LG1, LB1, "ln1_landed", "x2_ready")
            low_half(T_X2, None)

            for m in range(LISTS):
                wait("qh_ready", m + 1)
                V.tensor_tensor(QL[:, m, :], PS[:, 4 + m % 4, 0:S], plain(QH[:, m, :]), ALU.subtract).then_inc(
                    sem("ql_ready"), 1)

            wait("u_bank_free", NT)
            for t in range(NT):
                def best(values, top, index, lists, n):
                    for r in range(2):
                        for l in range(lists):
                            ins = V.max(top(l)[:, 8 * r:8 * r + 8], values(l))
                        link(ins)
                        for l in range(lists):
                            ins = V.max_index(index(l)[:, 8 * r:8 * r + 8], top(l)[:, 8 * r:8 * r + 8], values(l))
                        link(ins)
                        if r == 0:
                            for l in range(lists):
                                ins = V.match_replace(values(l), top(l)[:, 0:8], values(l), -3.0e38)
                            link(ins)

                best(lambda l: SC[:, t, l, :], lambda l: tv[:, l, :], lambda l: ti[:, l, :], LISTS, NK)
                V.tensor_copy(tif[:, :, :], ti[:, :, :])
                pair = tv[:, :, :].rearrange("p (h two) k -> p h two k", two=2)
                shape = [P, PH, TOPK, TOPK]
                link(V.tensor_tensor(cand[:, :, :, :], pair[:, :, 0, :].unsqueeze(3).broadcast_to(shape),
                                     pair[:, :, 1, :].unsqueeze(2).broadcast_to(shape), ALU.add))
                best(lambda l: cand[:, l, :, :].rearrange("p a b -> p (a b)"), lambda l: bv[:, t, l, :],
                     lambda l: bp[:, l, :], PH, TOPK * TOPK)
                V.tensor_scalar(bai[:, :, :], bp[:, :, :], 4, None, ALU.logical_shift_right)
                link(V.tensor_scalar(bbi[:, :, :], bp[:, :, :], TOPK - 1, None, ALU.bitwise_and))
                V.tensor_copy(baf[:, :, :], bai[:, :, :])
                link(V.tensor_copy(bbf[:, :, :], bbi[:, :, :]))
                keys = tif[:, :, :].rearrange("p (h two) k -> p h two k", two=2)
                for which, place in ((0, baf), (1, bbf)):
                    flat3 = tmp1[:, :, :, :].rearrange("p h k a -> p (h k) a")
                    link(V.tensor_tensor(flat3, iota_f[:, 0:TOPK].unsqueeze(1).broadcast_to([P, P, TOPK]),
                                         place[:, :, :].rearrange("p h k -> p (h k)").unsqueeze(2).broadcast_to(
                                             [P, P, TOPK]), ALU.is_equal))
                    link(V.tensor_tensor(tmp1[:, :, :, :], tmp1[:, :, :, :],
                                         keys[:, :, which, :].unsqueeze(2).broadcast_to(shape), ALU.mult))
                    link(V.tensor_reduce(ijg[:, t, which, :], flat3, AX_X, ALU.add))
                last = V.tensor_tensor(be[:, t], bv[:, t], bv[:, t, :, 0:1].broadcast_to([P, PH, TOPK]), ALU.subtract)
            last.then_inc(sem("bv_ready"), 1)
            wait("bexp_ready", 1)
            both = be[:, :, :, :].rearrange("p t h k -> p (t h) k")
            link(V.tensor_reduce(ST[:, 112:128], both, AX_X, ALU.add))
            link(V.reciprocal(ST[:, 112:128], ST[:, 112:128]))
            for t in range(NT):
                last = V.tensor_tensor(ijg[:, t, 2, :].rearrange("p (h k) -> p h k", h=PH), be[:, t],
                                       ST[:, 112 + 8 * t:120 + 8 * t].unsqueeze(2).broadcast_to([P, PH, TOPK]),
                                       ALU.mult)
            last.then_inc(sem("ijg_ready"), 1)

            wait("ijgT_ready", 1)

            def at_token(x, t):
                return x[:, t:t + 1] if isinstance(t, int) else x[:, bass.ds(t, 1)]

            def one_hots(i, c, first=False):
                for g in range(2):
                    if not first:
                        dve.wait_ge(sem("hot_used"), 8 * i + (2 * c + g - 1))
                    for a in range(2):
                        t = 16 * i + (4 * c + 2 * g + a)
                        V.tensor_scalar(hot_i[:, g, a, :], iota_f[:, :], at_token(IT, t), None, ALU.is_equal)
                        last = V.tensor_scalar(hot_j[:, g, a, :], iota_f[:, :], at_token(JT, t), at_token(GT, t),
                                               ALU.is_equal, ALU.mult)
                    last.then_inc(sem("hot_ready"), 1)

            def tokens(t, n):
                return slice(t, t + n) if isinstance(t, int) else bass.ds(t, n)

            def gate(i, c, first=False):
                dve.wait_ge(sem("hot_used"), 8 * i + (2 * c + 2))
                if c % 2 == 0 and not first:
                    dve.wait_ge(sem(f"parked{c // 2}"), 16 * i)
                hs = HS[:, 0:NK // 2, tokens(16 * i + 4 * c, 4)]
                made = PS[:, 4 + c, :].rearrange("p (a j) -> p j a", a=4)
                V.tensor_tensor(hs, hs, made[:, 0:NK // 2], ALU.mult)
                k = 4 * (c % 2)
                V.tensor_copy(stage[:, c // 2, :, k:k + 4], made[:, NK // 2:NK]).then_inc(sem("gated"), 1)

            def gate_rest(i, b):
                dve.wait_ge(sem(f"fetched{b}"), 16 * i + 16)
                hs = HS[:, NK // 2:NK, tokens(16 * i + 8 * b, 8)]
                V.tensor_tensor(hs, hs, stage[:, b, :, :], ALU.mult).then_inc(sem("rest_gated"), 1)

            def c_low(j, c):
                dve.wait_ge(sem("ch_ready"), j + 1)
                hs = HS[:, j, :] if isinstance(j, int) else HS[:, bass.ds(j, 1), :].rearrange("p a s -> p (a s)")
                V.tensor_tensor(CL[:, c, :], hs, plain(CH[:, c, :]), ALU.subtract).then_inc(sem("cl_ready"), 1)

            wait("u_bank_free", NT + NK // 4)
            wait("x2_stored", 16)
            for c in range(4):
                one_hots(0, c, first=(c == 0))
                if c:
                    gate(0, c - 1, first=True)
            with dve.Fori(1, S // 16) as i:
                one_hots(i, 0)
                gate(i - 1, 3)
                for c in range(1, 4):
                    one_hots(i, c)
                    gate(i, c - 1)
            gate(S // 16 - 1, 3)
            wait("u_bank_free", NT + NK // 2)
            for c in range(4):
                c_low(c, c)
            with dve.Fori(0, S // 16) as i:
                for b in range(2):
                    gate_rest(i, b)
                for c in range(4):
                    c_low(4 * i + RING + c, c)
            with dve.Fori(S // 16 + 1, NK // 4) as i:
                for c in range(4):
                    c_low(4 * i + c, c)
            used(N_ITEMS - 1)
            wait("x2_back", 16)
            for g in range(2):
                for t in range(NT):
                    k = slice(g * 512, (g + 1) * 512)
                    last = V.scalar_tensor_tensor(H[:, t, k], H[:, t, k], DN_ALPHA, PS[:, 2 * t + g, :], ALU.mult,
                                                  ALU.add, accum_out=ST[:, 80 + 2 * g + t:81 + 2 * g + t])
                last.then_inc(sem("h_sum"), 1)
            layer_norm(1, LG2, LB2, "ln2_landed", "y_ready")


def kernel(**inputs):
    import numpy as np
    import concourse.bacc as bacc
    from concourse.bass_utils import run_bass_kernel_spmd

    a = {k: np.asarray(v) for k, v in inputs.items()}

    def form_a(w):
        k, n = w.shape
        return w.reshape(k // 256, 2, P, n // 512, 512).transpose(3, 0, 2, 1, 4).reshape(-1, P, D)

    def form_b(w):
        return w.reshape(KC, P, -1, P).transpose(2, 1, 0, 3).reshape(-1, P, D)

    w1 = a["mlstm_w_in"][0]
    w2 = a["w_in_2"][0]
    fox = 3 * FH * FD + FH
    rw = fox + RW_CHUNKS * P
    parts = {
        "qk": form_b(w1[:, :1024]),
        "v": form_a(w1[:, 1024:2048]),
        "o": form_a(w1[:, 2048:3072]),
        "mix_out": form_a(a["mlstm_w_out"][0]),
        "w1": form_b(a["mlp_w1"][0]),
        "w2": form_a(a["mlp_w2"][0]),
        "ple_gate": form_a(a["ple_gate_w"][0]),
        "ple": form_a(a["ple_w"][0]),
        "rwkv": form_b(w2[:, fox:rw]),
        "fox_qk": form_b(w2[:, :1024]),
        "fox_v": form_a(w2[:, 1024:1536]),
        "gates": form_a(w2[:, rw:]),
        "p_fox": form_a(a["p_fox_2"][0]),
        "p_rwkv": form_a(a["p_rwkv_2"][0]),
        "w_o": form_a(a["w_o_2"][0]),
        "peer_q": form_b(a["peer_w_q_2"][0]),
        "keys": a["peer_sub_keys_2"][0].reshape(2, PH, NK, P).transpose(0, 3, 1, 2).reshape(2, P, D),
        "u": a["peer_u_2"][0].reshape(NK, NK, KC, P).transpose(1, 3, 2, 0).reshape(NK, P, D),
        "v_table": a["peer_v_2"][0].reshape(NK, NK, D).transpose(1, 0, 2),
    }
    for name, n in COUNTS:
        assert parts[name].shape == (n, P, D), name
    vectors = [a["norm_mix"], a["norm_mlp"], a["norm_ple"], a["mlstm_head_norm"], a["rwkv_mu_2"], a["rwkv_w0_2"],
               a["rwkv_a0_2"], a["rwkv_k_k_2"], a["rwkv_k_a_2"], a["rwkv_r_k_2"], a["rwkv_ln_g_2"], a["rwkv_ln_b_2"]]
    columns = lambda w: w.reshape(KC, P, -1).transpose(1, 0, 2)
    arrays = {
        "weights": np.concatenate([parts[name] for name, _ in COUNTS]),
        "x": a["x"][0],
        "p": a["p"][0, 0],
        "vectors": np.concatenate([v[0].reshape(-1, P).T for v in vectors], axis=1),
        "rows": np.stack([a["norm_final"], a["ple_gate_b"][0], a["ln1_g_2"][0], a["ln1_b_2"][0], a["ln2_g_2"][0],
                          a["ln2_b_2"][0]]),
        "gate_weights": np.concatenate([columns(w1[:, 3072:]), columns(w2[:, 1536:fox])], axis=2),
        "low_rank": np.stack([np.concatenate([a["rwkv_w2_2"][0], a["rwkv_a2_2"][0]]), a["rwkv_g2_2"][0]], axis=1),
        "gate_bias": a["mlstm_b_gates"][0].T,
        "fox_bias": a["fox_f_bias_2"][0].reshape(FH, 1),
    }
    arrays = {k: np.ascontiguousarray(v) for k, v in arrays.items()}
    nc = bacc.Bacc("TRN2", target_bir_lowering=False, num_devices=1)
    args = [nc.dram_tensor(k, v.shape, mybir.dt.from_np(v.dtype), kind="ExternalInput").ap() for k, v in arrays.items()]
    out = nc.dram_tensor("y", (S, D), F32, kind="ExternalOutput").ap()
    rest = nc.dram_tensor("gates_rest", (S // 8, P, NK // 2 * 8), F32, kind="Internal").ap()
    x2 = nc.dram_tensor("x2", (P, NT * D), F32, kind="Internal").ap()
    bass_blocks(nc, *args, out, rest, x2)
    r = run_bass_kernel_spmd(nc, [arrays], core_ids=[0])
    return r.results[0]["y"].reshape(1, S, D)
```
